# Optimizing a Trainium2 kernel written in Bass

```python
import math
import jax, jax.numpy as jnp
from jax import lax
import numpy as np

D_MODEL = 1024
BATCH = 1
SEQ = 256
DEPTH = 2

GRID_W = 64
HEAD_DIM = D_MODEL // 16
Q_BLOCK = 128
RMS_EPS = 1e-6
NEG_INF = -1e30

NA_HEADS = 4
NA_WIN_H = 8
NA_WIN_W = 16
DIFF_HEADS = 4
DIFF_QK_DIM = HEAD_DIM // 2
DIFF_V_DIM = HEAD_DIM
GQA_Q_HEADS = 4
GQA_KV_HEADS = 2
AXIAL_THETA = 10000.0
DIL_HEADS = 4
DIL_PAIRS = ((128, 1), (512, 4), (2048, 16))
ROPE_THETA = 500000.0
ROPE_FRACTION = 4
D_FF = ((8 * D_MODEL // 3 + 255) // 256) * 256

NA_W = NA_HEADS * HEAD_DIM
DIFF_QK_W = DIFF_HEADS * 2 * DIFF_QK_DIM
DIFF_V_W = DIFF_HEADS * DIFF_V_DIM
GQA_Q_W = GQA_Q_HEADS * HEAD_DIM
GQA_KV_W = GQA_KV_HEADS * HEAD_DIM
DIL_W = DIL_HEADS * HEAD_DIM
IN_SIZES = (NA_W, NA_W, NA_W, DIFF_QK_W, DIFF_QK_W, DIFF_V_W, GQA_Q_W, GQA_KV_W, GQA_KV_W, DIL_W, DIL_W, DIL_W)
IN_WIDTH = sum(IN_SIZES)
MIX_WIDTH = NA_W + DIFF_V_W + GQA_Q_W + DIL_W


def rms_norm(x, gain):
    xf = x.astype(jnp.float32)
    y = xf * lax.rsqrt(jnp.mean(xf * xf, axis=-1, keepdims=True) + RMS_EPS)
    return (y * gain.astype(jnp.float32)).astype(x.dtype)

def rope_tables(pos, dim, theta):
    inv_freq = 1.0 / (theta ** (jnp.arange(0, dim, 2, dtype=jnp.float32) / dim))
    ang = pos.astype(jnp.float32)[:, None] * inv_freq[None, :]
    return jnp.cos(ang), jnp.sin(ang)

def apply_rope(x, cos, sin):
    x1, x2 = jnp.split(x.astype(jnp.float32), 2, axis=-1)
    c = cos[None, :, None, :]
    s = sin[None, :, None, :]
    return jnp.concatenate([x1 * c - x2 * s, x1 * s + x2 * c], axis=-1).astype(x.dtype)

def partial_rope(x, cos, sin, n_rot):
    return jnp.concatenate([apply_rope(x[..., :n_rot], cos, sin), x[..., n_rot:]], axis=-1)

def swiglu(h, w_gate, w_up, w_down):
    return (jax.nn.silu(h @ w_gate) * (h @ w_up)) @ w_down

def split_in_proj(h):
    points = np.cumsum(IN_SIZES)[:-1].tolist()
    return jnp.split(h, points, axis=-1)

def neighborhood_attention(q, k, v, q_gain, k_gain, rel_bias, rows):
    B, S, _ = q.shape
    H, d = NA_HEADS, HEAD_DIM
    q = rms_norm(q.reshape(B, S, H, d), q_gain)
    k = rms_norm(k.reshape(B, S, H, d), k_gain)
    v = v.reshape(B, S, H, d)
    to_grid = lambda t: t.reshape(B, rows, GRID_W, H, d).transpose(0, 3, 1, 2, 4)
    qg, kg, vg = to_grid(q), to_grid(k), to_grid(v)
    kh = min(NA_WIN_H, rows)
    cols = jnp.arange(GRID_W)
    col_idx = jnp.clip(cols - NA_WIN_W // 2, 0, GRID_W - NA_WIN_W)[:, None] + jnp.arange(NA_WIN_W)[None, :]
    col_off = col_idx - cols[:, None] + (NA_WIN_W - 1)
    scale = d ** -0.5

    def row_fn(r):
        rs = jnp.clip(r - kh // 2, 0, rows - kh)
        q_r = lax.dynamic_index_in_dim(qg, r, axis=2, keepdims=False)
        k_rows = lax.dynamic_slice_in_dim(kg, rs, kh, axis=2)
        v_rows = lax.dynamic_slice_in_dim(vg, rs, kh, axis=2)
        k_win = k_rows[:, :, :, col_idx]
        v_win = v_rows[:, :, :, col_idx]
        row_off = rs + jnp.arange(kh) - r + (NA_WIN_H - 1)
        bias = rel_bias[:, row_off][:, :, col_off].transpose(0, 2, 1, 3)
        s = jnp.einsum('bhcd,bhacjd->bhcaj', q_r, k_win).astype(jnp.float32) * scale
        s = s + bias[None].astype(jnp.float32)
        p = jax.nn.softmax(s.reshape(B, H, GRID_W, kh * NA_WIN_W), axis=-1).reshape(s.shape)
        return jnp.einsum('bhcaj,bhacjd->bhcd', p.astype(v.dtype), v_win)

    out = lax.map(row_fn, jnp.arange(rows))
    return out.transpose(1, 0, 3, 2, 4).reshape(B, S, H * d)

def diff_attention(q, k, v, q_gain, k_gain, lq1, lk1, lq2, lk2, out_gain, lambda_init, cos, sin):
    B, S, _ = q.shape
    H, d = DIFF_HEADS, DIFF_QK_DIM
    n_rot = d // ROPE_FRACTION

    def prep(t, g):
        t = partial_rope(rms_norm(t.reshape(B, S, 2 * H, d), g), cos, sin, n_rot)
        return t.reshape(B, S, H, 2, d).transpose(3, 0, 2, 1, 4)

    q12 = prep(q, q_gain)
    k12 = prep(k, k_gain)
    vt = v.reshape(B, S, H, DIFF_V_DIM).transpose(0, 2, 1, 3)
    lam = (jnp.exp(jnp.sum(lq1.astype(jnp.float32) * lk1.astype(jnp.float32)))
           - jnp.exp(jnp.sum(lq2.astype(jnp.float32) * lk2.astype(jnp.float32))) + lambda_init)
    scale = d ** -0.5
    nb = S // Q_BLOCK
    qb = q12.reshape(2, B, H, nb, Q_BLOCK, d).transpose(3, 0, 1, 2, 4, 5)

    def block_fn(qblk):
        s = jnp.einsum('ibhqd,ibhkd->ibhqk', qblk, k12).astype(jnp.float32) * scale
        p = jax.nn.softmax(s, axis=-1)
        a = p[0] - lam * p[1]
        return jnp.einsum('bhqk,bhkd->bhqd', a.astype(vt.dtype), vt)

    o = lax.map(block_fn, qb)
    o = o.transpose(1, 2, 0, 3, 4).reshape(B, H, S, DIFF_V_DIM)
    o = rms_norm(o, out_gain) * (1.0 - lambda_init)
    return o.transpose(0, 2, 1, 3).reshape(B, S, H * DIFF_V_DIM)

def gqa_axial_attention(q, k, v, q_gain, k_gain, row_cs, col_cs):
    B, S, _ = q.shape
    Hq, Hkv, d = GQA_Q_HEADS, GQA_KV_HEADS, HEAD_DIM
    G = Hq // Hkv
    half = d // 2

    def axial(t):
        return jnp.concatenate([apply_rope(t[..., :half], *row_cs), apply_rope(t[..., half:], *col_cs)], axis=-1)

    q = axial(rms_norm(q.reshape(B, S, Hq, d), q_gain))
    k = axial(rms_norm(k.reshape(B, S, Hkv, d), k_gain))
    kt = k.transpose(0, 2, 1, 3)
    vt = v.reshape(B, S, Hkv, d).transpose(0, 2, 1, 3)
    nb = S // Q_BLOCK
    qb = q.reshape(B, nb, Q_BLOCK, Hkv, G, d).transpose(1, 0, 3, 4, 2, 5)
    scale = d ** -0.5

    def block_fn(qblk):
        s = jnp.einsum('bngqd,bnkd->bngqk', qblk, kt).astype(jnp.float32) * scale
        p = jax.nn.softmax(s, axis=-1)
        return jnp.einsum('bngqk,bnkd->bngqd', p.astype(vt.dtype), vt)

    o = lax.map(block_fn, qb)
    return o.transpose(1, 0, 4, 2, 3, 5).reshape(B, S, Hq * d)

def dilated_attention(q, k, v, q_gain, k_gain, cos, sin):
    B, S, _ = q.shape
    H, d = DIL_HEADS, HEAD_DIM
    n_rot = d // ROPE_FRACTION
    q = partial_rope(rms_norm(q.reshape(B, S, H, d), q_gain), cos, sin, n_rot).transpose(0, 2, 1, 3)
    k = partial_rope(rms_norm(k.reshape(B, S, H, d), k_gain), cos, sin, n_rot).transpose(0, 2, 1, 3)
    v = v.reshape(B, S, H, d).transpose(0, 2, 1, 3)
    nb = S // Q_BLOCK
    scale = d ** -0.5

    def block_fn(b):
        t = b * Q_BLOCK + jnp.arange(Q_BLOCK)
        q_b = lax.dynamic_slice_in_dim(q, b * Q_BLOCK, Q_BLOCK, axis=2)
        outs, lses = [], []
        for window, dil in DIL_PAIRS:
            n_side = (window // 2) // dil
            idx = t[:, None] + dil * jnp.arange(-n_side, n_side + 1)[None, :]
            valid = (idx >= 0) & (idx < S)
            idx = jnp.clip(idx, 0, S - 1)
            k_g = jnp.take(k, idx, axis=2)
            v_g = jnp.take(v, idx, axis=2)
            s = jnp.einsum('bhqd,bhqnd->bhqn', q_b, k_g).astype(jnp.float32) * scale
            s = jnp.where(valid[None, None], s, NEG_INF)
            lse = jax.nn.logsumexp(s, axis=-1, keepdims=True)
            p = jnp.exp(s - lse)
            outs.append(jnp.einsum('bhqn,bhqnd->bhqd', p.astype(v.dtype), v_g).astype(jnp.float32))
            lses.append(lse)
        w = jax.nn.softmax(jnp.stack(lses, axis=0), axis=0)
        return jnp.sum(w * jnp.stack(outs, axis=0), axis=0).astype(v.dtype)

    o = lax.map(block_fn, jnp.arange(nb))
    return o.transpose(1, 0, 3, 2, 4).reshape(B, S, H * d)

def first_inputs(seed: int = 0) -> dict:
    key = jax.random.key(seed)
    ks = jax.random.split(key, 32)
    L, D, F = DEPTH, D_MODEL, D_FF

    def w(i, shape, fan_in):
        return jax.random.normal(ks[i], shape, jnp.float32) * (fan_in ** -0.5)

    def gain(i, shape):
        return 1.0 + 0.02 * jax.random.normal(ks[i], shape, jnp.float32)

    def small(i, shape, sd):
        return sd * jax.random.normal(ks[i], shape, jnp.float32)

    return {
        'x': jax.random.normal(ks[0], (BATCH, SEQ, D), jnp.float32),
        'ffn1_norm': gain(1, (L, D)),
        'ffn1_w_gate': w(2, (L, D, F), D),
        'ffn1_w_up': w(3, (L, D, F), D),
        'ffn1_w_down': w(4, (L, F, D), F),
        'mix_norm': gain(5, (L, D)),
        'w_in': w(6, (L, D, IN_WIDTH), D),
        'w_out': w(7, (L, MIX_WIDTH, D), MIX_WIDTH),
        'na_q_norm': gain(8, (L, HEAD_DIM)),
        'na_k_norm': gain(9, (L, HEAD_DIM)),
        'na_rel_bias': small(10, (L, NA_HEADS, 2 * NA_WIN_H - 1, 2 * NA_WIN_W - 1), 0.02),
        'diff_q_norm': gain(11, (L, DIFF_QK_DIM)),
        'diff_k_norm': gain(12, (L, DIFF_QK_DIM)),
        'diff_lambda_q1': small(13, (L, DIFF_QK_DIM), 0.1),
        'diff_lambda_k1': small(14, (L, DIFF_QK_DIM), 0.1),
        'diff_lambda_q2': small(15, (L, DIFF_QK_DIM), 0.1),
        'diff_lambda_k2': small(16, (L, DIFF_QK_DIM), 0.1),
        'diff_out_norm': gain(17, (L, DIFF_V_DIM)),
        'gqa_q_norm': gain(18, (L, HEAD_DIM)),
        'gqa_k_norm': gain(19, (L, HEAD_DIM)),
        'dil_q_norm': gain(20, (L, HEAD_DIM)),
        'dil_k_norm': gain(21, (L, HEAD_DIM)),
        'ffn2_norm': gain(22, (L, D)),
        'ffn2_w_gate': w(23, (L, D, F), D),
        'ffn2_w_up': w(24, (L, D, F), D),
        'ffn2_w_down': w(25, (L, F, D), F),
    }

def first_block(x, ffn1_norm, ffn1_w_gate, ffn1_w_up, ffn1_w_down, mix_norm, w_in, w_out,
              na_q_norm, na_k_norm, na_rel_bias, diff_q_norm, diff_k_norm,
              diff_lambda_q1, diff_lambda_k1, diff_lambda_q2, diff_lambda_k2, diff_out_norm,
              gqa_q_norm, gqa_k_norm, dil_q_norm, dil_k_norm,
              ffn2_norm, ffn2_w_gate, ffn2_w_up, ffn2_w_down):
    B, S, _ = x.shape
    rows = S // GRID_W
    pos = jnp.arange(S, dtype=jnp.int32)
    diff_cs = rope_tables(pos, DIFF_QK_DIM // ROPE_FRACTION, ROPE_THETA)
    dil_cs = rope_tables(pos, HEAD_DIM // ROPE_FRACTION, ROPE_THETA)
    row_cs = rope_tables(pos // GRID_W, HEAD_DIM // 2, AXIAL_THETA)
    col_cs = rope_tables(pos % GRID_W, HEAD_DIM // 2, AXIAL_THETA)

    for l in range(DEPTH):
        h = rms_norm(x, ffn1_norm[l])
        x = x + 0.5 * swiglu(h, ffn1_w_gate[l], ffn1_w_up[l], ffn1_w_down[l])

        h = rms_norm(x, mix_norm[l])
        (na_q, na_k, na_v, df_q, df_k, df_v,
         gq_q, gq_k, gq_v, dl_q, dl_k, dl_v) = split_in_proj(h @ w_in[l])
        o_a = neighborhood_attention(na_q, na_k, na_v, na_q_norm[l], na_k_norm[l], na_rel_bias[l], rows)
        lambda_init = 0.8 - 0.6 * math.exp(-0.3 * l)
        o_b = diff_attention(df_q, df_k, df_v, diff_q_norm[l], diff_k_norm[l],
                             diff_lambda_q1[l], diff_lambda_k1[l], diff_lambda_q2[l], diff_lambda_k2[l],
                             diff_out_norm[l], lambda_init, *diff_cs)
        o_c = gqa_axial_attention(gq_q, gq_k, gq_v, gqa_q_norm[l], gqa_k_norm[l], row_cs, col_cs)
        o_d = dilated_attention(dl_q, dl_k, dl_v, dil_q_norm[l], dil_k_norm[l], *dil_cs)
        o = jnp.concatenate([o_a, o_b, o_c, o_d], axis=-1)
        x = x + o @ w_out[l]

        h = rms_norm(x, ffn2_norm[l])
        x = x + 0.5 * swiglu(h, ffn2_w_gate[l], ffn2_w_up[l], ffn2_w_down[l])
    return x


FOX_HEADS = 4
FOX_HEAD_DIM = 64
MOBA_HEADS = 4
MOBA_HEAD_DIM = 64
MOBA_BLOCK = 256
MOBA_TOPK = 3
MOBA_Q_CHUNK = 32
MLA_HEADS = 8
MLA_NOPE_DIM = 64
MLA_ROPE_DIM = 32
MLA_V_DIM = 64
MLA_Q_RANK = 256
MLA_KV_RANK = 128
ROPE_THETA_2 = 10000.0
T5_BUCKETS = 32
T5_MAX_DISTANCE = 128
D_FF_2 = -(-8 * D_MODEL // (3 * 256)) * 256

FOX_W = FOX_HEADS * FOX_HEAD_DIM
MOBA_W = MOBA_HEADS * MOBA_HEAD_DIM
MLA_W = MLA_HEADS * MLA_V_DIM
MIX_WIDTH_2 = FOX_W + MOBA_W + MLA_W
IN_SIZES_2 = (FOX_W, FOX_W, FOX_W, FOX_HEADS, MOBA_W, MOBA_W, MOBA_W, MLA_Q_RANK, MLA_KV_RANK, MLA_ROPE_DIM)
IN_WIDTH_2 = 3 * FOX_W + FOX_HEADS + 3 * MOBA_W + MLA_Q_RANK + MLA_KV_RANK + MLA_ROPE_DIM


def rmsnorm(x, g):
    x32 = x.astype(jnp.float32)
    y = x32 * lax.rsqrt(jnp.mean(x32 * x32, axis=-1, keepdims=True) + RMS_EPS)
    return (y * g.astype(jnp.float32)).astype(x.dtype)

def rope(x, pos):
    half = x.shape[-1] // 2
    inv_freq = 1.0 / (ROPE_THETA_2 ** (jnp.arange(half, dtype=jnp.float32) / half))
    ang = pos.astype(jnp.float32)[:, None] * inv_freq[None, :]
    cos, sin = jnp.cos(ang), jnp.sin(ang)
    x32 = x.astype(jnp.float32)
    x1, x2 = x32[..., :half], x32[..., half:]
    return jnp.concatenate([x1 * cos - x2 * sin, x2 * cos + x1 * sin], axis=-1).astype(x.dtype)

def t5_bucket(dist):
    n = jnp.maximum(dist, 0)
    max_exact = T5_BUCKETS // 2
    nf = jnp.maximum(n, max_exact).astype(jnp.float32)
    large = max_exact + (jnp.log(nf / max_exact) / math.log(T5_MAX_DISTANCE / max_exact)
                         * (T5_BUCKETS - max_exact)).astype(jnp.int32)
    large = jnp.minimum(large, T5_BUCKETS - 1)
    return jnp.where(n < max_exact, n, large)

def dense_causal_attention(q, k, v, log_decay_cum=None):
    B, H, S, dk = q.shape
    dv = v.shape[-1]
    nqb = S // Q_BLOCK
    scale = dk ** -0.5
    kpos = jnp.arange(S)
    q_blocks = q.reshape(B, H, nqb, Q_BLOCK, dk).transpose(2, 0, 1, 3, 4)
    starts = jnp.arange(nqb, dtype=jnp.int32) * Q_BLOCK
    if log_decay_cum is None:
        xs = (q_blocks, starts)
    else:
        xs = (q_blocks, starts, log_decay_cum.reshape(B, H, nqb, Q_BLOCK).transpose(2, 0, 1, 3))

    def step(blk):
        q_i, t0 = blk[0], blk[1]
        s = jnp.einsum('bhqd,bhkd->bhqk', q_i, k).astype(jnp.float32) * scale
        if log_decay_cum is not None:
            s = s + blk[2][..., None] - log_decay_cum[:, :, None, :]
        qpos = t0 + jnp.arange(Q_BLOCK)
        s = jnp.where(kpos[None, :] <= qpos[:, None], s, -jnp.inf)
        p = jax.nn.softmax(s, axis=-1)
        return jnp.einsum('bhqk,bhkd->bhqd', p.astype(v.dtype), v)

    out = lax.map(step, xs)
    return out.transpose(1, 2, 0, 3, 4).reshape(B, H, S, dv)

def moba_attention(q, k, v, t5_table):
    B, H, S, d = q.shape
    nb = -(-S // MOBA_BLOCK)
    s_pad = nb * MOBA_BLOCK
    n_sel = min(MOBA_TOPK, nb)
    scale = d ** -0.5
    pad = ((0, 0), (0, 0), (0, s_pad - S), (0, 0))
    k_blocks = jnp.pad(k, pad).reshape(B, H, nb, MOBA_BLOCK, d)
    v_blocks = jnp.pad(v, pad).reshape(B, H, nb, MOBA_BLOCK, d)
    k_mean = jnp.mean(k_blocks.astype(jnp.float32), axis=3)
    qpos = jnp.arange(S)
    gate = jnp.einsum('bhsd,bhnd->bhsn', q.astype(jnp.float32), k_mean)
    past = jnp.arange(nb)[None, :] < (qpos // MOBA_BLOCK)[:, None]
    gate = jnp.where(past, gate, -jnp.inf)
    _, sel = lax.top_k(gate, n_sel)

    nc = S // MOBA_Q_CHUNK
    q_c = q.reshape(B, H, nc, MOBA_Q_CHUNK, d).transpose(2, 0, 1, 3, 4)
    sel_c = sel.reshape(B, H, nc, MOBA_Q_CHUNK, n_sel).transpose(2, 0, 1, 3, 4)
    starts = jnp.arange(nc, dtype=jnp.int32) * MOBA_Q_CHUNK
    table_t = t5_table.T
    b_ix = jnp.arange(B)[:, None, None, None]
    h_ix = jnp.arange(H)[None, :, None, None]
    offs = jnp.arange(MOBA_BLOCK)

    def step(blk):
        q_i, sel_i, t0 = blk
        own = t0 // MOBA_BLOCK
        qp = t0 + jnp.arange(MOBA_Q_CHUNK)
        k_g = k_blocks[b_ix, h_ix, sel_i]
        v_g = v_blocks[b_ix, h_ix, sel_i]
        kp_sel = sel_i[..., None] * MOBA_BLOCK + offs
        bias_sel = table_t[h_ix[..., None], t5_bucket(qp[:, None, None] - kp_sel)]
        s_sel = jnp.einsum('bhqd,bhqnkd->bhqnk', q_i, k_g).astype(jnp.float32) * scale + bias_sel
        s_sel = jnp.where((sel_i < own)[..., None], s_sel, -jnp.inf)
        k_own = lax.dynamic_index_in_dim(k_blocks, own, axis=2, keepdims=False)
        v_own = lax.dynamic_index_in_dim(v_blocks, own, axis=2, keepdims=False)
        dist_own = qp[:, None] - (own * MOBA_BLOCK + offs)[None, :]
        s_own = (jnp.einsum('bhqd,bhkd->bhqk', q_i, k_own).astype(jnp.float32) * scale
                 + table_t[:, t5_bucket(dist_own)])
        s_own = jnp.where(dist_own >= 0, s_own, -jnp.inf)
        n_flat = n_sel * MOBA_BLOCK
        s = jnp.concatenate([s_sel.reshape(B, H, MOBA_Q_CHUNK, n_flat), s_own], axis=-1)
        p = jax.nn.softmax(s, axis=-1).astype(v.dtype)
        p_sel = p[..., :n_flat].reshape(B, H, MOBA_Q_CHUNK, n_sel, MOBA_BLOCK)
        p_own = p[..., n_flat:]
        return (jnp.einsum('bhqnk,bhqnkd->bhqd', p_sel, v_g)
                + jnp.einsum('bhqk,bhkd->bhqd', p_own, v_own))

    out = lax.map(step, (q_c, sel_c, starts))
    return out.transpose(1, 2, 0, 3, 4).reshape(B, H, S, d)

def hybrid_mixer(h, w_in, b_forget, g_q_lat, w_uq, g_kv_lat, w_ukv, g_group, w_out, t5_table):
    B, S, _ = h.shape
    proj = h @ w_in
    split_points = np.cumsum(IN_SIZES_2)[:-1].tolist()
    q_f, k_f, v_f, f_logit, q_m, k_m, v_m, c_q, c_kv, k_r = jnp.split(proj, split_points, axis=-1)

    def heads(t, n):
        return t.reshape(B, S, n, -1).transpose(0, 2, 1, 3)

    def flat(o):
        return o.transpose(0, 2, 1, 3).reshape(B, S, -1)

    pos = jnp.arange(S)
    log_f = jax.nn.log_sigmoid((f_logit + b_forget).astype(jnp.float32))
    F = jnp.cumsum(log_f, axis=1).transpose(0, 2, 1)
    o_f = dense_causal_attention(heads(q_f, FOX_HEADS), heads(k_f, FOX_HEADS), heads(v_f, FOX_HEADS), F)
    o_m = moba_attention(heads(q_m, MOBA_HEADS), heads(k_m, MOBA_HEADS), heads(v_m, MOBA_HEADS), t5_table)
    q_lat = heads(rmsnorm(c_q, g_q_lat) @ w_uq, MLA_HEADS)
    q_nope, q_rot = q_lat[..., :MLA_NOPE_DIM], q_lat[..., MLA_NOPE_DIM:]
    kv = heads(rmsnorm(c_kv, g_kv_lat) @ w_ukv, MLA_HEADS)
    k_nope, v_c = kv[..., :MLA_NOPE_DIM], kv[..., MLA_NOPE_DIM:]
    k_rot = rope(k_r[:, None], pos)
    q_c = jnp.concatenate([q_nope, rope(q_rot, pos)], axis=-1)
    k_c = jnp.concatenate([k_nope, jnp.broadcast_to(k_rot, (B, MLA_HEADS, S, MLA_ROPE_DIM))], axis=-1)
    o_c = dense_causal_attention(q_c, k_c, v_c)
    g_a, g_b, g_c = jnp.split(g_group, [FOX_W, FOX_W + MOBA_W])
    o = jnp.concatenate([rmsnorm(flat(o_f), g_a), rmsnorm(flat(o_m), g_b), rmsnorm(flat(o_c), g_c)], axis=-1)
    return o @ w_out

def swiglu_2(h, w_gate_up, w_down):
    g, u = jnp.split(h @ w_gate_up, 2, axis=-1)
    return (jax.nn.silu(g) * u) @ w_down

def second_inputs(seed: int = 0) -> dict:
    key = jax.random.key(seed)
    ks = jax.random.split(key, 20)
    f32 = jnp.float32

    def nrm(k, shape, scale):
        return jax.random.normal(k, shape, f32) * scale

    def gain(k, shape):
        return 1.0 + 0.1 * jax.random.normal(k, shape, f32)

    L = DEPTH
    return {
        'x': nrm(ks[0], (BATCH, SEQ, D_MODEL), 1.0),
        'c': nrm(ks[1], (BATCH, D_MODEL), 1.0),
        't5_table': nrm(ks[2], (T5_BUCKETS, MOBA_HEADS), 0.5),
        'w_ada': nrm(ks[3], (L, D_MODEL, 6 * D_MODEL), D_MODEL ** -0.5),
        'b_ada': nrm(ks[4], (L, 6 * D_MODEL), 0.02),
        'g_mix_pre': gain(ks[5], (L, D_MODEL)),
        'g_mix_post': gain(ks[6], (L, D_MODEL)),
        'w_in': nrm(ks[7], (L, D_MODEL, IN_WIDTH_2), D_MODEL ** -0.5),
        'b_forget': 2.0 + 0.5 * jax.random.normal(ks[8], (L, FOX_HEADS), f32),
        'g_q_lat': gain(ks[9], (L, MLA_Q_RANK)),
        'w_uq': nrm(ks[10], (L, MLA_Q_RANK, MLA_HEADS * (MLA_NOPE_DIM + MLA_ROPE_DIM)), MLA_Q_RANK ** -0.5),
        'g_kv_lat': gain(ks[11], (L, MLA_KV_RANK)),
        'w_ukv': nrm(ks[12], (L, MLA_KV_RANK, MLA_HEADS * (MLA_NOPE_DIM + MLA_V_DIM)), MLA_KV_RANK ** -0.5),
        'g_group': gain(ks[13], (L, MIX_WIDTH_2)),
        'w_out': nrm(ks[14], (L, MIX_WIDTH_2, D_MODEL), MIX_WIDTH_2 ** -0.5),
        'g_ffn_pre': gain(ks[15], (L, D_MODEL)),
        'g_ffn_post': gain(ks[16], (L, D_MODEL)),
        'w_gate_up': nrm(ks[17], (L, D_MODEL, 2 * D_FF_2), D_MODEL ** -0.5),
        'w_down': nrm(ks[18], (L, D_FF_2, D_MODEL), D_FF_2 ** -0.5),
    }

def second_block(x, c, t5_table, w_ada, b_ada, g_mix_pre, g_mix_post, w_in, b_forget, g_q_lat, w_uq,
              g_kv_lat, w_ukv, g_group, w_out, g_ffn_pre, g_ffn_post, w_gate_up, w_down):
    c_act = jax.nn.silu(c)
    for l in range(DEPTH):
        mod = (c_act @ w_ada[l] + b_ada[l])[:, None, :]
        shift_a, scale_a, gate_a, shift_f, scale_f, gate_f = jnp.split(mod, 6, axis=-1)
        h = rmsnorm(x, g_mix_pre[l]) * (1.0 + scale_a) + shift_a
        y = hybrid_mixer(h, w_in[l], b_forget[l], g_q_lat[l], w_uq[l], g_kv_lat[l], w_ukv[l],
                         g_group[l], w_out[l], t5_table)
        x = x + gate_a * rmsnorm(y, g_mix_post[l])
        h = rmsnorm(x, g_ffn_pre[l]) * (1.0 + scale_f) + shift_f
        x = x + gate_f * rmsnorm(swiglu_2(h, w_gate_up[l], w_down[l]), g_ffn_post[l])
    return x


def setup_inputs(seed=0):
    out = dict(first_inputs(seed))
    for name, value in second_inputs(seed + 1).items():
        if name != "x":
            out[name + "_2"] = value
    return out


def reference(
    x, ffn1_norm, ffn1_w_gate, ffn1_w_up, ffn1_w_down, mix_norm, w_in, w_out, na_q_norm,
    na_k_norm, na_rel_bias, diff_q_norm, diff_k_norm, diff_lambda_q1, diff_lambda_k1,
    diff_lambda_q2, diff_lambda_k2, diff_out_norm, gqa_q_norm, gqa_k_norm, dil_q_norm,
    dil_k_norm, ffn2_norm, ffn2_w_gate, ffn2_w_up, ffn2_w_down, c_2, t5_table_2, w_ada_2,
    b_ada_2, g_mix_pre_2, g_mix_post_2, w_in_2, b_forget_2, g_q_lat_2, w_uq_2, g_kv_lat_2,
    w_ukv_2, g_group_2, w_out_2, g_ffn_pre_2, g_ffn_post_2, w_gate_up_2, w_down_2,
):
    x = first_block(
        x, ffn1_norm, ffn1_w_gate, ffn1_w_up, ffn1_w_down, mix_norm, w_in, w_out, na_q_norm,
        na_k_norm, na_rel_bias, diff_q_norm, diff_k_norm, diff_lambda_q1, diff_lambda_k1,
        diff_lambda_q2, diff_lambda_k2, diff_out_norm, gqa_q_norm, gqa_k_norm, dil_q_norm,
        dil_k_norm, ffn2_norm, ffn2_w_gate, ffn2_w_up, ffn2_w_down,
    )
    return second_block(
        x, c_2, t5_table_2, w_ada_2, b_ada_2, g_mix_pre_2, g_mix_post_2, w_in_2, b_forget_2,
        g_q_lat_2, w_uq_2, g_kv_lat_2, w_ukv_2, g_group_2, w_out_2, g_ffn_pre_2, g_ffn_post_2,
        w_gate_up_2, w_down_2,
    )


_drawn_inputs = setup_inputs


def setup_inputs(seed=0):
    import zlib

    import numpy as np

    out = dict(_drawn_inputs(seed))
    spreads = {}
    factors = {'ffn1_norm': 4.075,
     'mix_norm': 2.83,
     'na_q_norm': 8.0,
     'na_k_norm': 8.0,
     'na_rel_bias': 34.966,
     'diff_q_norm': 6.767,
     'diff_k_norm': 7.377,
     'diff_lambda_k1': 3.935,
     'diff_out_norm': 12.795,
     'gqa_q_norm': 8.0,
     'gqa_k_norm': 8.0,
     'dil_q_norm': 8.0,
     'dil_k_norm': 8.0,
     'ffn2_norm': 5.401,
     'g_q_lat_2': 46.288,
     't5_table_2': 8.0,
     'b_ada_2': 8.0,
     'g_mix_pre_2': 5.769,
     'g_mix_post_2': 8.0,
     'b_forget_2': 8.0,
     'g_kv_lat_2': 8.0,
     'g_group_2': 8.0,
     'g_ffn_pre_2': 8.0,
     'g_ffn_post_2': 8.0}
    for name, (base, spread) in spreads.items():
        noise = np.random.default_rng([zlib.crc32(name.encode()), seed]).standard_normal(out[name].shape)
        drawn = base * np.exp(spread * noise) if base else spread * noise
        out[name] = __import__('jax').numpy.asarray(drawn.astype(out[name].dtype))
    for name, factor in factors.items():
        out[name] = (out[name] * factor).astype(out[name].dtype)
    return out
```

```python
import math
import numpy as np
import concourse.bass as bass
from concourse import mybir
from contextlib import ExitStack

L, D, S, F = 2, 1024, 256, 2816
NF = F // 128
EPS = 1e-6
BIG = 1e30
WIN_U, WIN_N = 8, 352
WIN2_U, WIN2_N = 6, 326
ADA_U, ADA_N = 16, 384
UNIT = 3072
RAW = 3

SMALL = []
for _l in range(L):
    SMALL += [(f"f1{_l}", 8), (f"mx{_l}", 8), (f"f2{_l}", 8), (f"os{_l}", 8), (f"la{_l}", 128),
              (f"pm{_l}", 8), (f"pf{_l}", 8), (f"pg{_l}", 8), (f"pq{_l}", 2), (f"pk{_l}", 1), (f"bf{_l}", 4)]
CONST = [("id", 128), ("pm", 256), ("ln", 512), ("U", 512), ("one", 1),
         ("dfc", 16), ("dfs", 16), ("dlc", 32), ("dls", 32), ("axc", 128), ("axs", 128), ("mlc", 64), ("mls", 64)]


def offsets(table):
    at, out = 0, {}
    for name, n in table:
        out[name] = (at, n)
        at += n
    return out, at


SM_OFF, SM_N = offsets(SMALL)
C_OFF, C_N = offsets(CONST)


class Recorder:

    def activation(self, *a, **k):
        return "activation", a, k

    def tensor_tensor(self, *a, **k):
        return "tensor_tensor", a, k

    def tensor_scalar(self, *a, **k):
        return "tensor_scalar", a, k

    def scalar_tensor_tensor(self, *a, **k):
        return "scalar_tensor_tensor", a, k

    def tensor_reduce(self, *a, **k):
        return "tensor_reduce", a, k

    def tensor_copy(self, *a, **k):
        return "tensor_copy", a, k

    def reciprocal(self, *a, **k):
        return "reciprocal", a, k

    def matmul(self, *a, **k):
        return "matmul", a, k

    def transpose(self, *a, **k):
        return "transpose", a, k

    def dma_start(self, *a, **k):
        return "dma_start", a, k

    def memset(self, *a, **k):
        return "memset", a, k


CALLS = {
    "activation": lambda e, a, k: e.activation(*a, **k),
    "tensor_tensor": lambda e, a, k: e.tensor_tensor(*a, **k),
    "tensor_scalar": lambda e, a, k: e.tensor_scalar(*a, **k),
    "scalar_tensor_tensor": lambda e, a, k: e.scalar_tensor_tensor(*a, **k),
    "tensor_reduce": lambda e, a, k: e.tensor_reduce(*a, **k),
    "tensor_copy": lambda e, a, k: e.tensor_copy(*a, **k),
    "reciprocal": lambda e, a, k: e.reciprocal(*a, **k),
    "matmul": lambda e, a, k: e.matmul(*a, **k),
    "transpose": lambda e, a, k: e.transpose(*a, **k),
    "dma_start": lambda e, a, k: e.dma_start(*a, **k),
    "memset": lambda e, a, k: e.memset(*a, **k),
}
recorder = Recorder()


def program(nc, d, out):
    f32, f32r = mybir.dt.float32, mybir.dt.float32r
    ACT, ALU, AX = mybir.ActivationFunctionType, mybir.AluOpType, mybir.AxisListType

    with ExitStack() as ctx:
        def sb(name, shape, dt=f32):
            return ctx.enter_context(nc.sbuf_tensor(name, shape, dt))

        def semaphore(name):
            return ctx.enter_context(nc.semaphore(name))

        X = sb("X", [128, 2, D])
        raw = [sb(f"raw{i}", [128, UNIT]) for i in range(RAW)]
        Wh = [sb(f"Wh{i}", [128, UNIT], f32r) for i in range(2)]
        Wl = [sb(f"Wl{i}", [128, UNIT], f32r) for i in range(2)]
        Hh = sb("Hh", [128, 8, S], f32r)
        Hl = sb("Hl", [128, 8, S], f32r)
        ah = [sb(f"ah{i}", [128, S], f32r) for i in range(2)]
        al = [sb(f"al{i}", [128, S], f32r) for i in range(2)]
        A = sb("A", [128, 2, 2816])
        QT = sb("QT", [128, 24, S])
        BT = sb("BT", [128, 2, 4, S])
        GQ = sb("GQ", [128, 1920])
        SB = sb("SB", [128, 2, 2, S])
        PB = sb("PB", [128, 2, 2, S])
        PT = sb("PT", [128, 2, 4, 128])
        HT = PT[:, :, :, :].rearrange("p a b c -> p (a b c)").rearrange("p (a b) -> p a b", a=4)
        G = sb("G", [128, D])
        SM = sb("SM", [128, SM_N])
        CT = sb("CT", [128, C_N])
        mhalf = sb("mhalf", [128, 64])
        st = sb("st", [128, 512])
        acc = sb("acc", [128, ADA_N])
        adab = sb("adab", [1, ADA_N])
        mcol = sb("mcol", [128, 4, 8])
        PS = ctx.enter_context(nc.psum_tensor("PS", [128, 8, 512], f32))
        modd = nc.dram_tensor("mod_scratch", (L, 6 * D), f32, kind="Internal").ap()

        def sm(name, a=0, b=None):
            o, n = SM_OFF[name]
            return SM[:, o + a:o + (n if b is None else b)]

        def cn(name, a=0, b=None):
            o, n = C_OFF[name]
            return CT[:, o + a:o + (n if b is None else b)]

        ident = cn("id")

        names = ["pe", "act", "dve", "pool"]
        sems = {n: semaphore("s_" + n) for n in names}
        count = {n: 0 for n in names}
        queue = {n: [] for n in names + ["sp"]}
        waited = {n: {} for n in queue}

        def emit(eng, fn, after, sem, by):
            for key, v in after:
                if waited[eng].get(key, 0) < v:
                    waited[eng][key] = v
                    queue[eng].append((("wait_ge", (key, v), {}), None, 0))
            if sem is None:
                queue[eng].append((fn(recorder), None, 0))
                return None
            count[sem] = count.get(sem, 0) + by
            queue[eng].append((fn(recorder), sem, by))
            return (sem, count[sem])

        def V(fn, *after):
            return emit("dve", fn, after, "dve", 1)

        def AC(fn, *after):
            return emit("act", fn, after, "act", 1)

        def GP(fn, *after):
            return emit("pool", fn, after, "pool", 1)

        def PE(fn, *after, inc=False):
            return emit("pe", fn, after, "pe" if inc else None, 1)

        def DMA(eng, sem, dst, src, *after, slow=False):
            if sem not in sems:
                sems[sem] = semaphore("d_" + sem)
            kw = dict(allow_slow_non_contiguous=True) if slow else {}
            return emit(eng, lambda e: e.dma_start(dst, src, **kw), after, sem, 16)

        free = [() for _ in range(8)]

        units = []

        def ffn_units(k, ada):
            for f in range(NF):
                units.append(("w", d["ffn"][k * NF + f], [(0, 1024), (1024, 2048), (2048, 3072)]))
                if f in ada:
                    units.append(("a", ada[f], None))

        def cparts(nch, n):
            cut = [0, 3, 6, 8] if nch == 8 else list(range(nch + 1))
            return [(a * n, b * n) for a, b in zip(cut, cut[1:])]

        def ada_plan(l, first):
            return {2 * i + 2: (l, first + i) for i in range(8)}

        for l in range(L):
            ffn_units(2 * l, ada_plan(l, 0))
            for u in range(WIN_U):
                units.append(("w", d["win"][l * WIN_U + u], cparts(8, WIN_N)))
            for a, b in ((0, 3), (3, 6), (6, 8)):
                units.append(("w", d["wo"][l][:, a * D:b * D], cparts(b - a, D)))
            ffn_units(2 * l + 1, ada_plan(l, 8))
        for l in range(L):
            for u in range(WIN2_U):
                units.append(("w", d["win2"][l * WIN2_U + u], cparts(8, WIN2_N)))
            units.append(("w", d["lat"][l], [(0, 768), (768, 1536), (1536, 2560)]))
            for a, b in ((0, 3), (3, 6), (6, 8)):
                units.append(("w", d["wo"][L + l][:, a * D:b * D], cparts(b - a, D)))
            ffn_units(4 + l, {})

        wslot = {}
        for n, u in enumerate(units):
            if u[0] == "w":
                wslot[n] = len(wslot) % 2
        order = [n for n, u in enumerate(units) if u[0] == "w"]
        pos = {n: i for i, n in enumerate(order)}
        loaded, raw_free = {}, {}
        ready = {}
        done = {}
        state = {"load": 0, "unit": 0, "part": 0, "cur": 0}
        ada_wait = []
        mod_written = {0: [], 1: []}

        def load_next():
            n = state["load"]
            if n >= len(units) or (n >= RAW and n - RAW not in raw_free):
                return False
            kind, src, _ = units[n]
            if kind == "a":
                src = d["ada"][src[0] * ADA_U + src[1]]
            w = src.shape[-1]
            loaded[n] = DMA("sp", f"raw{n % RAW}", raw[n % RAW][:, 0:w], src, *raw_free.get(n - RAW, ()))
            state["load"] += 1
            return True

        def released(n, k):
            i = pos[n] - 2
            if i < 0:
                return ()
            prev = order[i]
            a, b = units[n][2][k]
            got = []
            for j, (pa, pb) in enumerate(units[prev][2]):
                if pa < b and a < pb:
                    if (prev, j) not in done:
                        return None
                    got.append(done[prev, j])
            return got

        def tick():
            n, k = state["unit"], state["part"]
            if n >= len(units):
                return False
            while load_next():
                pass
            if n not in loaded:
                return False
            kind, src, parts = units[n]
            r = raw[n % RAW]
            if kind == "w":
                rel = released(n, k)
                if rel is None:
                    return False
                a, b = parts[k]
                h, lo = Wh[wslot[n]], Wl[wslot[n]]
                t1 = AC(lambda e: e.activation(h[:, a:b], r[:, a:b], ACT.Copy), loaded[n], *rel)
                t2 = V(lambda e: e.tensor_tensor(lo[:, a:b], r[:, a:b], h[:, a:b].bitcast(f32), ALU.subtract),
                       loaded[n], t1, *rel)
                ready[n, k] = (t1, t2)
                last = k == len(parts) - 1
                if last:
                    raw_free[n] = (t1, t2)
            else:
                l, g = src
                if k == 0 and ada_wait:
                    return False
                w = r[:, :].rearrange("p (c n) -> p c n", c=8)
                cc = d["_cact"]
                if k == 0:
                    t = V(lambda e: e.tensor_scalar(acc[:, :], w[:, 0, :], cc[:, 0:1], None, ALU.mult),
                          loaded[n], d["_cact_tok"], *d["_acc_free"])
                else:
                    t = V(lambda e: e.scalar_tensor_tensor(out=acc[:, :], in0=w[:, k, :], scalar=cc[:, k:k + 1],
                                                           in1=acc[:, :], op0=ALU.mult, op1=ALU.add),
                          d["_acc_tok"])
                d["_acc_tok"] = t
                last = k == 7
                if last:
                    raw_free[n] = (t,)
                    ada_wait.append((l, g, t))
            state["part"] += 1
            if last:
                state["unit"] += 1
                state["part"] = 0
                while load_next():
                    pass
            return True

        def need(n, k):
            while (n, k) not in ready:
                assert tick(), (n, k, state)
            return ready[n, k]

        def next_unit():
            while units[state["cur"]][0] != "w":
                state["cur"] += 1
            state["cur"] += 1
            return state["cur"] - 1

        def ada_finish(bank):
            if not ada_wait:
                return
            l, g, t = ada_wait.pop()
            cols = slice(g * ADA_N, (g + 1) * ADA_N)
            tb = DMA("sp", "adab", adab[:, :], d["b_ada"][l:l + 1, cols], *d["_adab_free"])
            tp = PE(lambda e: e.matmul(PS[0:1, bank, 0:ADA_N], cn("one"), acc[:, :], start=True, stop=True),
                    t, tc, *free[bank], inc=True)
            tv = V(lambda e: e.tensor_tensor(adab[:, :], PS[0:1, bank, 0:ADA_N], adab[:, :], ALU.add),
                   tp, tb)
            to = DMA("sp", "mod", modd[l:l + 1, cols], adab[:, :], tv)
            free[bank] = (tv,)
            d["_acc_free"], d["_adab_free"] = (tp,), (to,)
            mod_written[l].append(to)

        tc = DMA("act", "ct", CT[:, :], d["const"])
        tsm = DMA("act", "sm", SM[:, :], d["small"])
        tx0 = DMA("act", "x", X[:, :, :], d["x"].rearrange("(t p) n -> p t n", t=2))
        tcc = DMA("act", "cc", st[:, 0:8], d["c"])
        for _ in range(RAW):
            load_next()
        tmh = GP(lambda e: e.memset(mhalf[:, :], -0.5))
        cact = sb("cact", [128, 8])
        t = AC(lambda e: e.activation(cact[:, :], st[:, 0:8], ACT.Silu), tcc)
        d["_cact"], d["_cact_tok"] = cact, t
        d["_acc_free"], d["_adab_free"] = (), ()
        st_cact = t

        SS, RS, NM, Z, ZR, LA, LF, FQ = 16, 80, 144, 160, 240, 320, 330, 400

        def rstd(a, b, n, *after, mul=None):
            s, r = st[:, SS + a:SS + b], st[:, RS + a:RS + b]
            t = GP(lambda e: e.tensor_scalar(s, s, 1.0 / n, EPS, ALU.mult, ALU.add), *after)
            t = GP(lambda e: e.tensor_tensor(r, s, mhalf[:, 0:b - a], ALU.pow), t, tmh)
            if mul is not None:
                t = GP(lambda e: e.tensor_scalar(r, r, mul, None, ALU.mult), t)
            return t

        def to_T(src, cols, scale, shift, after, banks=(4, 5, 6, 7), dst0=0):
            got = []
            n = len(cols)
            for j in range(0, n, 2):
                b = banks[(j // 2) % len(banks)]
                two = range(j, min(j + 2, n))
                for i in two:
                    for t in range(2):
                        tp = PE(lambda e, i=i, t=t: e.transpose(
                            PS[:, b, (i % 2) * S + t * 128:(i % 2) * S + t * 128 + 128],
                            src[:, t, cols[i]:cols[i] + 128], ident), tc, *after[t], *free[b], inc=True)
                for i in two:
                    p = PS[:, b, (i % 2) * S:(i % 2) * S + S]
                    ht = HT[:, i % 4, :]
                    sc = scale[:, i:i + 1]
                    w = [tp, *d["_ht_free"][i % 4], *d["_h_free"], *d["_colw"]]
                    if shift is None:
                        t1 = V(lambda e: e.tensor_scalar(ht, p, sc, None, ALU.mult), *w)
                    else:
                        t1 = V(lambda e: e.tensor_scalar(ht, p, sc, shift[:, i:i + 1], ALU.mult, ALU.add), *w)
                    t2 = AC(lambda e: e.activation(Hh[:, dst0 + i, :], ht, ACT.Copy), t1, *d["_h_free"])
                    t3 = V(lambda e, i=i, ht=ht: e.tensor_tensor(Hl[:, dst0 + i, :], ht,
                                                                 Hh[:, dst0 + i, :].bitcast(f32), ALU.subtract), t1, t2)
                    d["_ht_free"][i % 4] = (t3,)
                    got.append((t2, t3))
                free[b] = (t1,)
            return got

        d["_ht_free"] = [(), (), (), ()]
        d["_h_free"] = ()
        d["_colw"] = (tsm,)
        x_tok = [(tx0,), (tx0,)]
        a_free = [()]

        def norm_T(scale, shift=None):
            xn = A
            ts = []
            for t in range(2):
                q = AC(lambda e, t=t: e.activation(xn[:, t, 0:D], X[:, t, :], ACT.Square,
                                                   accum_out=st[:, SS + t:SS + t + 1]),
                       *x_tok[t], *a_free[0], *d.get("_rs_free", ()))
                r = rstd(t, t + 1, D, q)
                ts.append((V(lambda e, t=t: e.tensor_scalar(xn[:, t, 0:D], X[:, t, :], st[:, RS + t:RS + t + 1],
                                                            None, ALU.mult), r, q),))
            d["_rs_free"] = (ts[0][0], ts[1][0])
            got = to_T(xn, [128 * c for c in range(8)], scale, shift, ts)
            a_free[0] = got[-1]
            return got

        def three(out_, xh, xl, wh, wl, first, last, *after, inc=False):
            PE(lambda e: e.matmul(out_, xh, wh, start=first, stop=False), *after)
            PE(lambda e: e.matmul(out_, xh, wl, start=False, stop=False))
            return PE(lambda e: e.matmul(out_, xl, wh, start=False, stop=last), inc=inc)

        def threeT(out_, xh, xl, wh, wl, first, last, *after, inc=False):
            PE(lambda e: e.matmul(out_, wh, xh, start=first, stop=False), *after)
            PE(lambda e: e.matmul(out_, wh, xl, start=False, stop=False))
            return PE(lambda e: e.matmul(out_, wl, xh, start=False, stop=last), inc=inc)

        def ffn(h_tok):
            sgt = SB[:, :, 0, :]
            att = SB[:, :, 1, :]
            silu_free = [d["_sb_free"], d["_sb_free"]]
            a_rel = d["_a_rel"]
            pend = None

            def down(f, n, s, tk):
                w = need(n, 2)
                h, lo = Wh[wslot[n]], Wl[wslot[n]]
                for t in range(2):
                    for j in range(2):
                        c = slice(2048 + 512 * j, 2560 + 512 * j)
                        tt = three(PS[:, 2 * t + j, :], ah[s][:, t * 128:t * 128 + 128], al[s][:, t * 128:t * 128 + 128],
                                   h[:, c], lo[:, c], f == 0, f == NF - 1, *w, *tk,
                                   *(free[2 * t + j] if f == 0 else ()), inc=(t == 1 and j == 1) or f == NF - 1)
                        if f == NF - 1:
                            last[2 * t + j] = tt
                done[n, 2] = tt
                a_rel[s] = (tt,)

            last = {}
            for f in range(NF):
                n = next_unit()
                b = 4 + f % 2
                s = f % 2
                h, lo = Wh[wslot[n]], Wl[wslot[n]]
                for m in range(2):
                    w = need(n, m)
                    for c in range(8):
                        cc = slice(m * 1024 + c * 128, m * 1024 + c * 128 + 128)
                        tp = threeT(PS[:, b, m * S:m * S + S], Hh[:, c, :], Hl[:, c, :], h[:, cc], lo[:, cc],
                                    c == 0, c == 7, *w, *h_tok[c], *(free[b] if c == 0 and m == 0 else ()), inc=c == 7)
                    done[n, m] = tp
                    if m == 0:
                        tg = tp
                        need(n, 1)
                ada_finish(7)
                need(n, 2)
                tick()
                ts = AC(lambda e: e.activation(sgt[:, s, :], PS[:, b, 0:S], ACT.Silu), tp, *silu_free[s])
                tm = V(lambda e, s=s: e.tensor_tensor(att[:, s, :], sgt[:, s, :], PS[:, b, S:2 * S], ALU.mult), ts, tp,
                       *silu_free[s])
                free[b] = (ts, tm)
                tick()
                t1 = AC(lambda e, s=s: e.activation(ah[s][:, :], att[:, s, :], ACT.Copy), tm, *a_rel[s])
                t2 = V(lambda e, s=s: e.tensor_tensor(al[s][:, :], att[:, s, :], ah[s][:, :].bitcast(f32), ALU.subtract),
                       t1, *a_rel[s])
                silu_free[s] = (t2,)
                if pend is not None:
                    down(*pend)
                    tick()
                pend = (f, n, s, (t1, t2))
                d["_h_free"] = (tp,)
            down(*pend)
            tick()
            ada_finish(7)
            d["_sb_free"] = silu_free[0] + silu_free[1]
            return last

        d["_a_rel"] = [(), ()]
        d["_sb_free"] = ()

        def residual(last, scale):
            for t in range(2):
                tt = []
                for j in range(2):
                    xs = X[:, t, j * 512:j * 512 + 512]
                    v = V(lambda e, xs=xs, t=t, j=j: e.scalar_tensor_tensor(
                        out=xs, in0=PS[:, 2 * t + j, :], scalar=scale, in1=xs, op0=ALU.mult, op1=ALU.add),
                        last[2 * t + j], *x_tok[t])
                    free[2 * t + j] = (v,)
                    tt.append(v)
                x_tok[t] = tuple(tt)

        def post_norm(last, g_tok):
            for t in range(2):
                q = AC(lambda e, t=t: e.activation(A[:, t, 0:D].rearrange("p (j n) -> p j n", j=2),
                                                   PS[:, 2 * t:2 * t + 2, :], ACT.Square,
                                                   accum_out=st[:, SS + t:SS + t + 1]),
                       last[2 * t], last[2 * t + 1], *a_free[0], *d["_rs_free"])
                r = rstd(t, t + 1, D, q)
                v = V(lambda e, t=t: e.scalar_tensor_tensor(
                    out=A[:, t, 0:D].rearrange("p (j n) -> p j n", j=2), in0=PS[:, 2 * t:2 * t + 2, :],
                    scalar=st[:, RS + t:RS + t + 1], in1=G[:, :].rearrange("p (j n) -> p j n", j=2),
                    op0=ALU.mult, op1=ALU.mult), r, q, g_tok)
                free[2 * t] = free[2 * t + 1] = (v,)
                v2 = V(lambda e, t=t: e.tensor_tensor(X[:, t, :], X[:, t, :], A[:, t, 0:D], ALU.add), v, *x_tok[t])
                x_tok[t] = (v2,)
            d["_rs_free"] = (v,)
            d["_g_free"] = (v,)
            a_free[0] = (v2,)

        def project(h_tok, nunits, ncol):
            got = []
            for u in range(nunits):
                n = next_unit()
                h, lo = Wh[wslot[n]], Wl[wslot[n]]
                for t in range(2):
                    b = (u % 2) * 2 + t
                    for c in range(8):
                        k = min(c // 3, 2)
                        w = need(n, k)
                        cc = slice(c * ncol, (c + 1) * ncol)
                        ts = slice(t * 128, t * 128 + 128)
                        tp = three(PS[:, b, 0:ncol], Hh[:, c, ts], Hl[:, c, ts], h[:, cc], lo[:, cc], c == 0, c == 7,
                                   *w, *h_tok[c], *(free[b] if c == 0 else ()), inc=c in (2, 5, 7))
                        if t == 1 and c in (2, 5, 7):
                            done[n, k] = tp
                    for _ in range(2):
                        tick()
                    dst = A[:, t, u * ncol:(u + 1) * ncol]
                    if t == 0:
                        e0 = AC(lambda e, dst=dst, b=b: e.activation(dst, PS[:, b, 0:ncol], ACT.Copy), tp, *a_free[0])
                        free[b] = (e0,)
                    else:
                        e1 = V(lambda e, dst=dst, b=b: e.tensor_copy(dst, PS[:, b, 0:ncol]), tp, *a_free[0])
                        free[b] = (e1,)
                got.append((e0, e1))
            d["_h_free"] = (tp,)
            return got

        def out_proj(h_tok):
            last = {}
            for a, b2 in ((0, 3), (3, 6), (6, 8)):
                n = next_unit()
                h, lo = Wh[wslot[n]], Wl[wslot[n]]
                for c in range(a, b2):
                    w = need(n, c - a)
                    for t in range(2):
                        for j in range(2):
                            cc = slice((c - a) * D + j * 512, (c - a) * D + j * 512 + 512)
                            ts = slice(t * 128, t * 128 + 128)
                            tp = three(PS[:, 2 * t + j, :], Hh[:, c, ts], Hl[:, c, ts], h[:, cc], lo[:, cc],
                                       c == 0, c == 7, *w, *h_tok[c], *(free[2 * t + j] if c == 0 else ()),
                                       inc=c == 7 or (t == 1 and j == 1))
                            if c == 7:
                                last[2 * t + j] = tp
                    done[n, c - a] = tp
                    tick()
            d["_h_free"] = (tp,)
            return last

        def transposes(jobs, after, banks):
            got = {}
            for i0 in range(0, len(jobs), 2):
                b = banks[(i0 // 2) % len(banks)]
                grp = jobs[i0:i0 + 2]
                for k, (src, blk, m) in enumerate(grp):
                    for t in range(2):
                        tp = PE(lambda e, k=k, t=t, src=src, m=m: e.transpose(
                            PS[0:m, b, k * S + t * 128:k * S + t * 128 + 128], src(t), ident),
                            tc, *after, *free[b], inc=True)
                blk0, m = grp[0][1], grp[0][2]
                g = len(grp)
                assert all(q[1] == blk0 + k and q[2] == m for k, q in enumerate(grp))
                dst = QT[0:m, blk0:blk0 + g, :]
                src = PS[0:m, b, 0:g * S].rearrange("p (k s) -> p k s", k=g)
                if (i0 // 2) % 2:
                    tv = V(lambda e, dst=dst, src=src: e.tensor_copy(dst, src), tp, *d["_qt_free"])
                else:
                    tv = AC(lambda e, dst=dst, src=src: e.activation(dst, src, ACT.Copy), tp, *d["_qt_free"])
                free[b] = (tv,)
                for k in range(g):
                    got[blk0 + k] = tv
            return got

        def rope(xs, cs, ss, h, ta, tb, *after):
            t1 = V(lambda e: e.tensor_tensor(ta, xs, cs, ALU.mult), *after)
            t2 = V(lambda e: e.tensor_tensor(tb[..., 0:h], xs[..., h:2 * h], ss[..., 0:h], ALU.mult), *after)
            t3 = V(lambda e: e.tensor_tensor(tb[..., h:2 * h], xs[..., 0:h], ss[..., h:2 * h], ALU.mult), *after)
            return V(lambda e: e.tensor_tensor(xs, ta, tb, ALU.add), t1, t2, t3)

        def attention(items):
            n = len(items)
            sS = [None] * n
            sE = [None] * n
            sP = [None] * n
            sb_free = [d["_sb_free"], d["_sb_free"]]
            pb_free = [(), ()]
            pt_free = [(), ()]
            outs = []

            def stage_a(i):
                it = items[i]
                t, nk, s = it["t"], it["nk"], i % 2
                b = 2 * s
                for k, (q, kk, _) in enumerate(it["heads"]):
                    tp = PE(lambda e, q=q, kk=kk, k=k: e.matmul(PS[:, b + k, 0:nk], q, kk, start=True, stop=True),
                            *it["after"], *free[b + k], inc=k == 1)
                src = PS[:, b:b + 2, 0:nk]
                nm = st[:, NM + 2 * s:NM + 2 * s + 2]
                if it["bias"] is not None:
                    dst = SB[:, s, :, 0:nk]
                    tb = V(lambda e, src=src, dst=dst: e.scalar_tensor_tensor(
                        out=dst, in0=src, scalar=it["scale"], in1=it["bias"], op0=ALU.mult, op1=it["op"]),
                        tp, *sb_free[s], *it["after"])
                    free[b] = free[b + 1] = (tb,)
                    tm = V(lambda e, dst=dst: e.tensor_reduce(nm, dst, AX.X, ALU.max, negate=True), tb,
                           *sb_free[s])
                    src, sc = dst, 1.0
                else:
                    tb = tp
                    tm0 = V(lambda e, src=src: e.tensor_reduce(nm, src, AX.X, ALU.max, negate=True), tp, *sb_free[s])
                    tm = V(lambda e: e.tensor_scalar(nm, nm, it["scale"], None, ALU.mult), tm0)
                    sc = it["scale"]
                for k in range(2):
                    te = AC(lambda e, k=k, src=src, sc=sc: e.activation(
                        PB[:, s, k, 0:nk], src[:, k, :], ACT.Exp, bias=nm[:, k:k + 1], scale=sc,
                        accum_out=st[:, Z + 2 * i + k:Z + 2 * i + k + 1]), tb, tm, *pb_free[s], *d["_z_free"])
                sb_free[s] = (te,)
                if it["bias"] is None:
                    free[b] = free[b + 1] = (te, tm)
                sE[i] = te

            def stage_b(i):
                it = items[i]
                nk, s = it["nk"], i % 2
                nc_ = nk // 128
                b = 4 + s
                for k in range(2):
                    for c in range(nc_):
                        tp = PE(lambda e, k=k, c=c: e.transpose(
                            PS[:, b, (k * nc_ + c) * 128:(k * nc_ + c) * 128 + 128],
                            PB[:, s, k, c * 128:c * 128 + 128], ident), sE[i], *free[b], inc=True)
                w = 2 * nc_
                dst = PT[:, s, 0:w, :]
                src = PS[:, b, 0:w * 128].rearrange("p (a q) -> p a q", a=w)
                if i % 2:
                    te = V(lambda e: e.tensor_copy(dst, src), tp, *pt_free[s])
                else:
                    te = AC(lambda e: e.activation(dst, src, ACT.Copy), tp, *pt_free[s])
                pb_free[s] = (tp,)
                free[b] = (te,)
                sP[i] = te

            def stage_c(i):
                it = items[i]
                nk, s, t = it["nk"], i % 2, it["t"]
                nc_ = nk // 128
                b = 6 + s
                for k, (_, _, v) in enumerate(it["heads"]):
                    for c in range(nc_):
                        tp = PE(lambda e, k=k, c=c, v=v: e.matmul(
                            PS[:, b, k * 64:k * 64 + 64], PT[:, s, k * nc_ + c, :], v[c],
                            start=c == 0, stop=c == nc_ - 1), sP[i], *it["after"], *free[b], inc=k == 1 and c == nc_ - 1)
                pt_free[s] = (tp,)
                zr = st[:, ZR + 2 * i:ZR + 2 * i + 2]
                z = st[:, Z + 2 * i:Z + 2 * i + 2]
                t1 = V(lambda e: e.reciprocal(zr, z), sE[i], *d["_z_free"])
                if it["diff"]:
                    t2 = V(lambda e: e.tensor_tensor(zr[:, 1:2], zr[:, 1:2], st[:, LA:LA + 1], ALU.mult), t1,
                           it["lam"])
                    tmp = st[:, FQ + 32:FQ + 96]
                    t3 = V(lambda e: e.tensor_scalar(tmp, PS[:, b, 64:128], zr[:, 1:2], None, ALU.mult), t2, tp)
                    t4 = V(lambda e: e.scalar_tensor_tensor(
                        out=A[:, t, it["out"]:it["out"] + 64], in0=PS[:, b, 0:64], scalar=zr[:, 0:1], in1=tmp,
                        op0=ALU.mult, op1=ALU.add), t3, *it["ofree"])
                else:
                    o = A[:, t, it["out"]:it["out"] + 128].rearrange("p (k n) -> p k n", k=2)
                    t4 = V(lambda e: e.tensor_tensor(
                        o, PS[:, b, 0:128].rearrange("p (k n) -> p k n", k=2),
                        zr.unsqueeze(2).to_broadcast([128, 2, 64]), ALU.mult), t1, tp, *it["ofree"])
                free[b] = (t4,)
                outs.append(t4)

            for i in range(n + 2):
                if i < n:
                    stage_a(i)
                if 0 <= i - 1 < n:
                    stage_b(i - 1)
                if 0 <= i - 2 < n:
                    stage_c(i - 2)
                if i % 3 == 0:
                    tick()
            d["_sb_free"] = sb_free[0] + sb_free[1] + (outs[-1],)
            d["_qt_free"] = (outs[-1], sP[-1])
            d["_z_free"] = (outs[-1],)
            return outs

        d["_z_free"] = ()
        d["_qt_free"] = ()
        d["_rs_free"] = ()
        d["_g_free"] = ()
        d["_bt_free"] = ()
        d["_gq_free"] = ()

        def bc(ap, shape):
            return ap.to_broadcast(shape)

        def first_mixer(l):
            tbt = DMA("sp", "bt", BT[:, :, :, :], d["nab"][l], *d["_bt_free"])
            tgq = DMA("sp", "gq", GQ[:, :], d["gq"][l], *d["_gq_free"])
            lam_init = 0.8 - 0.6 * math.exp(-0.3 * l)
            la = sm(f"la{l}")
            lt = st[:, FQ + 32:FQ + 96].rearrange("p (a n) -> p a n", a=2)
            t = V(lambda e: e.tensor_tensor(lt, la.rearrange("p (a b n) -> p a b n", a=2, b=2)[:, :, 0, :],
                                            la.rearrange("p (a b n) -> p a b n", a=2, b=2)[:, :, 1, :], ALU.mult),
                  tsm, *d["_z_free"])
            t = V(lambda e: e.tensor_reduce(st[:, LA:LA + 2], lt, AX.X, ALU.add), t)
            h_tok = norm_T(sm(f"mx{l}"))
            t = AC(lambda e: e.activation(st[:, LA + 2:LA + 4], st[:, LA:LA + 2], ACT.Exp), t)
            t = V(lambda e: e.tensor_scalar(st[:, LA + 3:LA + 4], st[:, LA + 3:LA + 4], -lam_init, None, ALU.add), t)
            lam_tok = V(lambda e: e.tensor_tensor(st[:, LA:LA + 1], st[:, LA + 3:LA + 4], st[:, LA + 2:LA + 3],
                                                  ALU.subtract), t)
            pr = project(h_tok, WIN_U, WIN_N)
            sqf = QT[:, :, :].rearrange("p a b -> p (a b)")
            sq = sqf[:, 0:2816].rearrange("p (t h n) -> p t h n", t=2, h=22)
            qk = A[:, :, 0:1408].rearrange("p t (h n) -> p t h n", n=64)
            sq2 = sqf[:, 2816:3840].rearrange("p (t h n) -> p t h n", t=2, h=16)
            qk2 = A[:, :, 1408:1920].rearrange("p t (h n) -> p t h n", n=32)
            fin = []
            for (q, s_, nh, n, o, g, deps) in ((qk, sq, 22, 64, 0, GQ[:, 0:1408], pr[0:4]),
                                               (qk2, sq2, 16, 32, 44, GQ[:, 1408:1920], pr[4:6])):
                dep = [x for p in deps for x in p]
                ss = st[:, SS + o:SS + o + 2 * nh].rearrange("p (t h) -> p t h", t=2)
                if o:
                    ss = st[:, SS:SS + 2 * nh].rearrange("p (t h) -> p t h", t=2)
                rs = st[:, RS:RS + 2 * nh].rearrange("p (t h) -> p t h", t=2)
                t = V(lambda e, q=q, s_=s_: e.tensor_tensor(s_, q, q, ALU.mult), *dep, *d["_qt_free"])
                t = V(lambda e, s_=s_, ss=ss: e.tensor_reduce(ss, s_, AX.X, ALU.add), t, *d["_rs_free"])
                r = rstd(0, 2 * nh, n, t)
                gb = g.rearrange("p (h n) -> p h n", n=n)
                for t_ in range(2):
                    v1 = V(lambda e, t_=t_, q=q, rs=rs: e.tensor_tensor(
                        q[:, t_], q[:, t_], rs[:, t_].unsqueeze(2).to_broadcast([128, nh, n]), ALU.mult), r)
                    v2 = V(lambda e, t_=t_, q=q, gb=gb: e.tensor_tensor(q[:, t_], q[:, t_], gb, ALU.mult), v1, tgq)
                    fin.append(v2)
                d["_rs_free"] = (v1,)
            d["_gq_free"] = (fin[-1],)
            ta = SB[:, :, :, :].rearrange("p a b c -> p (a b c)")
            tb = PB[:, :, :, :].rearrange("p a b c -> p (a b c)")
            rp = [*d["_sb_free"], tc]
            for t_ in range(2):
                xs = A[:, t_, 512:1024].rearrange("p (h n) -> p h n", n=64)[:, :, 0:16]
                cs = bc(cn("dlc", t_ * 16, t_ * 16 + 16).unsqueeze(1), [128, 8, 16])
                s_ = bc(cn("dls", t_ * 16, t_ * 16 + 16).unsqueeze(1), [128, 8, 16])
                r1 = rope(xs, cs, s_, 8, ta[:, 0:128].rearrange("p (h n) -> p h n", n=16),
                          tb[:, 0:128].rearrange("p (h n) -> p h n", n=16), fin[t_], *rp)
                rp = [r1]
                for y in range(2):
                    xs = A[:, t_, 1024:1408].rearrange("p (h y n) -> p h y n", y=2, n=32)[:, :, y, :]
                    cs = bc(cn("axc", t_ * 64 + y * 32, t_ * 64 + y * 32 + 32).unsqueeze(1), [128, 6, 32])
                    s_ = bc(cn("axs", t_ * 64 + y * 32, t_ * 64 + y * 32 + 32).unsqueeze(1), [128, 6, 32])
                    r1 = rope(xs, cs, s_, 16, ta[:, 0:192].rearrange("p (h n) -> p h n", n=32),
                              tb[:, 0:192].rearrange("p (h n) -> p h n", n=32), *rp)
                    rp = [r1]
                xs = A[:, t_, 1408:1920].rearrange("p (h n) -> p h n", n=32)[:, :, 0:8]
                cs = bc(cn("dfc", t_ * 8, t_ * 8 + 8).unsqueeze(1), [128, 16, 8])
                s_ = bc(cn("dfs", t_ * 8, t_ * 8 + 8).unsqueeze(1), [128, 16, 8])
                r1 = rope(xs, cs, s_, 4, ta[:, 0:128].rearrange("p (h n) -> p h n", n=8),
                          tb[:, 0:128].rearrange("p (h n) -> p h n", n=8), fin[2 + t_], *rp)
                rp = [r1]
            d["_sb_free"] = (r1,)
            tk = transposes([(lambda t, c=c: A[:, t, c * 128:c * 128 + 128], c, 128) for c in range(15)],
                            (r1, fin[3], fin[1]), (4, 5, 6, 7))
            vt = [x for p in pr for x in p]
            VN, VD, VG, VF = 1920, 2176, 2432, 2560
            items = []

            def item(t, heads, bias, op, outc, scale, blocks, diff=False, extra=()):
                items.append(dict(t=t, nk=S, heads=heads, bias=bias, op=op, out=outc, scale=scale, diff=diff,
                                  lam=lam_tok, after=tuple(tk[b] for b in blocks) + tuple(vt) + tuple(extra),
                                  ofree=tuple(tk.values())))

            def vv(c0):
                return [A[:, c, c0:c0 + 64] for c in range(2)]

            for t in range(2):
                q_ = slice(t * 128, t * 128 + 128)
                for p in range(2):
                    hs = [(QT[64 * k:64 * k + 64, p, q_], QT[64 * k:64 * k + 64, 2 + p, :], vv(VN + (2 * p + k) * 64))
                          for k in range(2)]
                    item(t, hs, BT[:, t, 2 * p:2 * p + 2, :], ALU.add, p * 128, 0.125, (p, 2 + p), extra=(tbt,))
                for p in range(2):
                    hs = [(QT[64 * k:64 * k + 64, 4 + p, q_], QT[64 * k:64 * k + 64, 6 + p, :], vv(VD + (2 * p + k) * 64))
                          for k in range(2)]
                    lnb = cn("ln", t * S, t * S + S).unsqueeze(1).to_broadcast([128, 2, S])
                    item(t, hs, lnb, ALU.add, 256 + p * 128, 0.125, (4 + p, 6 + p))
                for p in range(2):
                    hs = [(QT[64 * k:64 * k + 64, 8 + p, q_], QT[64 * k:64 * k + 64, 10, :], vv(VG + k * 64))
                          for k in range(2)]
                    item(t, hs, None, None, 512 + p * 128, 0.125, (8 + p, 10))
                for h in range(4):
                    hs = []
                    for k in range(2):
                        r = (2 * h + k) % 4 * 32
                        blk = (2 * h + k) // 4
                        hs.append((QT[r:r + 32, 11 + blk, q_], QT[r:r + 32, 13 + blk, :], vv(VF + h * 64)))
                    item(t, hs, None, None, 768 + h * 64, 32 ** -0.5, (11 + blk, 13 + blk), diff=True)
            outs = attention(items)
            d["_bt_free"] = (outs[-1],)
            do = A[:, :, 768:1024].rearrange("p t (h n) -> p t h n", n=64)
            sq = A[:, :, 1024:1280].rearrange("p t (h n) -> p t h n", n=64)
            ss = st[:, SS:SS + 8].rearrange("p (t h) -> p t h", t=2)
            rs = st[:, RS:RS + 8].rearrange("p (t h) -> p t h", t=2)
            t = V(lambda e: e.tensor_tensor(sq, do, do, ALU.mult), *outs)
            t = V(lambda e: e.tensor_reduce(ss, sq, AX.X, ALU.add), t, *d["_rs_free"])
            r = rstd(0, 8, 64, t, mul=1.0 - lam_init)
            fin = []
            for t_ in range(2):
                v = V(lambda e, t_=t_: e.tensor_tensor(do[:, t_], do[:, t_],
                                                       rs[:, t_].unsqueeze(2).to_broadcast([128, 4, 64]), ALU.mult), r)
                fin.append((v, *outs))
            d["_rs_free"] = (v,)
            h_tok = to_T(A, [128 * c for c in range(8)], sm(f"os{l}"), None, fin)
            a_free[0] = h_tok[-1]
            residual(out_proj(h_tok), 1.0)

        def load_g(l, which, post):
            tmp = QT[:, 0:4, :].rearrange("p a b -> p (a b)")
            w = (*mod_written[l], *d["_g_free"], *d["_qt_free"])
            t1 = DMA("sp", "g", G[:, :], modd[l:l + 1, which * D:(which + 1) * D].to_broadcast([128, D]), *w)
            t2 = DMA("sp", "g2", tmp, d[post][l:l + 1, :].to_broadcast([128, D]), *w)
            t = V(lambda e: e.tensor_tensor(G[:, :], G[:, :], tmp, ALU.mult), t1, t2)
            d["_qt_free"] = (*d["_qt_free"], t)
            return t

        def load_cols(l):
            for i, k in enumerate((0, 1, 3, 4)):
                t = DMA("sp", f"mc{i}", mcol[:, i, :], modd[l, k * D:(k + 1) * D].rearrange("(c p) -> p c", p=128),
                        *mod_written[l], *d["_mc_free"], slow=True)
                d["_mc"][i] = t
            t = V(lambda e: e.scalar_tensor_tensor(out=mcol[:, 1, :], in0=mcol[:, 1, :], scalar=1.0,
                                                   in1=sm(f"pm{l}"), op0=ALU.add, op1=ALU.mult), d["_mc"][1], tsm)
            t2 = V(lambda e: e.scalar_tensor_tensor(out=mcol[:, 3, :], in0=mcol[:, 3, :], scalar=1.0,
                                                    in1=sm(f"pf{l}"), op0=ALU.add, op1=ALU.mult), d["_mc"][3], tsm)
            d["_colw"] = (tsm, t, t2, d["_mc"][0], d["_mc"][2])

        d["_mc"] = {}
        d["_mc_free"] = ()

        def second_mixer(l):
            tbt = DMA("sp", "bt", BT[:, :, :, :], d["t5b"], *d["_bt_free"])
            load_cols(l)
            h_tok = norm_T(mcol[:, 1, :], mcol[:, 0, :])
            pr = project(h_tok, WIN2_U, WIN2_N)
            pa = [x for p in pr for x in p]
            tk = transposes([(lambda t, c=c: A[:, t, c * 128:c * 128 + 128], c, 128) for c in range(8)],
                            pa[0:8], (4, 5, 6, 7))
            z = st[:, LF:LF + 8].rearrange("p (t h) -> p t h", t=2)
            mn = st[:, LF + 8:LF + 16]
            mx = st[:, LF + 16:LF + 24]
            lf = st[:, LF + 24:LF + 32]
            bfv = sm(f"bf{l}").unsqueeze(1).to_broadcast([128, 2, 4])
            t0 = V(lambda e: e.tensor_tensor(z, A[:, :, 1952:1956], bfv, ALU.add), *pa, tsm, *d["_lf_free"])
            zf = st[:, LF:LF + 8]
            t1 = V(lambda e: e.tensor_scalar(mn, zf, 0.0, None, ALU.min), t0)
            t2 = V(lambda e: e.tensor_scalar(mx, zf, 0.0, None, ALU.max), t0)
            t3 = V(lambda e: e.tensor_tensor(mx, mn, mx, ALU.subtract), t1, t2)
            t4 = AC(lambda e: e.activation(mx, mx, ACT.Exp), t3)
            t4 = AC(lambda e: e.activation(mx, mx, ACT.Ln, bias=1.0), t4)
            tl = V(lambda e: e.tensor_tensor(lf, mn, mx, ALU.subtract), t4, t1)
            U = cn("U").rearrange("p (c q) -> p c q", c=2)
            for h in range(4):
                b = 4 + h // 2
                for c in range(2):
                    tf = PE(lambda e, h=h, c=c, b=b: e.matmul(
                        PS[:, b, (h % 2) * S:(h % 2) * S + S], lf[:, 4 * c + h:4 * c + h + 1].to_broadcast([128, 128]),
                        U[:, c, :], start=c == 0, stop=c == 1), tl, tc, *free[b], inc=h == 3 and c == 1)
            for t_ in range(2):
                for c in range(2):
                    tq = PE(lambda e, t_=t_, c=c: e.matmul(
                        PS[:, 6, 4 * t_:4 * t_ + 4], U[:, c, t_ * 128:t_ * 128 + 128], lf[:, 4 * c:4 * c + 4],
                        start=c == 0, stop=c == 1), *free[6], inc=True)
            fq = V(lambda e: e.tensor_copy(st[:, FQ:FQ + 8], PS[:, 6, 0:8]), tq)
            free[6] = (fq,)
            FB = GQ[:, 0:1536].rearrange("p (h n) -> p h n", h=4)
            pmask = cn("pm")
            for h in range(4):
                for t_ in range(2):
                    nk = 128 * (t_ + 1)
                    o = 0 if t_ == 0 else 128
                    src = PS[:, 4 + h // 2, (h % 2) * S:(h % 2) * S + nk]
                    tfb = V(lambda e, h=h, t_=t_, nk=nk, o=o, src=src: e.scalar_tensor_tensor(
                        out=FB[:, h, o:o + nk], in0=src, scalar=st[:, FQ + 4 * t_ + h:FQ + 4 * t_ + h + 1],
                        in1=pmask[:, 256 - nk:256], op0=ALU.subtract, op1=ALU.add), tf, fq, *d["_gq_free"])
                    if t_:
                        free[4 + h // 2] = (tfb,)
            d["_lf_free"] = (tq, tfb)
            fin = []
            sqs = QT[:, 8:12, :].rearrange("p a b -> p (a b)")
            for t_ in range(2):
                q1 = AC(lambda e, t_=t_: e.activation(sqs[:, 512 * t_:512 * t_ + 256], A[:, t_, 1536:1792], ACT.Square,
                                                      accum_out=st[:, SS + t_:SS + t_ + 1]), *pa, *d["_qt_free"],
                        *d["_rs_free"])
                q2 = AC(lambda e, t_=t_: e.activation(sqs[:, 512 * t_ + 256:512 * t_ + 384], A[:, t_, 1792:1920], ACT.Square,
                                                      accum_out=st[:, SS + 2 + t_:SS + 3 + t_]), *d["_rs_free"])
            r1 = rstd(0, 2, 256, q1, q2)
            r2 = rstd(2, 4, 128, q2)
            for t_ in range(2):
                v1 = V(lambda e, t_=t_: e.tensor_scalar(A[:, t_, 1536:1792], A[:, t_, 1536:1792],
                                                        st[:, RS + t_:RS + t_ + 1], None, ALU.mult), r1, q1)
                v2 = V(lambda e, t_=t_: e.tensor_scalar(A[:, t_, 1792:1920], A[:, t_, 1792:1920],
                                                        st[:, RS + 2 + t_:RS + 3 + t_], None, ALU.mult), r2, q2)
                fin.append((v1, v2))
            d["_rs_free"] = (v1, v2)
            o0 = SM_OFF[f"pq{l}"][0]
            lt = to_T(A, [1536, 1664, 1792], SM[:, o0:o0 + 3], None, fin)
            n = next_unit()
            h, lo = Wh[wslot[n]], Wl[wslot[n]]
            ev = []
            kr_tok = None
            ta = SB[:, :, :, :].rearrange("p a b c -> p (a b c)")
            tb = PB[:, :, :, :].rearrange("p a b c -> p (a b c)")
            rp = [*d["_sb_free"], tc, *pa]
            for t_ in range(2):
                xs = A[:, t_, 1920:1952]
                kr = rope(xs, cn("mlc", t_ * 32, t_ * 32 + 32), cn("mls", t_ * 32, t_ * 32 + 32), 16,
                          ta[:, 0:32], tb[:, 0:32], *rp)
                rp = [kr]
            KLv = A[:, :, 2048:2816].rearrange("p t (h n) -> p t h n", n=96)
            QLv = A[:, :, 0:768].rearrange("p t (h n) -> p t h n", n=96)
            kc_ = None
            for t_ in range(2):
                kc_ = V(lambda e, t_=t_: e.tensor_copy(
                    KLv[:, t_, :, 64:96], A[:, t_, 1920:1952].unsqueeze(1).to_broadcast([128, 8, 32])), kr,
                    *a_free[0])
            tkv = tuple(tk.values())
            for t_ in range(2):
                ts = slice(t_ * 128, t_ * 128 + 128)
                for j, (a, w_) in enumerate(((0, 512), (512, 256))):
                    b = 2 * 0 + j
                    for c in range(2):
                        w = need(n, c)
                        cc = slice(c * 768 + a, c * 768 + a + w_)
                        tp = three(PS[:, b, 0:w_], Hh[:, c, ts], Hl[:, c, ts], h[:, cc], lo[:, cc], c == 0, c == 1,
                                   *w, *lt[c], *(free[b] if c == 0 else ()), inc=c == 1)
                    dst = QLv[:, t_, :, 0:64] if j == 0 else QLv[:, t_, :, 64:96]
                    src = PS[:, b, 0:w_].rearrange("p (h n) -> p h n", h=8)
                    e_ = AC(lambda e, dst=dst, src=src: e.activation(dst, src, ACT.Copy), tp, *tkv)
                    free[b] = (e_,)
                    ev.append(e_)
                if t_ == 1:
                    done[n, 0] = done[n, 1] = tp
                w = need(n, 2)
                for j in range(2):
                    b = 2 + j
                    cc = slice(1536 + j * 512, 2048 + j * 512)
                    tp = three(PS[:, b, 0:512], Hh[:, 2, ts], Hl[:, 2, ts], h[:, cc], lo[:, cc], True, True,
                               *w, *lt[2], *free[b], inc=True)
                    src = PS[:, b, 0:512].rearrange("p (h n) -> p h n", h=8)
                    dst = KLv[:, t_, :, 0:64] if j == 0 else A[:, t_, 1536:2048].rearrange("p (h n) -> p h n", h=8)
                    e_ = V(lambda e, dst=dst, src=src: e.tensor_copy(dst, src), tp, kc_, *lt[2], *a_free[0])
                    free[b] = (e_,)
                    ev.append(e_)
                if t_ == 1:
                    done[n, 2] = tp
            d["_h_free"] = (tp,)
            rp = [kr, *ev]
            for t_ in range(2):
                xs = QLv[:, t_, :, 64:96]
                cs = bc(cn("mlc", t_ * 32, t_ * 32 + 32).unsqueeze(1), [128, 8, 32])
                s_ = bc(cn("mls", t_ * 32, t_ * 32 + 32).unsqueeze(1), [128, 8, 32])
                r1_ = rope(xs, cs, s_, 16, ta[:, 0:256].rearrange("p (h n) -> p h n", n=32),
                           tb[:, 0:256].rearrange("p (h n) -> p h n", n=32), *rp)
                rp = [r1_]
            d["_sb_free"] = (r1_,)
            jobs = [(lambda t, hh=hh: A[:, t, hh * 96:hh * 96 + 96], 8 + hh, 96) for hh in range(8)]
            jobs += [(lambda t, hh=hh: A[:, t, 2048 + hh * 96:2048 + hh * 96 + 96], 16 + hh, 96) for hh in range(8)]
            d["_qt_free"] = (*d["_qt_free"], q2)
            tk2 = transposes(jobs, (r1_, kc_, *ev), (4, 5, 6, 7))
            of = tuple(tk2.values())
            items = []

            def vv(c0, nk):
                return [A[:, c, c0:c0 + 64] for c in range(nk // 128)]

            for t in range(2):
                nk = 128 * (t + 1)
                q_ = slice(t * 128, t * 128 + 128)
                o = 0 if t == 0 else 128
                aft = (*tk.values(), *tk2.values(), *ev, *pa, tbt, tfb, tc)
                for p in range(2):
                    hs = [(QT[64 * k:64 * k + 64, p, q_], QT[64 * k:64 * k + 64, 2 + p, 0:nk],
                           vv(1024 + (2 * p + k) * 64, nk)) for k in range(2)]
                    items.append(dict(t=t, nk=nk, heads=hs, bias=FB[:, 2 * p:2 * p + 2, o:o + nk], op=ALU.subtract,
                                      out=p * 128, scale=0.125, diff=False, after=aft, ofree=of))
                for p in range(2):
                    hs = [(QT[64 * k:64 * k + 64, 4 + p, q_], QT[64 * k:64 * k + 64, 6 + p, 0:nk],
                           vv(1280 + (2 * p + k) * 64, nk)) for k in range(2)]
                    items.append(dict(t=t, nk=nk, heads=hs, bias=BT[:, t, 2 * p:2 * p + 2, 0:nk], op=ALU.add,
                                      out=256 + p * 128, scale=0.125, diff=False, after=aft, ofree=of))
                for p in range(4):
                    hs = [(QT[0:96, 8 + 2 * p + k, q_], QT[0:96, 16 + 2 * p + k, 0:nk],
                           vv(1536 + (2 * p + k) * 64, nk)) for k in range(2)]
                    items.append(dict(t=t, nk=nk, heads=hs,
                                      bias=pmask[:, 256 - nk:256].unsqueeze(1).to_broadcast([128, 2, nk]),
                                      op=ALU.subtract, out=512 + p * 128, scale=96 ** -0.5, diff=False,
                                      after=aft, ofree=of))
            outs = attention(items)
            d["_bt_free"] = d["_gq_free"] = (outs[-1],)
            tg = load_g(l, 2, "g_mix_post")
            fin = []
            for g, (a, b) in enumerate(((0, 256), (256, 512), (512, 1024))):
                for t_ in range(2):
                    i = 2 * g + t_
                    q1 = AC(lambda e, t_=t_, a=a, b=b, i=i: e.activation(
                        A[:, t_, 1024 + a:1024 + b], A[:, t_, a:b], ACT.Square, accum_out=st[:, SS + i:SS + i + 1]),
                        *outs, *d["_rs_free"])
                r = rstd(2 * g, 2 * g + 2, b - a, q1)
                for t_ in range(2):
                    i = 2 * g + t_
                    v1 = V(lambda e, t_=t_, a=a, b=b, i=i: e.tensor_scalar(
                        A[:, t_, a:b], A[:, t_, a:b], st[:, RS + i:RS + i + 1], None, ALU.mult), r, q1)
                    fin.append(v1)
            d["_rs_free"] = (v1,)
            h_tok = to_T(A, [128 * c for c in range(8)], sm(f"pg{l}"), None, (tuple(fin), tuple(fin)))
            a_free[0] = h_tok[-1]
            post_norm(out_proj(h_tok), tg)

        d["_lf_free"] = ()

        for l in range(L):
            residual(ffn(norm_T(sm(f"f1{l}"))), 0.5)
            first_mixer(l)
            residual(ffn(norm_T(sm(f"f2{l}"))), 0.5)
        for l in range(L):
            second_mixer(l)
            h = norm_T(mcol[:, 3, :], mcol[:, 2, :])
            tg = load_g(l, 5, "g_ffn_post")
            last = ffn(h)
            d["_mc_free"] = h[-1]
            post_norm(last, tg)
        assert state["unit"] == len(units) and state["load"] == len(units)
        DMA("sp", "out", out.rearrange("(t p) n -> p t n", t=2), X[:, :, :], *x_tok[0], *x_tok[1])
        for key in ("out", "mod"):
            queue["sp"].append((("wait_ge", (key, count[key]), {}), None, 0))

        block = ctx.enter_context(nc.Block())

        def run(e, name):
            for (op, a, k), sem, by in queue[name]:
                if op == "wait_ge":
                    e.wait_ge(sems[a[0]], a[1])
                    continue
                ins = CALLS[op](e, a, k)
                if sem is not None:
                    ins.then_inc(sems[sem], by)

        block.sync(lambda e: run(e, "sp"))
        block.scalar(lambda e: run(e, "act"))
        block.vector(lambda e: run(e, "dve"))
        block.gpsimd(lambda e: run(e, "pool"))
        block.tensor(lambda e: run(e, "pe"))


def constants():
    f = np.float32
    c = np.zeros((128, C_N), f)

    def put(name, v):
        o, n = C_OFF[name]
        c[:, o:o + n] = np.asarray(v, f).reshape(128, n)

    i = np.arange(128)
    put("id", np.eye(128))
    pm = np.zeros((128, 256), f)
    pm[:, 128:] = np.where(i[None, :] <= i[:, None], 0.0, BIG)
    put("pm", pm)
    q = np.arange(S)
    dd = q[None, :] - q[:, None]
    m = (np.abs(dd) <= 64).astype(np.float64) + (dd % 4 == 0) + (dd % 16 == 0)
    ln = np.where(m > 0, np.log(np.maximum(m, 1)), -BIG).astype(f)
    put("ln", ln.reshape(2, 128, S).transpose(1, 0, 2))
    u = (q[:, None] <= q[None, :]).astype(f)
    put("U", u.reshape(2, 128, S).transpose(1, 0, 2))
    put("one", np.ones((128, 1)))

    def table(pos, dim, theta):
        inv = (f(1.0) / (f(theta) ** (np.arange(0, dim, 2, dtype=f) / f(dim)))).astype(f)
        ang = pos.astype(f)[:, None] * inv[None, :]
        co, si = np.cos(ang).astype(f), np.sin(ang).astype(f)
        return np.concatenate([co, co], 1), np.concatenate([-si, si], 1)

    def halves(a):
        return a.reshape(2, 128, -1).transpose(1, 0, 2)

    for n, args in (("df", (q, 8, 500000.0)), ("dl", (q, 16, 500000.0)), ("ml", (q, 32, 10000.0))):
        a, b = table(*args)
        put(n + "c", halves(a))
        put(n + "s", halves(b))
    r, k = table(q // 64, 32, 10000.0), table(q % 64, 32, 10000.0)
    put("axc", halves(np.concatenate([r[0], k[0]], 1)))
    put("axs", halves(np.concatenate([r[1], k[1]], 1)))
    return c


def t5_buckets(n):
    f = np.float32
    nf = np.maximum(n, 16).astype(f)
    large = 16 + (np.log(nf / f(16)).astype(f) / f(math.log(128 / 16)) * f(16)).astype(np.int32)
    return np.where(n < 16, n, np.minimum(large, 31))


def kernel(**inputs):
    import numpy as np
    import concourse.bacc as _bacc
    from concourse import mybir as _mybir
    from concourse.bass_utils import run_bass_kernel_spmd as _run

    I = {k: np.asarray(v) for k, v in inputs.items()}
    f = np.float32
    C = np.ascontiguousarray

    def chunks(w, a, b):
        k = w.shape[0] // 128
        return w[:, a:b].reshape(k, 128, b - a).transpose(1, 0, 2).reshape(128, -1)

    def ffn(gate, up, down):
        g = gate.reshape(8, 128, NF, 128).transpose(2, 1, 0, 3).reshape(NF, 128, 1024)
        u = up.reshape(8, 128, NF, 128).transpose(2, 1, 0, 3).reshape(NF, 128, 1024)
        return np.concatenate([g, u, down.reshape(NF, 128, 1024)], axis=2)

    ffns = []
    for l in range(L):
        ffns.append(ffn(I["ffn1_w_gate"][l], I["ffn1_w_up"][l], I["ffn1_w_down"][l]))
        ffns.append(ffn(I["ffn2_w_gate"][l], I["ffn2_w_up"][l], I["ffn2_w_down"][l]))
    for l in range(L):
        gu = I["w_gate_up_2"][l]
        ffns.append(ffn(gu[:, :F], gu[:, F:], I["w_down_2"][l]))
    A = {"ffn": np.concatenate(ffns)}

    names = ["nq", "nk", "nv", "fq", "fk", "fv", "gq", "gk", "gv", "dq", "dk", "dv"]
    sizes = [256, 256, 256, 256, 256, 256, 256, 128, 128, 256, 256, 256]
    at = dict(zip(names, np.cumsum([0] + sizes[:-1])))
    sz = dict(zip(names, sizes))
    rng = {n: np.arange(at[n], at[n] + sz[n]) for n in names}
    gq_perm = np.concatenate([np.arange(h * 64, h * 64 + 64) for h in (0, 2, 1, 3)])
    cols = np.concatenate([rng["nq"], rng["nk"], rng["dq"], rng["dk"], rng["gq"][gq_perm], rng["gk"],
                           rng["fq"], rng["fk"], rng["nv"], rng["dv"], rng["gv"], rng["fv"]])
    A["win"] = np.concatenate([np.stack([chunks(I["w_in"][l][:, cols], u * WIN_N, (u + 1) * WIN_N)
                                         for u in range(WIN_U)]) for l in range(L)])
    rows = np.concatenate([np.arange(0, 256), np.arange(768, 1024), 512 + gq_perm, np.arange(256, 512)])
    A["wo"] = np.stack([chunks(I["w_out"][l][rows], 0, D) for l in range(L)]
                       + [chunks(I["w_out_2"][l], 0, D) for l in range(L)])
    n2 = ["fq", "fk", "fv", "fl", "mq", "mk", "mv", "cq", "ck", "kr"]
    s2 = [256, 256, 256, 4, 256, 256, 256, 256, 128, 32]
    a2 = dict(zip(n2, np.cumsum([0] + s2[:-1])))
    z2 = dict(zip(n2, s2))
    cols2 = np.concatenate([np.arange(a2[n], a2[n] + z2[n])
                            for n in ("fq", "fk", "mq", "mk", "fv", "mv", "cq", "ck", "kr", "fl")])
    A["win2"] = np.concatenate([np.stack([chunks(I["w_in_2"][l][:, cols2], u * WIN2_N, (u + 1) * WIN2_N)
                                          for u in range(WIN2_U)]) for l in range(L)])
    uq = np.concatenate([np.arange(h * 96, h * 96 + 64) for h in range(8)]
                        + [np.arange(h * 96 + 64, h * 96 + 96) for h in range(8)])
    ukv = np.concatenate([np.arange(h * 128, h * 128 + 64) for h in range(8)]
                         + [np.arange(h * 128 + 64, h * 128 + 128) for h in range(8)])
    A["lat"] = np.stack([np.concatenate([chunks(I["w_uq_2"][l][:, uq], 0, 768),
                                         chunks(I["w_ukv_2"][l][:, ukv], 0, 1024)], 1) for l in range(L)])
    A["ada"] = np.concatenate([np.stack([chunks(I["w_ada_2"][l], g * ADA_N, (g + 1) * ADA_N)
                                         for g in range(ADA_U)]) for l in range(L)])
    A["b_ada"] = I["b_ada_2"]
    A["g_mix_post"] = I["g_mix_post_2"]
    A["g_ffn_post"] = I["g_ffn_post_2"]
    A["x"] = I["x"][0]
    A["c"] = I["c_2"][0].reshape(8, 128).T
    A["const"] = constants()

    small = np.zeros((128, SM_N), f)

    def col(v):
        return v.reshape(-1, 128).T

    def row(v):
        return np.broadcast_to(v.reshape(1, -1), (128, v.size))

    for l in range(L):
        osc = np.concatenate([np.ones(768, f), np.tile(I["diff_out_norm"][l], 4)])
        vals = {"f1": col(I["ffn1_norm"][l]), "mx": col(I["mix_norm"][l]), "f2": col(I["ffn2_norm"][l]),
                "os": col(osc),
                "la": row(np.concatenate([I["diff_lambda_q1"][l], I["diff_lambda_k1"][l],
                                          I["diff_lambda_q2"][l], I["diff_lambda_k2"][l]])),
                "pm": col(I["g_mix_pre_2"][l]), "pf": col(I["g_ffn_pre_2"][l]), "pg": col(I["g_group_2"][l]),
                "pq": col(I["g_q_lat_2"][l]), "pk": col(I["g_kv_lat_2"][l]), "bf": row(I["b_forget_2"][l])}
        for k, v in vals.items():
            o, n = SM_OFF[f"{k}{l}"]
            small[:, o:o + n] = v
    A["small"] = small
    A["gq"] = np.stack([row(np.concatenate([
        np.tile(I["na_q_norm"][l], 4), np.tile(I["na_k_norm"][l], 4), np.tile(I["dil_q_norm"][l], 4),
        np.tile(I["dil_k_norm"][l], 4), np.tile(I["gqa_q_norm"][l], 4), np.tile(I["gqa_k_norm"][l], 2),
        np.tile(I["diff_q_norm"][l], 8), np.tile(I["diff_k_norm"][l], 8)])) for l in range(L)])

    q = np.arange(S)
    r, c = q // 64, q % 64
    start = np.clip(c - 8, 0, 48)
    inside = (c[None, :] >= start[:, None]) & (c[None, :] < start[:, None] + 16)
    ro = r[None, :] - r[:, None] + 7
    co = np.clip(c[None, :] - c[:, None] + 15, 0, 30)
    nab = np.where(inside[None, None], I["na_rel_bias"][:, :, ro, co], f(-BIG))
    A["nab"] = nab.reshape(L, 4, 2, 128, S).transpose(0, 3, 2, 1, 4)
    dist = q[:, None] - q[None, :]
    t5 = I["t5_table_2"].T[:, t5_buckets(np.maximum(dist, 0))]
    t5 = np.where(dist[None] >= 0, t5, f(-BIG))
    A["t5b"] = t5.reshape(4, 2, 128, S).transpose(2, 1, 0, 3)

    nc = _bacc.Bacc("TRN2", target_bir_lowering=False, num_devices=1)
    arrays, d = {}, {}
    for name, a in A.items():
        a = C(a)
        arrays[f"in_{name}"] = a
        d[name] = nc.dram_tensor(f"in_{name}", a.shape, _mybir.dt.from_np(a.dtype), kind="ExternalInput").ap()
    out = nc.dram_tensor("out_x", (S, D), _mybir.dt.float32, kind="ExternalOutput").ap()
    program(nc, d, out)
    res = _run(nc, [arrays], core_ids=[0])
    return res.results[0]["out_x"].reshape(1, S, D)
```

```python
import math
import numpy as np
import concourse.bass as bass
from concourse import mybir
from contextlib import ExitStack

L, D, S, F = 2, 1024, 256, 2816
NF = F // 128
EPS = 1e-6
BIG = 1e30
WIN_U, WIN_N = 8, 352
WIN2_U, WIN2_N = 6, 326
ADA_G, ADA_N = 12, 512
UNIT = 3072
PIECE = 1056
RAW = 7

SMALL = []
for _l in range(L):
    SMALL += [(f"f1{_l}", 8), (f"mx{_l}", 8), (f"f2{_l}", 8), (f"os{_l}", 8), (f"la{_l}", 128),
              (f"pm{_l}", 8), (f"pf{_l}", 8), (f"pg{_l}", 8), (f"pq{_l}", 2), (f"pk{_l}", 1), (f"bf{_l}", 4)]
CONST = [("id", 128), ("pm", 256), ("ln", 512), ("bo", 4),
         ("dfc", 16), ("dfs", 16), ("dlc", 32), ("dls", 32), ("axc", 128), ("axs", 128), ("mlc", 64), ("mls", 64)]


def offsets(table):
    at, out = 0, {}
    for name, n in table:
        out[name] = (at, n)
        at += n
    return out, at


SM_OFF, SM_N = offsets(SMALL)
C_OFF, C_N = offsets(CONST)


class Recorder:

    def activation(self, *a, **k):
        return "activation", a, k

    def tensor_tensor(self, *a, **k):
        return "tensor_tensor", a, k

    def tensor_scalar(self, *a, **k):
        return "tensor_scalar", a, k

    def scalar_tensor_tensor(self, *a, **k):
        return "scalar_tensor_tensor", a, k

    def tensor_reduce(self, *a, **k):
        return "tensor_reduce", a, k

    def tensor_copy(self, *a, **k):
        return "tensor_copy", a, k

    def reciprocal(self, *a, **k):
        return "reciprocal", a, k

    def matmul(self, *a, **k):
        return "matmul", a, k

    def transpose(self, *a, **k):
        return "transpose", a, k

    def dma_start(self, *a, **k):
        return "dma_start", a, k

    def memset(self, *a, **k):
        return "memset", a, k


CALLS = {
    "activation": lambda e, a, k: e.activation(*a, **k),
    "tensor_tensor": lambda e, a, k: e.tensor_tensor(*a, **k),
    "tensor_scalar": lambda e, a, k: e.tensor_scalar(*a, **k),
    "scalar_tensor_tensor": lambda e, a, k: e.scalar_tensor_tensor(*a, **k),
    "tensor_reduce": lambda e, a, k: e.tensor_reduce(*a, **k),
    "tensor_copy": lambda e, a, k: e.tensor_copy(*a, **k),
    "reciprocal": lambda e, a, k: e.reciprocal(*a, **k),
    "matmul": lambda e, a, k: e.matmul(*a, **k),
    "transpose": lambda e, a, k: e.transpose(*a, **k),
    "dma_start": lambda e, a, k: e.dma_start(*a, **k),
    "memset": lambda e, a, k: e.memset(*a, **k),
}
recorder = Recorder()


def program(nc, d, out):
    f32, f32r, i32 = mybir.dt.float32, mybir.dt.float32r, mybir.dt.int32
    ACT, ALU, AX = mybir.ActivationFunctionType, mybir.AluOpType, mybir.AxisListType

    with ExitStack() as ctx:
        def sb(name, shape, dt=f32):
            return ctx.enter_context(nc.sbuf_tensor(name, shape, dt))

        def semaphore(name):
            return ctx.enter_context(nc.semaphore(name))

        X = sb("X", [128, 2, D])
        raw = [sb(f"raw{i}", [128, PIECE]) for i in range(RAW)]
        Wh = [sb(f"Wh{i}", [128, UNIT], f32r) for i in range(2)]
        Wl = [sb(f"Wl{i}", [128, UNIT], f32r) for i in range(2)]
        Hh = sb("Hh", [128, 8, S], f32r)
        Hl = sb("Hl", [128, 8, S], f32r)
        A = sb("A", [128, 2, 1920])
        QTh = sb("QTh", [128, 16, S], f32r)
        QTl = sb("QTl", [128, 16, S], f32r)
        Vh = sb("Vh", [128, 2, D], f32r)
        Vl = sb("Vl", [128, 2, D], f32r)
        BT = sb("BT", [128, 2, 4, S])
        GQ = sb("GQ", [128, 1920])
        G = GQ[:, 0:D]
        WK = sb("WK", [128, 1536])
        SB = WK[:, 0:1536].rearrange("p (a b c) -> p a b c", a=3, b=2)
        HT = WK[:, 0:1024].rearrange("p (a b) -> p a b", a=4)
        PTh = sb("PTh", [128, 2, 4, 128], f32r)
        PTl = sb("PTl", [128, 2, 4, 128], f32r)
        ah = [PTh[:, i, 0:2, :].rearrange("p a b -> p (a b)") for i in range(2)]
        al = [PTl[:, i, 0:2, :].rearrange("p a b -> p (a b)") for i in range(2)]
        R = sb("R", [128, S])
        SM = sb("SM", [128, SM_N])
        CT = sb("CT", [128, C_N])
        Ur = sb("Ur", [128, 2, S], f32r)
        oner = sb("oner", [128, 2], f32r)
        lfr = sb("lfr", [128, 2, 8], f32r)
        mhalf = sb("mhalf", [128, 8])
        st = sb("st", [128, 640])
        ada_raw = BT[:, :, :, :].rearrange("p a b c -> p (a b c)").rearrange("p (s n) -> p s n", s=2)
        acc = GQ[:, 0:ADA_N]
        adab = GQ[0:1, ADA_N:2 * ADA_N]
        acch = Vh[:, 0, 0:ADA_N]
        accl = Vl[:, 0, 0:ADA_N]
        mcol = sb("mcol", [128, 4, 8])
        PS = ctx.enter_context(nc.psum_tensor("PS", [128, 8, 512], f32))
        modd = nc.dram_tensor("mod_scratch", (L, 6 * D), f32, kind="Internal").ap()

        def sm(name, a=0, b=None):
            o, n = SM_OFF[name]
            return SM[:, o + a:o + (n if b is None else b)]

        def cn(name, a=0, b=None):
            o, n = C_OFF[name]
            return CT[:, o + a:o + (n if b is None else b)]

        ident = cn("id")

        names = ["pe", "act", "dve", "pool"]
        sems = {n: semaphore("s_" + n) for n in names}
        count = {n: 0 for n in names}
        queue = {n: [] for n in names + ["sp"]}
        waited = {n: {} for n in queue}

        def emit(eng, fn, after, sem, by):
            for key, v in after:
                if waited[eng].get(key, 0) < v:
                    waited[eng][key] = v
                    queue[eng].append((("wait_ge", (key, v), {}), None, 0))
            if sem is None:
                queue[eng].append((fn(recorder), None, 0))
                return None
            count[sem] = count.get(sem, 0) + by
            queue[eng].append((fn(recorder), sem, by))
            return (sem, count[sem])

        def V(fn, *after):
            return emit("dve", fn, after, "dve", 1)

        def AC(fn, *after):
            return emit("act", fn, after, "act", 1)

        def GP(fn, *after):
            return emit("pool", fn, after, "pool", 1)

        def PE(fn, *after, inc=False):
            return emit("pe", fn, after, "pe" if inc else None, 1)

        def DMA(eng, sem, dst, src, *after, slow=False):
            if sem not in sems:
                sems[sem] = semaphore("d_" + sem)
            kw = dict(allow_slow_non_contiguous=True) if slow else {}
            return emit(eng, lambda e: e.dma_start(dst, src, **kw), after, sem, 16)

        free = [() for _ in range(8)]

        units = []

        def ffn_units(k):
            for f in range(NF):
                units.append((d["ffn"][k * NF + f], [(0, 1024), (1024, 2048), (2048, 3072)]))

        def cparts(nch, n):
            cut = [0, 3, 6, 8] if nch == 8 else list(range(nch + 1))
            return [(a * n, b * n) for a, b in zip(cut, cut[1:])]

        for l in range(L):
            ffn_units(2 * l)
            for u in range(WIN_U):
                units.append((d["win"][l * WIN_U + u], cparts(8, WIN_N)))
            for a, b in ((0, 3), (3, 6), (6, 8)):
                units.append((d["wo"][l][:, a * D:b * D], cparts(b - a, D)))
            ffn_units(2 * l + 1)
        for l in range(L):
            for u in range(WIN2_U):
                units.append((d["win2"][l * WIN2_U + u], cparts(8, WIN2_N)))
            units.append((d["lat"][l], [(0, 768), (768, 1536), (1536, 2560)]))
            for a, b in ((0, 3), (3, 6), (6, 8)):
                units.append((d["wo"][L + l][:, a * D:b * D], cparts(b - a, D)))
            ffn_units(4 + l)

        loaded = {}
        ready = {}
        done = {}
        state = {"load": 0, "piece": 0, "cur": 0}

        pieces = [(n, k) for n, u in enumerate(units) for k in range(len(u[1]))]

        def load_next():
            i = state["load"]
            if i >= len(pieces) or (i >= RAW and pieces[i - RAW] not in ready):
                return False
            n, k = pieces[i]
            a, b = units[n][1][k]
            loaded[n, k] = DMA("sp", f"raw{i % RAW}", raw[i % RAW][:, 0:b - a], units[n][0][:, a:b],
                               *(ready[pieces[i - RAW]] if i >= RAW else ()))
            state["load"] += 1
            return True

        def released(n, k):
            if n < 2:
                return ()
            a, b = units[n][1][k]
            got = []
            for j, (pa, pb) in enumerate(units[n - 2][1]):
                if pa < b and a < pb:
                    if (n - 2, j) not in done:
                        return None
                    got.append(done[n - 2, j])
            return got

        def tick():
            i = state["piece"]
            if i >= len(pieces):
                return False
            while load_next():
                pass
            n, k = pieces[i]
            rel = released(n, k)
            if rel is None:
                return False
            a, b = units[n][1][k]
            r = raw[i % RAW][:, 0:b - a]
            h, lo = Wh[n % 2], Wl[n % 2]
            t1 = AC(lambda e: e.activation(h[:, a:b], r, ACT.Copy), loaded[n, k], *rel)
            t2 = V(lambda e: e.tensor_tensor(lo[:, a:b], r, h[:, a:b].bitcast(f32), ALU.subtract),
                   loaded[n, k], t1, *rel)
            ready[n, k] = (t1, t2)
            state["piece"] += 1
            while load_next():
                pass
            return True

        ada = {"load": 0, "op": 0, "tok": None, "free": [(), ()], "acc_free": (), "row_free": (), "wait": [], "v_free": (),
               "loaded": {}}
        NADA = L * ADA_G * 4
        mod_written = {0: [], 1: []}

        def ada_load(limit):
            while ada["load"] < min(limit, ada["op"] // 2 + 2):
                u = ada["load"]
                ada["loaded"][u] = DMA("act", f"ada{u % 2}", ada_raw[:, u % 2, :], d["ada"][u], *ada["free"][u % 2])
                ada["load"] += 1

        def ada_tick(limit):
            ada_load(limit)
            u, k = ada["op"] // 2, ada["op"] % 2
            if u >= limit:
                return
            g = u // 4
            c = u % 4 * 2 + k
            if c == 0 and ada["wait"]:
                return
            w = ada_raw[:, u % 2, k * ADA_N:(k + 1) * ADA_N]
            if c == 0:
                t = V(lambda e: e.tensor_scalar(acc, w, cact[:, 0:1], None, ALU.mult),
                      ada["loaded"][u], cact_tok, *ada["acc_free"])
            else:
                t = V(lambda e: e.scalar_tensor_tensor(out=acc, in0=w, scalar=cact[:, c:c + 1], in1=acc,
                                                       op0=ALU.mult, op1=ALU.add), ada["loaded"][u], ada["tok"])
            ada["tok"] = t
            ada["op"] += 1
            if k == 1:
                ada["free"][u % 2] = (t,)
            if c == 7:
                t1 = AC(lambda e: e.activation(acch, acc, ACT.Copy), t, *ada["acc_free"], *ada["v_free"])
                t2 = V(lambda e: e.tensor_tensor(accl, acc, acch.bitcast(f32), ALU.subtract), t1)
                ada["wait"].append((g, (t1, t2)))

        def need(n, k):
            while (n, k) not in ready:
                assert tick(), (n, k, state)
            return ready[n, k]

        def next_unit():
            state["cur"] += 1
            return state["cur"] - 1

        def ada_finish(bank):
            if not ada["wait"]:
                return
            g, t = ada["wait"].pop()
            l, g = g // ADA_G, g % ADA_G
            cols = slice(g * ADA_N, (g + 1) * ADA_N)
            tb = DMA("act", "adab", adab, d["b_ada"][l:l + 1, cols], *ada["row_free"])
            PE(lambda e: e.matmul(PS[:, bank, 0:ADA_N], oner[:, 0:1].to_broadcast([128, 128]), acch, start=True,
                                  stop=False), *t, t_one, *free[bank])
            tp = PE(lambda e: e.matmul(PS[:, bank, 0:ADA_N], oner[:, 0:1].to_broadcast([128, 128]), accl, start=False,
                                       stop=True), inc=True)
            tv = V(lambda e: e.tensor_tensor(adab, PS[0:1, bank, 0:ADA_N], adab, ALU.add), tp, tb)
            to = DMA("sp", "mod", modd[l:l + 1, cols], adab, tv)
            free[bank] = (tv,)
            ada["acc_free"], ada["row_free"] = (tp,), (to,)
            mod_written[l].append(to)

        tx = [DMA("act", f"x{t}", X[:, t, :], d["x"][t * 128:t * 128 + 128, :]) for t in range(2)]
        tid = DMA("sp", "id", CT[:, 0:128], d["const"][:, 0:128])
        tsm = DMA("sp", "sm", SM[:, :], d["small"])
        for _ in range(RAW):
            load_next()
        tc = DMA("act", "ct", CT[:, 128:C_N], d["const"][:, 128:C_N])
        tcc = DMA("act", "cc", st[:, 0:8], d["c"])
        tu = DMA("act", "u", A[:, 0, 1408:1920], d["tri"])
        t_u = AC(lambda e: e.activation(Ur[:, :, :], A[:, 0, 1408:1920].rearrange("p (c q) -> p c q", c=2), ACT.Copy), tu)
        t = V(lambda e: e.memset(st[:, 8:10], 1.0))
        t_one = AC(lambda e: e.activation(oner[:, :], st[:, 8:10], ACT.Copy), t)
        tmh = GP(lambda e: e.memset(mhalf[:, :], -0.5))
        cact = sb("cact", [128, 8])
        t = AC(lambda e: e.activation(cact[:, :], st[:, 0:8], ACT.Silu), tcc)
        cact_tok = t

        SS, RS, NM, Z, ZR, LA, LF, FQ, NT = 16, 80, 144, 160, 240, 320, 330, 400, 512

        def rstd(a, b, n, *after, mul=None):
            s, r = st[:, SS + a:SS + b], st[:, RS + a:RS + b]
            t = GP(lambda e: e.tensor_scalar(s, s, 1.0 / n, EPS, ALU.mult, ALU.add), *after)
            t = GP(lambda e: e.tensor_tensor(r, s, mhalf[:, 0:b - a], ALU.pow), t, tmh)
            if mul is not None:
                t = GP(lambda e: e.tensor_scalar(r, r, mul, None, ALU.mult), t)
            return t

        def rstd_v(a, b, n, *after, mul=None):
            s, r, w = st[:, SS + a:SS + b], st[:, RS + a:RS + b], st[:, NT:NT + b - a]
            t = V(lambda e: e.tensor_scalar(s, s, 1.0 / n, EPS, ALU.mult, ALU.add), *after)
            t = V(lambda e: e.tensor_scalar(w.bitcast(i32), s.bitcast(i32), 1, None, ALU.logical_shift_right), t)
            t = V(lambda e: e.tensor_scalar(r.bitcast(i32), w.bitcast(i32), -1.0, 1597463007.0, ALU.mult, ALU.add), t)
            for _ in range(3):
                t = V(lambda e: e.tensor_tensor(w, r, r, ALU.mult), t)
                t = V(lambda e: e.scalar_tensor_tensor(out=w, in0=w, scalar=-0.5, in1=s, op0=ALU.mult, op1=ALU.mult), t)
                t = V(lambda e: e.scalar_tensor_tensor(out=r, in0=w, scalar=1.5, in1=r, op0=ALU.add, op1=ALU.mult), t)
            if mul is not None:
                t = V(lambda e: e.tensor_scalar(r, r, mul, None, ALU.mult), t)
            return t

        def to_T(src, cols, scale, after, shift=None, row=None, dst0=0, before=None):
            got, tps = [], {}
            n = len(cols)

            def turn(j):
                b = 4 + (j // 2) % 4
                for i in range(j, min(j + 2, n)):
                    for t in range(2):
                        tps[j] = PE(lambda e: e.transpose(
                            PS[:, b, (i % 2) * S + t * 128:(i % 2) * S + t * 128 + 128],
                            src[:, t, cols[i]:cols[i] + 128], ident), tid, *after(i, t), *free[b], inc=True)

            if before is not None:
                for j in range(0, n, 2):
                    turn(j)
                row_tok = (before(),)
            else:
                row_tok = ()
            late = []

            def flush():
                while late:
                    t2, fn, key = late.pop(0)
                    t3 = V(fn, t2)
                    d["_ht_free"][key] = (t3,)
                    got.append((t2, t3))

            for j in range(0, n, 2):
                if j not in tps:
                    turn(j)
                b = 4 + (j // 2) % 4
                for i in range(j, min(j + 2, n)):
                    p = PS[:, b, (i % 2) * S:(i % 2) * S + S]
                    ht, hh, hl = HT[:, i % 4, :], Hh[:, dst0 + i, :], Hl[:, dst0 + i, :]
                    sc = scale[:, i:i + 1]
                    w = [tps[j], *d["_ht_free"][i % 4], *d["_h_free"], *d["_colw"], *row_tok]
                    if row is None:
                        t1 = V(lambda e: e.tensor_scalar(ht, p, sc, None, ALU.mult), *w)
                    else:
                        t1 = V(lambda e: e.scalar_tensor_tensor(out=ht, in0=p, scalar=sc, in1=row, op0=ALU.mult,
                                                                op1=ALU.mult), *w)
                    flush()
                    if shift is None:
                        t2 = AC(lambda e: e.activation(hh, ht, ACT.Copy), t1, *d["_h_free"])
                        late.append((t2, lambda e, hl=hl, ht=ht, hh=hh: e.tensor_tensor(
                            hl, ht, hh.bitcast(f32), ALU.subtract), i % 4))
                    else:
                        sh = shift[:, i:i + 1]
                        t2 = AC(lambda e: e.activation(hh, ht, ACT.Identity, bias=sh), t1, *d["_h_free"], *d["_colw"])
                        late.append((t2, lambda e, hl=hl, ht=ht, hh=hh, sh=sh: e.scalar_tensor_tensor(
                            out=hl, in0=ht, scalar=sh, in1=hh.bitcast(f32), op0=ALU.add, op1=ALU.subtract), i % 4))
                free[b] = (t1,)
            flush()
            return got

        d["_ht_free"] = [(), (), (), ()]
        d["_h_free"] = ()
        d["_colw"] = (tsm,)
        x_tok = [(tx[0],), (tx[1],)]
        a_free = [(t_u,)]

        def norm_T(scale, shift=None):
            rs = []
            for t in range(2):
                q = AC(lambda e: e.activation(A[:, t, 0:D], X[:, t, :], ACT.Square,
                                              accum_out=st[:, SS + t:SS + t + 1]),
                       *x_tok[t], *a_free[0], *d.get("_rs_free", ()))
                rs.append(rstd(t, t + 1, D, q))
                a_free[0] = (*a_free[0], q)

            def spread():
                for t in range(2):
                    tp = PE(lambda e: e.matmul(PS[:, 0, t * 128:t * 128 + 128],
                                               st[:, RS + t:RS + t + 1].to_broadcast([128, 128]), ident,
                                               start=True, stop=True), rs[t], tid, *free[0], inc=True)
                tr = AC(lambda e: e.activation(R[:, :], PS[:, 0, 0:S], ACT.Copy), tp)
                free[0] = (tr,)
                d["_rs_free"] = (tp,)
                return tr

            return to_T(X, [128 * c for c in range(8)], scale, lambda i, t: x_tok[t], shift, R[:, :], before=spread)

        def three(out_, xh, xl, wh, wl, first, last, *after, inc=False):
            PE(lambda e: e.matmul(out_, xh, wh, start=first, stop=False), *after)
            PE(lambda e: e.matmul(out_, xh, wl, start=False, stop=False))
            return PE(lambda e: e.matmul(out_, xl, wh, start=False, stop=last), inc=inc)

        def threeT(out_, xh, xl, wh, wl, first, last, *after, inc=False):
            PE(lambda e: e.matmul(out_, wh, xh, start=first, stop=False), *after)
            PE(lambda e: e.matmul(out_, wh, xl, start=False, stop=False))
            return PE(lambda e: e.matmul(out_, wl, xh, start=False, stop=last), inc=inc)

        def ffn(h_tok, ada_to=0):
            sgt = SB[:, :, 0, :]
            att = SB[:, :, 1, :]
            silu_free = [d["_sb_free"], d["_sb_free"]]
            a_rel = d["_a_rel"]
            pend = None

            def down(f, n, s, tk):
                w = need(n, 2)
                h, lo = Wh[n % 2], Wl[n % 2]
                for t in range(2):
                    for j in range(2):
                        c = slice(2048 + 512 * j, 2560 + 512 * j)
                        tt = three(PS[:, 2 * t + j, :], ah[s][:, t * 128:t * 128 + 128], al[s][:, t * 128:t * 128 + 128],
                                   h[:, c], lo[:, c], f == 0, f == NF - 1, *w, *tk,
                                   *(free[2 * t + j] if f == 0 else ()), inc=(t == 1 and j == 1) or f == NF - 1)
                        if f == NF - 1:
                            last[2 * t + j] = tt
                done[n, 2] = tt
                a_rel[s] = (tt,)

            last = {}
            for f in range(NF):
                n = next_unit()
                b = 4 + f % 2
                s = f % 2
                h, lo = Wh[n % 2], Wl[n % 2]
                for m in range(2):
                    w = need(n, m)
                    for c in range(8):
                        cc = slice(m * 1024 + c * 128, m * 1024 + c * 128 + 128)
                        tp = threeT(PS[:, b, m * S:m * S + S], Hh[:, c, :], Hl[:, c, :], h[:, cc], lo[:, cc],
                                    c == 0, c == 7, *w, *h_tok[c], *(free[b] if c == 0 and m == 0 else ()), inc=c == 7)
                    done[n, m] = tp
                    if m == 0:
                        tg = tp
                        need(n, 1)
                ada_finish(7)
                need(n, 2)
                tick()
                ada_tick(ada_to)
                tick()
                ts = AC(lambda e: e.activation(sgt[:, s, :], PS[:, b, 0:S], ACT.Silu), tp, *silu_free[s])
                tm = V(lambda e, s=s: e.tensor_tensor(att[:, s, :], sgt[:, s, :], PS[:, b, S:2 * S], ALU.mult), ts, tp,
                       *silu_free[s])
                free[b] = (ts, tm)
                t1 = AC(lambda e, s=s: e.activation(ah[s], att[:, s, :], ACT.Copy), tm, *a_rel[s])
                t2 = V(lambda e, s=s: e.tensor_tensor(al[s], att[:, s, :], ah[s].bitcast(f32), ALU.subtract),
                       t1, *a_rel[s])
                silu_free[s] = (t2,)
                ada_tick(ada_to)
                if pend is not None:
                    down(*pend)
                tick()
                ada_tick(ada_to)
                pend = (f, n, s, (t1, t2))
                d["_h_free"] = (tp,)
            while tick():
                pass
            down(*pend)
            while ada["op"] < 2 * ada_to:
                ada_finish(7)
                ada_tick(ada_to)
            ada_finish(7)
            d["_sb_free"] = silu_free[0] + silu_free[1]
            return last

        d["_a_rel"] = [(), ()]
        d["_sb_free"] = ()

        def residual(last, scale):
            for t in range(2):
                tt = []
                for j in range(2):
                    xs = X[:, t, j * 512:j * 512 + 512]
                    v = V(lambda e, xs=xs, t=t, j=j: e.scalar_tensor_tensor(
                        out=xs, in0=PS[:, 2 * t + j, :], scalar=scale, in1=xs, op0=ALU.mult, op1=ALU.add),
                        last[2 * t + j], *x_tok[t])
                    free[2 * t + j] = (v,)
                    tt.append(v)
                x_tok[t] = tuple(tt)

        def post_norm(last, g_tok):
            for t in range(2):
                q = AC(lambda e, t=t: e.activation(A[:, t, 0:D].rearrange("p (j n) -> p j n", j=2),
                                                   PS[:, 2 * t:2 * t + 2, :], ACT.Square,
                                                   accum_out=st[:, SS + t:SS + t + 1]),
                       last[2 * t], last[2 * t + 1], *a_free[0], *d["_rs_free"])
                r = rstd(t, t + 1, D, q)
                v = V(lambda e, t=t: e.scalar_tensor_tensor(
                    out=A[:, t, 0:D].rearrange("p (j n) -> p j n", j=2), in0=PS[:, 2 * t:2 * t + 2, :],
                    scalar=st[:, RS + t:RS + t + 1], in1=G.rearrange("p (j n) -> p j n", j=2),
                    op0=ALU.mult, op1=ALU.mult), r, q, g_tok)
                free[2 * t] = free[2 * t + 1] = (v,)
                v2 = V(lambda e, t=t: e.tensor_tensor(X[:, t, :], X[:, t, :], A[:, t, 0:D], ALU.add), v, *x_tok[t])
                x_tok[t] = (v2,)
            d["_rs_free"] = (v,)
            d["_g_free"] = (v,)
            d["_gq_free"] = (v,)
            a_free[0] = (v2,)

        bg = []

        def background(k):
            for _ in range(k):
                if bg:
                    bg.pop(0)()

        def project(h_tok, nunits, ncol, v0, hook):
            got = []
            for u in range(nunits):
                n = next_unit()
                h, lo = Wh[n % 2], Wl[n % 2]
                c0, c1 = u * ncol, (u + 1) * ncol
                m = min(max(v0 - c0, 0), ncol)
                toks = []
                for t in range(2):
                    b = (u % 2) * 2 + t
                    for c in range(8):
                        k = min(c // 3, 2)
                        w = need(n, k)
                        cc = slice(c * ncol, (c + 1) * ncol)
                        ts = slice(t * 128, t * 128 + 128)
                        tp = three(PS[:, b, 0:ncol], Hh[:, c, ts], Hl[:, c, ts], h[:, cc], lo[:, cc], c == 0, c == 7,
                                   *w, *h_tok[c], *(free[b] if c == 0 else ()), inc=c in (2, 5, 7))
                        if t == 1 and c in (2, 5, 7):
                            done[n, k] = tp
                    for _ in range(3):
                        if pieces[state["piece"]][0] <= n + nunits - 1 - u:
                            tick()
                    if m:
                        e1 = AC(lambda e: e.activation(A[:, t, c0:c0 + m], PS[:, b, 0:m], ACT.Copy), tp, *a_free[0])
                        toks.append(e1)
                    if m < ncol:
                        vs = slice(c0 + m - v0, c1 - v0)
                        e0 = AC(lambda e: e.activation(Vh[:, t, vs], PS[:, b, m:ncol], ACT.Copy), tp, *d["_v_free"])
                        e1 = V(lambda e: e.tensor_tensor(Vl[:, t, vs], PS[:, b, m:ncol], Vh[:, t, vs].bitcast(f32),
                                                         ALU.subtract), e0)
                        toks += [e0, e1]
                    free[b] = (e1,)
                    background(3)
                got.append(tuple(toks))
                hook(u, got)
            d["_h_free"] = (tp,)
            background(len(bg))
            return got

        def out_proj(h_tok):
            last = {}
            for a, b2 in ((0, 3), (3, 6), (6, 8)):
                n = next_unit()
                h, lo = Wh[n % 2], Wl[n % 2]
                for c in range(a, b2):
                    w = need(n, c - a)
                    for t in range(2):
                        for j in range(2):
                            cc = slice((c - a) * D + j * 512, (c - a) * D + j * 512 + 512)
                            ts = slice(t * 128, t * 128 + 128)
                            tp = three(PS[:, 2 * t + j, :], Hh[:, c, ts], Hl[:, c, ts], h[:, cc], lo[:, cc],
                                       c == 0, c == 7, *w, *h_tok[c], *(free[2 * t + j] if c == 0 else ()),
                                       inc=c == 7 or (t == 1 and j == 1))
                            if c == 7:
                                last[2 * t + j] = tp
                    done[n, c - a] = tp
                    tick()
            d["_h_free"] = (tp,)
            return last

        def transposes(jobs, after, banks):
            got = {}
            for i0 in range(0, len(jobs), 2):
                b = banks[(i0 // 2) % len(banks)]
                grp = jobs[i0:i0 + 2]
                for k, (src, blk, m) in enumerate(grp):
                    for t in range(2):
                        tp = PE(lambda e, k=k, t=t, src=src, m=m: e.transpose(
                            PS[0:m, b, k * S + t * 128:k * S + t * 128 + 128], src(t), ident),
                            tid, *after, *free[b], inc=True)
                blk0, m = grp[0][1], grp[0][2]
                g = len(grp)
                assert all(q[1] == blk0 + k and q[2] == m for k, q in enumerate(grp))
                th, tl = (QTh, QTl) if blk0 < 16 else (Hh, Hl)
                o = blk0 % 16
                src = PS[0:m, b, 0:g * S].rearrange("p (k s) -> p k s", k=g)
                t1 = AC(lambda e: e.activation(th[0:m, o:o + g, :], src, ACT.Copy), tp, *d["_qt_free"])
                t2 = V(lambda e: e.tensor_tensor(tl[0:m, o:o + g, :], src, th[0:m, o:o + g, :].bitcast(f32),
                                                 ALU.subtract), t1, *d["_qt_free"])
                free[b] = (t2,)
                for k in range(g):
                    got[blk0 + k] = t2
            return got

        def qk_parts(rows, blk, cols):
            th, tl = (QTh, QTl) if blk < 16 else (Hh, Hl)
            return th[rows, blk % 16, cols], tl[rows, blk % 16, cols]

        def rope(xs, cs, ss, h, ta, tb, *after, dst=None):
            t1 = V(lambda e: e.tensor_tensor(ta, xs, cs, ALU.mult), *after)
            t2 = V(lambda e: e.tensor_tensor(tb[..., 0:h], xs[..., h:2 * h], ss[..., 0:h], ALU.mult), *after)
            t3 = V(lambda e: e.tensor_tensor(tb[..., h:2 * h], xs[..., 0:h], ss[..., h:2 * h], ALU.mult), *after)
            dst = xs if dst is None else dst
            return V(lambda e: e.tensor_tensor(dst, ta, tb, ALU.add), t1, t2, t3)

        OT = A[:, :, 0:D].rearrange("p t (c q) -> p t c q", q=128)

        def attention(items):
            n = len(items)
            score, probs, ptoks, unit = {}, {}, {}, {}
            u = 0
            for i, it in enumerate(items):
                unit[i] = u
                if it["part"] != "first":
                    u += 1
            sb_free = [d["_sb_free"]] * 3
            pt_free = [(), ()]
            outs = {}

            def stage_s(i):
                it = items[i]
                nk = it["nk"]
                b = 2 * (i % 2)
                for k, (q, kk) in enumerate(it["heads"]):
                    tp = three(PS[:, b + k, 0:nk], *q, *kk, True, True, *it["after"], *free[b + k], inc=k == 1)
                score[i] = tp

            def stage_a(i):
                it = items[i]
                nk, s = it["nk"], i % 3
                b = 2 * (i % 2)
                tp = score[i]
                src = PS[:, b:b + 2, 0:nk]
                nm = st[:, NM + 2 * s:NM + 2 * s + 2]
                if it["bias"] is not None:
                    dst = SB[:, s, :, 0:nk]
                    tb = V(lambda e: e.scalar_tensor_tensor(out=dst, in0=src, scalar=it["scale"], in1=it["bias"],
                                                            op0=ALU.mult, op1=it["op"]), tp, *sb_free[s], *it["after"])
                    free[b] = free[b + 1] = (tb,)
                    tm = V(lambda e: e.tensor_reduce(nm, dst, AX.X, ALU.max, negate=True), tb)
                    src, sc = dst, 1.0
                else:
                    tb = tp
                    tm = V(lambda e: e.tensor_reduce(nm, src, AX.X, ALU.max, negate=True), tp, *sb_free[s])
                    tm = V(lambda e: e.tensor_scalar(nm, nm, it["scale"], None, ALU.mult), tm)
                    sc = it["scale"]
                score[i] = (src, sc, nm, tb, tm, b)

            def stage_e(i):
                it = items[i]
                nk, s = it["nk"], i % 3
                src, sc, nm, tb, tm, b = score[i]
                for k in range(2):
                    te = AC(lambda e: e.activation(SB[:, s, k, 0:nk], src[:, k, :], ACT.Exp, bias=nm[:, k:k + 1], scale=sc,
                                                   accum_out=st[:, Z + 2 * i + k:Z + 2 * i + k + 1]),
                            tb, tm, *sb_free[s], *d["_z_free"])
                if it["bias"] is None:
                    free[b] = free[b + 1] = (te, tm)
                probs[i] = te

            def stage_n(i):
                it = items[i]
                nk, s = it["nk"], i % 3
                zr = st[:, ZR + 2 * i:ZR + 2 * i + 2]
                p0, p1 = SB[:, s, 0, 0:nk], SB[:, s, 1, 0:nk]
                t = V(lambda e: e.reciprocal(zr, st[:, Z + 2 * i:Z + 2 * i + 2]), probs[i], *d["_z_free"])
                if it["part"] == "pair":
                    GP(lambda e: e.tensor_scalar(p0, p0, zr[:, 0:1], None, ALU.mult), t)
                    t = GP(lambda e: e.tensor_scalar(p1, p1, zr[:, 1:2], None, ALU.mult))
                else:
                    t = V(lambda e: e.tensor_tensor(zr[:, 1:2], zr[:, 1:2], st[:, LA:LA + 1], ALU.mult), t, it["lam"])
                    t = V(lambda e: e.tensor_scalar(p1, p1, zr[:, 1:2], None, ALU.mult), t)
                    t = V(lambda e: e.scalar_tensor_tensor(out=p0, in0=p0, scalar=zr[:, 0:1], in1=p1,
                                                           op0=ALU.mult, op1=ALU.add), t)
                ptoks[i] = t

            def stage_b(i):
                it = items[i]
                nk, s, s3 = it["nk"], unit[i] % 2, i % 3
                nc_ = nk // 128
                b = 4 + s
                for k in {"pair": (0, 1), "first": (0,), "last": (1,)}[it["part"]]:
                    for c in range(nc_):
                        col = (2 * c + k) * 128
                        half = k if it["part"] == "pair" else 0
                        tp = PE(lambda e: e.transpose(PS[:, b, col:col + 128], SB[:, s3, half, c * 128:c * 128 + 128],
                                                      ident), ptoks[i], *free[b], inc=True)
                sb_free[s3] = (tp,)
                if it["part"] == "first":
                    return
                w = 2 * nc_ * 128
                src = PS[:, b, 0:w]
                ph, pl = PTh[:, s, :, :].rearrange("p a b -> p (a b)")[:, 0:w], PTl[:, s, :, :].rearrange("p a b -> p (a b)")[:, 0:w]
                t1 = AC(lambda e: e.activation(ph, src, ACT.Copy), tp, *pt_free[s])
                te = V(lambda e: e.tensor_tensor(pl, src, ph.bitcast(f32), ALU.subtract), t1, *pt_free[s])
                free[b] = (te,)
                ptoks["u", i] = te

            def stage_c(i):
                it = items[i]
                if it["part"] == "first":
                    return
                nk, s, t, ch = it["nk"], unit[i] % 2, it["t"], it["chunk"]
                nc_ = nk // 128
                b = 6 + s
                ph, pl = PTh[:, s, :, :].rearrange("p a b -> p (a b)"), PTl[:, s, :, :].rearrange("p a b -> p (a b)")
                for c in range(nc_):
                    m = slice(c * S, c * S + S)
                    tp = threeT(PS[:, b, 0:S], ph[:, m], pl[:, m], *it["v"][c], c == 0, c == nc_ - 1,
                                ptoks["u", i], *it["after"], *free[b], inc=c == nc_ - 1)
                pt_free[s] = (tp,)
                got = []
                for k in range(2):
                    rows = slice(64 * k, 64 * k + 64)
                    src = PS[rows, b, k * 128:k * 128 + 128]
                    if it["direct"]:
                        hh = Hh[rows, ch, t * 128:t * 128 + 128]
                        hl = Hl[rows, ch, t * 128:t * 128 + 128]
                        t1 = AC(lambda e: e.activation(hh, src, ACT.Copy), tp, *d["_h_free"])
                        got.append(V(lambda e: e.tensor_tensor(hl, src, hh.bitcast(f32), ALU.subtract), t1,
                                     *d["_h_free"]))
                    elif k == 0:
                        got.append(AC(lambda e: e.activation(OT[rows, t, ch, :], src, ACT.Copy), tp, *it["ofree"]))
                    else:
                        got.append(V(lambda e: e.tensor_copy(OT[rows, t, ch, :], src), tp, *it["ofree"]))
                free[b] = tuple(got)
                outs[ch, t] = tuple(got)
                if it.get("done") is not None:
                    it["done"](ch, t, outs)

            stage_s(0)
            for i in range(n + 3):
                if i + 1 < n:
                    stage_s(i + 1)
                if i < n:
                    stage_a(i)
                if 0 <= i - 1 < n:
                    stage_n(i - 1)
                if 0 <= i - 2 < n:
                    stage_b(i - 2)
                if i < n:
                    stage_e(i)
                if 0 <= i - 3 < n:
                    stage_c(i - 3)
                if i % 3 == 0:
                    tick()
            every = tuple(x for o in outs.values() for x in o)
            last = (*outs[items[-1]["chunk"], items[-1]["t"]], *outs[items[-2]["chunk"], items[-2]["t"]])
            d["_sb_free"] = every
            d["_qt_free"] = d["_v_free"] = ada["v_free"] = last
            d["_z_free"] = last
            return outs, every

        def chunk_scaled(ch, row, scale, *after):
            ht = HT[:, ch % 4, :].rearrange("p (t q) -> p t q", t=2)
            t1 = V(lambda e: e.scalar_tensor_tensor(out=ht, in0=row, scalar=scale, in1=OT[:, :, ch, :],
                                                    op0=ALU.mult, op1=ALU.mult),
                   *after, *d["_ht_free"][ch % 4], *d["_sb_free"])
            hh, hl = Hh[:, ch, :], Hl[:, ch, :]
            hf = HT[:, ch % 4, :]
            t2 = AC(lambda e: e.activation(hh, hf, ACT.Copy), t1, *d["_h_free"])

            def rest():
                t3 = V(lambda e: e.tensor_tensor(hl, hf, hh.bitcast(f32), ALU.subtract), t2, *d["_h_free"])
                d["_ht_free"][ch % 4] = (t3,)
                return (t2, t3)

            return rest, t1

        d["_z_free"] = d["_v_free"] = ()
        d["_qt_free"] = ()
        d["_rs_free"] = ()
        d["_g_free"] = ()
        d["_bt_free"] = ()
        d["_gq_free"] = ()

        def bc(ap, shape):
            return ap.to_broadcast(shape)

        def first_mixer(l):
            tbt = DMA("sp", "bt", BT[:, :, :, :], d["nab"][l], *d["_bt_free"], *ada["free"][0], *ada["free"][1])
            tgq = DMA("sp", "gq", GQ[:, :], d["gq"][l], *d["_gq_free"], *ada["acc_free"], *ada["row_free"])
            lam_init = 0.8 - 0.6 * math.exp(-0.3 * l)
            la = sm(f"la{l}")
            lt = st[:, FQ + 32:FQ + 96].rearrange("p (a n) -> p a n", a=2)
            t = V(lambda e: e.tensor_tensor(lt, la.rearrange("p (a b n) -> p a b n", a=2, b=2)[:, :, 0, :],
                                            la.rearrange("p (a b n) -> p a b n", a=2, b=2)[:, :, 1, :], ALU.mult),
                  tsm, *d["_z_free"])
            t = V(lambda e: e.tensor_reduce(st[:, LA:LA + 2], lt, AX.X, ALU.add), t)
            h_tok = norm_T(sm(f"mx{l}"))
            t = AC(lambda e: e.activation(st[:, LA + 2:LA + 4], st[:, LA:LA + 2], ACT.Exp), t)
            t = V(lambda e: e.tensor_scalar(st[:, LA + 3:LA + 4], st[:, LA + 3:LA + 4], -lam_init, None, ALU.add), t)
            lam_tok = V(lambda e: e.tensor_tensor(st[:, LA:LA + 1], st[:, LA + 3:LA + 4], st[:, LA + 2:LA + 3],
                                                  ALU.subtract), t)
            groups = {1: (0, 11, 64), 3: (704, 11, 64), 5: (1408, 16, 32)}
            fin = {}
            toks_qk = []

            def norms(u, got):
                if u in groups:
                    bg.extend(norm_steps(u, [x for p in got for x in p]))
                if u == 7:
                    d["_v_tok"] = [x for p in got for x in p]

            def norm_steps(u, dep):
                c0, nh, n = groups[u]
                q = A[:, :, c0:c0 + nh * n].rearrange("p t (h n) -> p t h n", n=n)
                s_ = WK[:, 0:nh * n].rearrange("p (h n) -> p h n", h=nh)
                gb = GQ[:, c0:c0 + nh * n].rearrange("p (h n) -> p h n", n=n)
                ss = st[:, SS:SS + 2 * nh].rearrange("p (t h) -> p t h", t=2)
                rs = st[:, RS:RS + 2 * nh].rearrange("p (t h) -> p t h", t=2)
                box = {"t": None}

                def sums(t_):
                    t = AC(lambda e: e.activation(s_, q[:, t_], ACT.Square), *dep, *d["_sb_free"], *d.get("_rope_free", ()))
                    t = V(lambda e: e.tensor_reduce(ss[:, t_], s_, AX.X, ALU.add), t, *d["_rs_free"])
                    d["_sb_free"] = (t,)
                    box["t"] = t

                def root():
                    box["t"] = rstd_v(0, 2 * nh, n, box["t"])

                def scaled(t_):
                    v = V(lambda e: e.tensor_tensor(q[:, t_], q[:, t_],
                                                    rs[:, t_].unsqueeze(2).to_broadcast([128, nh, n]), ALU.mult),
                          box["t"])
                    d["_rs_free"] = (v,)
                    box[t_] = v

                def gained(t_):
                    fin[u, t_] = V(lambda e: e.tensor_tensor(q[:, t_], q[:, t_], gb, ALU.mult), box[t_], tgq)
                    toks_qk.append(fin[u, t_])

                return [lambda: sums(0), lambda: sums(1), root, lambda: scaled(0), lambda: gained(0),
                        lambda: scaled(1), lambda: gained(1), *rope_steps(u)]

            ta, tb = WK[:, 0:256], WK[:, 256:512]

            def rope_steps(u):
                steps = []
                for t_ in range(2):
                    if u == 1:
                        continue
                    if u == 3:
                        jobs = [(A[:, t_, 512:1024].rearrange("p (h n) -> p h n", n=64)[:, :, 0:16], "dl", t_ * 16, 8, 16)]
                        for y in range(2):
                            jobs.append((A[:, t_, 1024:1408].rearrange("p (h y n) -> p h y n", y=2, n=32)[:, :, y, :],
                                         "ax", t_ * 64 + y * 32, 6, 32))
                    else:
                        jobs = [(A[:, t_, 1408:1920].rearrange("p (h n) -> p h n", n=32)[:, :, 0:8], "df", t_ * 8, 16, 8)]
                    for job in jobs:
                        steps.append(lambda t_=t_, job=job: rope_step(u, t_, *job))
                return steps

            def rope_step(u, t_, xs, nm, o, nh, n):
                cs = bc(cn(nm + "c", o, o + n).unsqueeze(1), [128, nh, n])
                s_ = bc(cn(nm + "s", o, o + n).unsqueeze(1), [128, nh, n])
                d["_rope"] = rope(xs, cs, s_, n // 2, ta[:, 0:nh * n].rearrange("p (h n) -> p h n", n=n),
                                  tb[:, 0:nh * n].rearrange("p (h n) -> p h n", n=n),
                                  fin[u, t_], fin[1, t_], tc, *d["_sb_free"], *d.get("_rope_free", ()))
                d["_rope_free"] = (d["_rope"],)

            pr = project(h_tok, WIN_U, WIN_N, 1920, norms)
            r1 = d["_rope"]
            d["_sb_free"] = (r1,)
            tk = transposes([(lambda t, c=c: A[:, t, c * 128:c * 128 + 128], c, 128) for c in range(15)],
                            (r1, *toks_qk), (4, 5, 6, 7))
            vt = [x for p in pr for x in p]
            VN, VD, VG, VF = 0, 256, 512, 640
            items = []

            def item(t, heads, bias, op, chunk, scale, blocks, v0, part="pair", extra=()):
                items.append(dict(t=t, nk=S, heads=heads, bias=bias, op=op, chunk=chunk, scale=scale, part=part,
                                  lam=lam_tok, after=tuple(tk[b] for b in blocks) + tuple(vt) + tuple(extra),
                                  direct=part == "pair", ofree=tuple(tk.values()),
                                  v=[(Vh[:, c, v0:v0 + 128], Vl[:, c, v0:v0 + 128]) for c in range(2)]))

            al_ = slice(0, S)
            for t in range(2):
                q_ = slice(t * 128, t * 128 + 128)
                half = [slice(64 * k, 64 * k + 64) for k in range(2)]
                for h in range(4):
                    hs = []
                    for k in range(2):
                        r = (2 * h + k) % 4 * 32
                        blk = (2 * h + k) // 4
                        rr = slice(r, r + 32)
                        hs.append((qk_parts(rr, 11 + blk, q_), qk_parts(rr, 13 + blk, al_)))
                    item(t, hs, None, None, 6 + h // 2, 32 ** -0.5, (11 + blk, 13 + blk), VF + h // 2 * 128,
                         part=("first", "last")[h % 2])
                for p in range(2):
                    hs = [(qk_parts(half[k], 4 + p, q_), qk_parts(half[k], 6 + p, al_)) for k in range(2)]
                    lnb = cn("ln", t * S, t * S + S).unsqueeze(1).to_broadcast([128, 2, S])
                    item(t, hs, lnb, ALU.add, 2 + p, 0.125, (4 + p, 6 + p), VD + p * 128, extra=(tc,))
                for p in range(2):
                    hs = [(qk_parts(half[k], 8 + p, q_), qk_parts(half[k], 10, al_)) for k in range(2)]
                    item(t, hs, None, None, 4 + p, 0.125, (8 + p, 10), VG)
                for p in range(2):
                    hs = [(qk_parts(half[k], p, q_), qk_parts(half[k], 2 + p, al_)) for k in range(2)]
                    item(t, hs, BT[:, t, 2 * p:2 * p + 2, :], ALU.add, p, 0.125, (p, 2 + p), VN + p * 128,
                         extra=(tbt,))
            outs, every = attention(items)
            d["_bt_free"] = every
            ada["free"] = [every, every]
            ada["acc_free"] = ada["row_free"] = every
            sq = WK[:, 1024:1536].rearrange("p (t c q) -> p t c q", t=2, c=2)
            tsq = AC(lambda e: e.activation(sq, OT[:, :, 6:8, :], ACT.Square),
                     *outs[6, 0], *outs[7, 0], *outs[6, 1], *outs[7, 1], *d["_sb_free"])
            for t_ in range(2):
                for c in range(2):
                    o = 4 * t_ + 2 * c
                    tp = PE(lambda e: e.matmul(PS[:, 4, o:o + 2], sq[:, t_, c, :], cn("bo", 0, 2), start=True,
                                               stop=True), tsq, tc, *free[4], inc=True)
            tv = V(lambda e: e.tensor_copy(st[:, SS:SS + 8], PS[:, 4, 0:8]), tp, *d["_rs_free"])
            free[4] = (tv,)
            r = rstd_v(0, 8, 64, tv, mul=1.0 - lam_init)
            rw = V(lambda e: e.tensor_copy(WK[:, 1024:1536].rearrange("p (g n) -> p g n", n=64),
                                           st[:, RS:RS + 8].unsqueeze(2).to_broadcast([128, 8, 64])), r, tp)
            for c in range(2):
                for t_ in range(2):
                    tp = PE(lambda e: e.matmul(PS[:, 5, c * S + t_ * 128:c * S + t_ * 128 + 128], sq[:, t_, c, :], ident,
                                               start=True, stop=True), rw, tid, *free[5], inc=True)
            d["_sb_free"] = (*d["_sb_free"], tp)
            h_tok = [(*outs[ch, 0], *outs[ch, 1]) for ch in range(6)]
            rests = []
            for c in range(2):
                rest, tr = chunk_scaled(6 + c, PS[:, 5, c * S:c * S + S].rearrange("p (t q) -> p t q", t=2),
                                        sm(f"os{l}", 6 + c, 7 + c), tp, tsm)
                rests.append(rest)
            h_tok += [rest() for rest in rests]
            free[5] = (tr,)
            d["_rs_free"] = (tp,)
            a_free[0] = (tr, tsq)
            residual(out_proj(h_tok), 1.0)

        def load_g(l, which, post):
            tmp = BT[:, 0, :, :].rearrange("p a b -> p (a b)")
            w = (*mod_written[l], *d["_g_free"], *d["_bt_free"], *d["_gq_free"], *x_tok[1])
            t1 = DMA("sp", "g", G, modd[l:l + 1, which * D:(which + 1) * D].to_broadcast([128, D]), *w)
            t2 = DMA("sp", "g2", tmp, d[post][l:l + 1, :].to_broadcast([128, D]), *w)
            t = V(lambda e: e.tensor_tensor(G, G, tmp, ALU.mult), t1, t2)
            d["_bt_free"] = (t,)
            return t

        def load_cols(l):
            for i, k in enumerate((0, 1, 3, 4)):
                t = DMA("sp", f"mc{i}", mcol[:, i, :], modd[l, k * D:(k + 1) * D].rearrange("(c p) -> p c", p=128),
                        *mod_written[l], *d["_mc_free"], slow=True)
                d["_mc"][i] = t
            t = V(lambda e: e.scalar_tensor_tensor(out=mcol[:, 1, :], in0=mcol[:, 1, :], scalar=1.0,
                                                   in1=sm(f"pm{l}"), op0=ALU.add, op1=ALU.mult), d["_mc"][1], tsm)
            t2 = V(lambda e: e.scalar_tensor_tensor(out=mcol[:, 3, :], in0=mcol[:, 3, :], scalar=1.0,
                                                    in1=sm(f"pf{l}"), op0=ALU.add, op1=ALU.mult), d["_mc"][3], tsm)
            d["_colw"] = (tsm, t, t2, d["_mc"][0], d["_mc"][2])

        d["_mc"] = {}
        d["_mc_free"] = ()

        def second_mixer(l):
            tbt = DMA("sp", "bt", BT[:, :, :, :], d["t5b"], *d["_bt_free"], *ada["free"][0], *ada["free"][1])
            load_cols(l)
            h_tok = norm_T(mcol[:, 1, :], mcol[:, 0, :])
            tk = {}
            box = {}

            def hook(u, got):
                if u == 3:
                    box["qk"] = [x for p in got for x in p]
                if u == 4:
                    tk.update(transposes([(lambda t, c=c: A[:, t, c * 128:c * 128 + 128], c, 128) for c in range(8)],
                                         box["qk"], (4, 5, 6, 7)))
                    bg.extend(late_steps([x for p in got for x in p]))

            z = st[:, LF:LF + 8].rearrange("p (t h) -> p t h", t=2)
            mn = st[:, LF + 8:LF + 16]
            mx = st[:, LF + 16:LF + 24]
            lf = st[:, LF + 24:LF + 32]
            lh, ll = lfr[:, 0, :], lfr[:, 1, :]
            KR = GQ[:, 1536:1600].rearrange("p (t n) -> p t n", t=2)
            ta, tb = WK[:, 0:256], WK[:, 256:512]

            def late_steps(dep):
                def forget():
                    bfv = sm(f"bf{l}").unsqueeze(1).to_broadcast([128, 2, 4])
                    t0 = V(lambda e: e.tensor_tensor(z, A[:, :, 1440:1444], bfv, ALU.add), *dep, tsm, *d["_lf_free"])
                    zf = st[:, LF:LF + 8]
                    t1 = V(lambda e: e.tensor_scalar(mn, zf, 0.0, None, ALU.min), t0)
                    t2 = V(lambda e: e.tensor_scalar(mx, zf, 0.0, None, ALU.max), t0)
                    t3 = V(lambda e: e.tensor_tensor(mx, mn, mx, ALU.subtract), t1, t2)
                    t4 = AC(lambda e: e.activation(mx, mx, ACT.Exp), t3)
                    t4 = AC(lambda e: e.activation(mx, mx, ACT.Ln, bias=1.0), t4)
                    t5 = V(lambda e: e.tensor_tensor(lf, mn, mx, ALU.subtract), t4, t1)
                    t6 = AC(lambda e: e.activation(lh, lf, ACT.Copy), t5)
                    box["lf"] = (t6, V(lambda e: e.tensor_tensor(ll, lf, lh.bitcast(f32), ALU.subtract), t6))

                def squares(t_):
                    q1 = AC(lambda e: e.activation(WK[:, 512 * t_:512 * t_ + 256], A[:, t_, 1024:1280], ACT.Square,
                                                   accum_out=st[:, SS + t_:SS + t_ + 1]), *dep, *d["_rs_free"],
                            *d["_sb_free"])
                    q2 = AC(lambda e: e.activation(WK[:, 512 * t_ + 256:512 * t_ + 384], A[:, t_, 1280:1408], ACT.Square,
                                                   accum_out=st[:, SS + 2 + t_:SS + 3 + t_]), *d["_rs_free"])
                    box["q", t_] = (q1, q2)

                def roots():
                    box["r"] = (rstd(0, 2, 256, *box["q", 0], *box["q", 1]), rstd(2, 4, 128))

                def scales(t_):
                    v1 = V(lambda e: e.tensor_scalar(A[:, t_, 1024:1280], A[:, t_, 1024:1280],
                                                     st[:, RS + t_:RS + t_ + 1], None, ALU.mult), *box["r"])
                    v2 = V(lambda e: e.tensor_scalar(A[:, t_, 1280:1408], A[:, t_, 1280:1408],
                                                     st[:, RS + 2 + t_:RS + 3 + t_], None, ALU.mult), *box["r"])
                    box["s", t_] = (v1, v2)
                    d["_rs_free"] = (v1, v2)

                def kr_rope(t_):
                    box["kr"] = rope(A[:, t_, 1408:1440], cn("mlc", t_ * 32, t_ * 32 + 32),
                                     cn("mls", t_ * 32, t_ * 32 + 32), 16, ta[:, 0:32], tb[:, 0:32],
                                     *dep, tc, *box["q", 0], *box["q", 1], *d["_sb_free"], *d["_gq_free"],
                                     *([box["kr"]] if "kr" in box else []), dst=KR[:, t_, :])

                return [lambda: squares(0), lambda: squares(1), roots, forget, lambda: scales(0), lambda: scales(1),
                        lambda: kr_rope(0), lambda: kr_rope(1)]

            pr = project(h_tok, WIN2_U, WIN2_N, 1444, hook)
            pa = [x for p in pr for x in p]
            kr = box["kr"]
            tl = box["lf"]
            for h in range(4):
                b = 4 + h // 2
                for c in range(2):
                    for k, part in enumerate((lh, ll)):
                        tf = PE(lambda e: e.matmul(
                            PS[:, b, (h % 2) * S:(h % 2) * S + S],
                            part[:, 4 * c + h:4 * c + h + 1].to_broadcast([128, 128]), Ur[:, c, :],
                            start=c == 0 and k == 0, stop=c == 1 and k == 1), *tl, t_u, *free[b],
                            inc=h == 3 and c == 1 and k == 1)
            for t_ in range(2):
                for c in range(2):
                    for k, part in enumerate((lh, ll)):
                        tq = PE(lambda e: e.matmul(
                            PS[:, 6, 4 * t_:4 * t_ + 4], Ur[:, c, t_ * 128:t_ * 128 + 128], part[:, 4 * c:4 * c + 4],
                            start=c == 0 and k == 0, stop=c == 1 and k == 1), *free[6], inc=True)
            fq = V(lambda e: e.tensor_copy(st[:, FQ:FQ + 8], PS[:, 6, 0:8]), tq)
            free[6] = (fq,)
            FB = GQ[:, 0:1536].rearrange("p (h n) -> p h n", h=4)
            pmask = cn("pm")
            for h in range(4):
                for t_ in range(2):
                    nk = 128 * (t_ + 1)
                    o = 0 if t_ == 0 else 128
                    src = PS[:, 4 + h // 2, (h % 2) * S:(h % 2) * S + nk]
                    tfb = V(lambda e, h=h, t_=t_, nk=nk, o=o, src=src: e.scalar_tensor_tensor(
                        out=FB[:, h, o:o + nk], in0=src, scalar=st[:, FQ + 4 * t_ + h:FQ + 4 * t_ + h + 1],
                        in1=pmask[:, 256 - nk:256], op0=ALU.subtract, op1=ALU.add), tf, fq, *d["_gq_free"],
                        *ada["acc_free"], *ada["row_free"])
                    if t_:
                        free[4 + h // 2] = (tfb,)
            d["_lf_free"] = (tq, tfb)
            o0 = SM_OFF[f"pq{l}"][0]
            lt = to_T(A, [1024, 1152, 1280], SM[:, o0:o0 + 3], lambda i, t: box["s", t])
            n = next_unit()
            h, lo = Wh[n % 2], Wl[n % 2]
            ev = []
            KLv = A[:, :, 768:1536].rearrange("p t (h n) -> p t h n", n=96)
            QLv = A[:, :, 0:768].rearrange("p t (h n) -> p t h n", n=96)
            for t_ in range(2):
                kc_ = V(lambda e: e.tensor_copy(
                    KLv[:, t_, :, 64:96], KR[:, t_, :].unsqueeze(1).to_broadcast([128, 8, 32])), kr,
                    *tk.values(), *lt[0], *lt[1], *lt[2], *tl)
            tkv = tuple(tk.values())
            for t_ in range(2):
                ts = slice(t_ * 128, t_ * 128 + 128)
                for j, (a, w_) in enumerate(((0, 512), (512, 256))):
                    b = 2 * 0 + j
                    for c in range(2):
                        w = need(n, c)
                        cc = slice(c * 768 + a, c * 768 + a + w_)
                        tp = three(PS[:, b, 0:w_], Hh[:, c, ts], Hl[:, c, ts], h[:, cc], lo[:, cc], c == 0, c == 1,
                                   *w, *lt[c], *(free[b] if c == 0 else ()), inc=c == 1)
                    dst = QLv[:, t_, :, 0:64] if j == 0 else QLv[:, t_, :, 64:96]
                    src = PS[:, b, 0:w_].rearrange("p (h n) -> p h n", h=8)
                    e_ = AC(lambda e, dst=dst, src=src: e.activation(dst, src, ACT.Copy), tp, *tkv)
                    free[b] = (e_,)
                    ev.append(e_)
                if t_ == 1:
                    done[n, 0] = done[n, 1] = tp
                w = need(n, 2)
                for j in range(2):
                    b = 2 + j
                    cc = slice(1536 + j * 512, 2048 + j * 512)
                    tp = three(PS[:, b, 0:512], Hh[:, 2, ts], Hl[:, 2, ts], h[:, cc], lo[:, cc], True, True,
                               *w, *lt[2], *free[b], inc=True)
                    src = PS[:, b, 0:512].rearrange("p (h n) -> p h n", h=8)
                    if j == 0:
                        e_ = V(lambda e: e.tensor_copy(KLv[:, t_, :, 0:64], src), tp, kc_)
                    else:
                        vh_, vl_ = Vh[:, t_, 512:1024], Vl[:, t_, 512:1024]
                        e0 = AC(lambda e: e.activation(vh_, PS[:, b, 0:512], ACT.Copy), tp, *d["_v_free"])
                        e_ = V(lambda e: e.tensor_tensor(vl_, PS[:, b, 0:512], vh_.bitcast(f32), ALU.subtract), e0)
                        ev.append(e0)
                    free[b] = (e_,)
                    ev.append(e_)
                if t_ == 1:
                    done[n, 2] = tp
            d["_h_free"] = (tp,)
            rp = [kr, *ev]
            for t_ in range(2):
                xs = QLv[:, t_, :, 64:96]
                cs = bc(cn("mlc", t_ * 32, t_ * 32 + 32).unsqueeze(1), [128, 8, 32])
                s_ = bc(cn("mls", t_ * 32, t_ * 32 + 32).unsqueeze(1), [128, 8, 32])
                r1_ = rope(xs, cs, s_, 16, ta[:, 0:256].rearrange("p (h n) -> p h n", n=32),
                           tb[:, 0:256].rearrange("p (h n) -> p h n", n=32), *rp)
                rp = [r1_]
            d["_sb_free"] = (r1_,)
            jobs = [(lambda t, hh=hh: A[:, t, hh * 96:hh * 96 + 96], 8 + hh, 96) for hh in range(8)]
            jobs += [(lambda t, hh=hh: A[:, t, 768 + hh * 96:768 + hh * 96 + 96], 16 + hh, 96) for hh in range(8)]
            d["_qt_free"] = (*d["_qt_free"], *d["_h_free"])
            tk2 = transposes(jobs, (r1_, kc_, *ev), (4, 5, 6, 7))
            of = tuple(tk2.values())
            items = []

            def vv(c0, nk):
                return [(Vh[:, c, c0:c0 + 128], Vl[:, c, c0:c0 + 128]) for c in range(nk // 128)]

            sq_tok = {}

            def sqv(ch):
                return (R[:, :].rearrange("p (t q) -> p t q", t=2) if ch == 7
                        else A[:, :, D + 128 * ch:D + 128 * ch + 128])

            def squared(ch, t, outs):
                dst = sqv(ch)
                sq_tok[ch] = AC(lambda e: e.activation(dst, OT[:, :, ch, :], ACT.Square), *outs[ch, 0], *outs[ch, 1],
                                *of)

            for t in range(2):
                nk = 128 * (t + 1)
                q_ = slice(t * 128, t * 128 + 128)
                o = 0 if t == 0 else 128
                half = [slice(64 * k, 64 * k + 64) for k in range(2)]
                aft = (*tk.values(), *tk2.values(), *ev, *pa, tbt, tfb, tc)
                rest = dict(t=t, nk=nk, part="pair", direct=False, after=aft, ofree=of, done=squared if t else None)
                for p in range(2):
                    hs = [(qk_parts(half[k], p, q_), qk_parts(half[k], 2 + p, slice(0, nk))) for k in range(2)]
                    items.append(dict(heads=hs, bias=FB[:, 2 * p:2 * p + 2, o:o + nk], op=ALU.subtract,
                                      chunk=p, scale=0.125, v=vv(128 * p, nk), **rest))
                for p in range(2):
                    hs = [(qk_parts(half[k], 4 + p, q_), qk_parts(half[k], 6 + p, slice(0, nk))) for k in range(2)]
                    items.append(dict(heads=hs, bias=BT[:, t, 2 * p:2 * p + 2, 0:nk], op=ALU.add,
                                      chunk=2 + p, scale=0.125, v=vv(256 + 128 * p, nk), **rest))
                for p in range(4):
                    hs = [(qk_parts(slice(0, 96), 8 + 2 * p + k, q_), qk_parts(slice(0, 96), 16 + 2 * p + k, slice(0, nk)))
                          for k in range(2)]
                    items.append(dict(heads=hs,
                                      bias=pmask[:, 256 - nk:256].unsqueeze(1).to_broadcast([128, 2, nk]),
                                      op=ALU.subtract, chunk=4 + p, scale=96 ** -0.5, v=vv(512 + 128 * p, nk), **rest))
            outs, every = attention(items)
            d["_bt_free"] = d["_gq_free"] = d["_h_free"] = every
            tg = load_g(l, 2, "g_mix_post")
            for t_ in range(2):
                for ch in range(8):
                    tp = PE(lambda e: e.matmul(PS[:, 6, 8 * t_ + ch:8 * t_ + ch + 1], sqv(ch)[:, t_, :], cn("bo", 2, 3),
                                               start=True, stop=True), sq_tok[ch], tc, *free[6], inc=ch == 7)
            for g, (a, b) in enumerate(((0, 2), (2, 4), (4, 8))):
                tv = V(lambda e: e.tensor_reduce(
                    st[:, SS + 2 * g:SS + 2 * g + 2], PS[:, 6, 0:16].rearrange("p (t c) -> p t c", t=2)[:, :, a:b],
                    AX.X, ALU.add), tp, *d["_rs_free"])
            free[6] = (tv,)
            tv = V(lambda e: e.tensor_scalar(st[:, SS + 4:SS + 6], st[:, SS + 4:SS + 6], 0.5, None, ALU.mult), tv)
            r = rstd_v(0, 6, 256, tv)
            for g in range(3):
                for t_ in range(2):
                    o = RS + 2 * g + t_
                    tp = PE(lambda e: e.matmul(PS[:, 4 + g // 2, g % 2 * S + t_ * 128:g % 2 * S + t_ * 128 + 128],
                                               st[:, o:o + 1].to_broadcast([128, 128]), ident,
                                               start=True, stop=True), r, tid, *free[4], *free[5], inc=True)
            h_tok = []
            rest = None
            for ch in range(8):
                g = (0, 0, 1, 1, 2, 2, 2, 2)[ch]
                before = rest
                rest, tr = chunk_scaled(ch, PS[:, 4 + g // 2, g % 2 * S:g % 2 * S + S].rearrange("p (t q) -> p t q", t=2),
                                        sm(f"pg{l}", ch, ch + 1), tp, tsm, *every)
                if before is not None:
                    h_tok.append(before())
            h_tok.append(rest())
            free[4] = free[5] = (tr,)
            d["_rs_free"] = (tp,)
            a_free[0] = (tr, tp)
            post_norm(out_proj(h_tok), tg)

        d["_lf_free"] = ()

        for l in range(L):
            residual(ffn(norm_T(sm(f"f1{l}")), NADA * (2 * l + 1) // 4), 0.5)
            first_mixer(l)
            residual(ffn(norm_T(sm(f"f2{l}")), NADA * (2 * l + 2) // 4), 0.5)
        for l in range(L):
            second_mixer(l)
            h = norm_T(mcol[:, 3, :], mcol[:, 2, :])
            tg = load_g(l, 5, "g_ffn_post")
            last = ffn(h)
            d["_mc_free"] = h[-1]
            post_norm(last, tg)
        assert state["piece"] == len(pieces) == state["load"]
        DMA("sp", "out", out.rearrange("(t p) n -> p t n", t=2), X[:, :, :], *x_tok[0], *x_tok[1])
        for key in ("out", "mod"):
            queue["sp"].append((("wait_ge", (key, count[key]), {}), None, 0))

        block = ctx.enter_context(nc.Block())

        def run(e, name):
            for (op, a, k), sem, by in queue[name]:
                if op == "wait_ge":
                    e.wait_ge(sems[a[0]], a[1])
                    continue
                ins = CALLS[op](e, a, k)
                if sem is not None:
                    ins.then_inc(sems[sem], by)

        block.sync(lambda e: run(e, "sp"))
        block.scalar(lambda e: run(e, "act"))
        block.vector(lambda e: run(e, "dve"))
        block.gpsimd(lambda e: run(e, "pool"))
        block.tensor(lambda e: run(e, "pe"))


def constants():
    f = np.float32
    c = np.zeros((128, C_N), f)
    bo = np.ones((128, 4), f)
    bo[64:, 0] = 0
    bo[:64, 1] = 0

    def put(name, v):
        o, n = C_OFF[name]
        c[:, o:o + n] = np.asarray(v, f).reshape(128, n)

    i = np.arange(128)
    put("id", np.eye(128))
    put("bo", bo)
    pm = np.zeros((128, 256), f)
    pm[:, 128:] = np.where(i[None, :] <= i[:, None], 0.0, BIG)
    put("pm", pm)
    q = np.arange(S)
    dd = q[None, :] - q[:, None]
    m = (np.abs(dd) <= 64).astype(np.float64) + (dd % 4 == 0) + (dd % 16 == 0)
    ln = np.where(m > 0, np.log(np.maximum(m, 1)), -BIG).astype(f)
    put("ln", ln.reshape(2, 128, S).transpose(1, 0, 2))

    def table(pos, dim, theta):
        inv = (f(1.0) / (f(theta) ** (np.arange(0, dim, 2, dtype=f) / f(dim)))).astype(f)
        ang = pos.astype(f)[:, None] * inv[None, :]
        co, si = np.cos(ang).astype(f), np.sin(ang).astype(f)
        return np.concatenate([co, co], 1), np.concatenate([-si, si], 1)

    def halves(a):
        return a.reshape(2, 128, -1).transpose(1, 0, 2)

    for n, args in (("df", (q, 8, 500000.0)), ("dl", (q, 16, 500000.0)), ("ml", (q, 32, 10000.0))):
        a, b = table(*args)
        put(n + "c", halves(a))
        put(n + "s", halves(b))
    r, k = table(q // 64, 32, 10000.0), table(q % 64, 32, 10000.0)
    put("axc", halves(np.concatenate([r[0], k[0]], 1)))
    put("axs", halves(np.concatenate([r[1], k[1]], 1)))
    return c


def t5_buckets(n):
    f = np.float32
    nf = np.maximum(n, 16).astype(f)
    large = 16 + (np.log(nf / f(16)).astype(f) / f(math.log(128 / 16)) * f(16)).astype(np.int32)
    return np.where(n < 16, n, np.minimum(large, 31))


def kernel(**inputs):
    import numpy as np
    import concourse.bacc as _bacc
    from concourse import mybir as _mybir
    from concourse.bass_utils import run_bass_kernel_spmd as _run

    I = {k: np.asarray(v) for k, v in inputs.items()}
    f = np.float32
    C = np.ascontiguousarray

    def chunks(w, a, b):
        k = w.shape[0] // 128
        return w[:, a:b].reshape(k, 128, b - a).transpose(1, 0, 2).reshape(128, -1)

    def ffn(gate, up, down):
        g = gate.reshape(8, 128, NF, 128).transpose(2, 1, 0, 3).reshape(NF, 128, 1024)
        u = up.reshape(8, 128, NF, 128).transpose(2, 1, 0, 3).reshape(NF, 128, 1024)
        return np.concatenate([g, u, down.reshape(NF, 128, 1024)], axis=2)

    ffns = []
    for l in range(L):
        ffns.append(ffn(I["ffn1_w_gate"][l], I["ffn1_w_up"][l], I["ffn1_w_down"][l]))
        ffns.append(ffn(I["ffn2_w_gate"][l], I["ffn2_w_up"][l], I["ffn2_w_down"][l]))
    for l in range(L):
        gu = I["w_gate_up_2"][l]
        ffns.append(ffn(gu[:, :F], gu[:, F:], I["w_down_2"][l]))
    A = {"ffn": np.concatenate(ffns)}

    names = ["nq", "nk", "nv", "fq", "fk", "fv", "gq", "gk", "gv", "dq", "dk", "dv"]
    sizes = [256, 256, 256, 256, 256, 256, 256, 128, 128, 256, 256, 256]
    at = dict(zip(names, np.cumsum([0] + sizes[:-1])))
    sz = dict(zip(names, sizes))
    rng = {n: np.arange(at[n], at[n] + sz[n]) for n in names}
    gq_perm = np.concatenate([np.arange(h * 64, h * 64 + 64) for h in (0, 2, 1, 3)])
    cols = np.concatenate([rng["nq"], rng["nk"], rng["dq"], rng["dk"], rng["gq"][gq_perm], rng["gk"],
                           rng["fq"], rng["fk"], rng["nv"], rng["dv"], rng["gv"], rng["fv"]])
    A["win"] = np.concatenate([np.stack([chunks(I["w_in"][l][:, cols], u * WIN_N, (u + 1) * WIN_N)
                                         for u in range(WIN_U)]) for l in range(L)])
    rows = np.concatenate([np.arange(0, 256), np.arange(768, 1024), 512 + gq_perm, np.arange(256, 512)])
    A["wo"] = np.stack([chunks(I["w_out"][l][rows], 0, D) for l in range(L)]
                       + [chunks(I["w_out_2"][l], 0, D) for l in range(L)])
    n2 = ["fq", "fk", "fv", "fl", "mq", "mk", "mv", "cq", "ck", "kr"]
    s2 = [256, 256, 256, 4, 256, 256, 256, 256, 128, 32]
    a2 = dict(zip(n2, np.cumsum([0] + s2[:-1])))
    z2 = dict(zip(n2, s2))
    cols2 = np.concatenate([np.arange(a2[n], a2[n] + z2[n])
                            for n in ("fq", "fk", "mq", "mk", "cq", "ck", "kr", "fl", "fv", "mv")])
    A["win2"] = np.concatenate([np.stack([chunks(I["w_in_2"][l][:, cols2], u * WIN2_N, (u + 1) * WIN2_N)
                                          for u in range(WIN2_U)]) for l in range(L)])
    uq = np.concatenate([np.arange(h * 96, h * 96 + 64) for h in range(8)]
                        + [np.arange(h * 96 + 64, h * 96 + 96) for h in range(8)])
    ukv = np.concatenate([np.arange(h * 128, h * 128 + 64) for h in range(8)]
                         + [np.arange(h * 128 + 64, h * 128 + 128) for h in range(8)])
    A["lat"] = np.stack([np.concatenate([chunks(I["w_uq_2"][l][:, uq], 0, 768),
                                         chunks(I["w_ukv_2"][l][:, ukv], 0, 1024)], 1) for l in range(L)])
    A["ada"] = np.concatenate([I["w_ada_2"][l].reshape(4, 2, 128, ADA_G, ADA_N).transpose(3, 0, 2, 1, 4)
                               .reshape(ADA_G * 4, 128, 2 * ADA_N) for l in range(L)])
    A["b_ada"] = I["b_ada_2"]
    A["g_mix_post"] = I["g_mix_post_2"]
    A["g_ffn_post"] = I["g_ffn_post_2"]
    A["x"] = I["x"][0]
    A["c"] = I["c_2"][0].reshape(8, 128).T
    A["const"] = constants()
    A["tri"] = (np.arange(S)[:, None] <= np.arange(S)[None, :]).astype(f).reshape(2, 128, S).transpose(1, 0, 2).reshape(128, 512)

    small = np.zeros((128, SM_N), f)

    def col(v):
        return v.reshape(-1, 128).T

    def row(v):
        return np.broadcast_to(v.reshape(1, -1), (128, v.size))

    for l in range(L):
        osc = np.concatenate([np.ones(768, f), np.tile(I["diff_out_norm"][l], 4)])
        vals = {"f1": col(I["ffn1_norm"][l]), "mx": col(I["mix_norm"][l]), "f2": col(I["ffn2_norm"][l]),
                "os": col(osc),
                "la": row(np.concatenate([I["diff_lambda_q1"][l], I["diff_lambda_k1"][l],
                                          I["diff_lambda_q2"][l], I["diff_lambda_k2"][l]])),
                "pm": col(I["g_mix_pre_2"][l]), "pf": col(I["g_ffn_pre_2"][l]), "pg": col(I["g_group_2"][l]),
                "pq": col(I["g_q_lat_2"][l]), "pk": col(I["g_kv_lat_2"][l]), "bf": row(I["b_forget_2"][l])}
        for k, v in vals.items():
            o, n = SM_OFF[f"{k}{l}"]
            small[:, o:o + n] = v
    A["small"] = small
    A["gq"] = np.stack([row(np.concatenate([
        np.tile(I["na_q_norm"][l], 4), np.tile(I["na_k_norm"][l], 4), np.tile(I["dil_q_norm"][l], 4),
        np.tile(I["dil_k_norm"][l], 4), np.tile(I["gqa_q_norm"][l], 4), np.tile(I["gqa_k_norm"][l], 2),
        np.tile(I["diff_q_norm"][l], 8), np.tile(I["diff_k_norm"][l], 8)])) for l in range(L)])

    q = np.arange(S)
    r, c = q // 64, q % 64
    start = np.clip(c - 8, 0, 48)
    inside = (c[None, :] >= start[:, None]) & (c[None, :] < start[:, None] + 16)
    ro = r[None, :] - r[:, None] + 7
    co = np.clip(c[None, :] - c[:, None] + 15, 0, 30)
    nab = np.where(inside[None, None], I["na_rel_bias"][:, :, ro, co], f(-BIG))
    A["nab"] = nab.reshape(L, 4, 2, 128, S).transpose(0, 3, 2, 1, 4)
    dist = q[:, None] - q[None, :]
    t5 = I["t5_table_2"].T[:, t5_buckets(np.maximum(dist, 0))]
    t5 = np.where(dist[None] >= 0, t5, f(-BIG))
    A["t5b"] = t5.reshape(4, 2, 128, S).transpose(2, 1, 0, 3)

    nc = _bacc.Bacc("TRN2", target_bir_lowering=False, num_devices=1)
    arrays, d = {}, {}
    for name, a in A.items():
        a = C(a)
        arrays[f"in_{name}"] = a
        d[name] = nc.dram_tensor(f"in_{name}", a.shape, _mybir.dt.from_np(a.dtype), kind="ExternalInput").ap()
    out = nc.dram_tensor("out_x", (S, D), _mybir.dt.float32, kind="ExternalOutput").ap()
    program(nc, d, out)
    res = _run(nc, [arrays], core_ids=[0])
    return res.results[0]["out_x"].reshape(1, S, D)
```

```python
import math
import numpy as np
import concourse.bass as bass
from concourse import mybir
from contextlib import ExitStack

L, D, S, F = 2, 1024, 256, 2816
NF = F // 128
EPS = 1e-6
BIG = 1e30
WIN_U, WIN_N = 8, 352
WIN2_U, WIN2_N = 6, 326
ADA_G, ADA_N = 12, 512
UNIT = 3072
BG, BG2, BG3 = 2, 2, 2
PIECE = 1056
RAW = 6

SMALL = []
for _l in range(L):
    SMALL += [(f"f1{_l}", 8), (f"mx{_l}", 8), (f"f2{_l}", 8), (f"os{_l}", 8), (f"la{_l}", 128),
              (f"pm{_l}", 8), (f"pf{_l}", 8), (f"pg{_l}", 8), (f"pq{_l}", 2), (f"pk{_l}", 1), (f"bf{_l}", 4)]
CONST = [("id", 128), ("pm", 256), ("ln", 512), ("bo", 4),
         ("dfc", 16), ("dfs", 16), ("dlc", 32), ("dls", 32), ("axc", 128), ("axs", 128), ("mlc", 64), ("mls", 64)]


def offsets(table):
    at, out = 0, {}
    for name, n in table:
        out[name] = (at, n)
        at += n
    return out, at


SM_OFF, SM_N = offsets(SMALL)
C_OFF, C_N = offsets(CONST)


class Recorder:

    def activation(self, *a, **k):
        return "activation", a, k

    def tensor_tensor(self, *a, **k):
        return "tensor_tensor", a, k

    def tensor_scalar(self, *a, **k):
        return "tensor_scalar", a, k

    def scalar_tensor_tensor(self, *a, **k):
        return "scalar_tensor_tensor", a, k

    def tensor_reduce(self, *a, **k):
        return "tensor_reduce", a, k

    def tensor_copy(self, *a, **k):
        return "tensor_copy", a, k

    def reciprocal(self, *a, **k):
        return "reciprocal", a, k

    def matmul(self, *a, **k):
        return "matmul", a, k

    def transpose(self, *a, **k):
        return "transpose", a, k

    def dma_start(self, *a, **k):
        return "dma_start", a, k

    def memset(self, *a, **k):
        return "memset", a, k


CALLS = {
    "activation": lambda e, a, k: e.activation(*a, **k),
    "tensor_tensor": lambda e, a, k: e.tensor_tensor(*a, **k),
    "tensor_scalar": lambda e, a, k: e.tensor_scalar(*a, **k),
    "scalar_tensor_tensor": lambda e, a, k: e.scalar_tensor_tensor(*a, **k),
    "tensor_reduce": lambda e, a, k: e.tensor_reduce(*a, **k),
    "tensor_copy": lambda e, a, k: e.tensor_copy(*a, **k),
    "reciprocal": lambda e, a, k: e.reciprocal(*a, **k),
    "matmul": lambda e, a, k: e.matmul(*a, **k),
    "transpose": lambda e, a, k: e.transpose(*a, **k),
    "dma_start": lambda e, a, k: e.dma_start(*a, **k),
    "memset": lambda e, a, k: e.memset(*a, **k),
}
recorder = Recorder()


def program(nc, d, out):
    f32, f32r, i32 = mybir.dt.float32, mybir.dt.float32r, mybir.dt.int32
    ACT, ALU, AX = mybir.ActivationFunctionType, mybir.AluOpType, mybir.AxisListType

    with ExitStack() as ctx:
        def sb(name, shape, dt=f32):
            return ctx.enter_context(nc.sbuf_tensor(name, shape, dt))

        def semaphore(name):
            return ctx.enter_context(nc.semaphore(name))

        X = sb("X", [128, 2, D])
        raw = [sb(f"raw{i}", [128, PIECE]) for i in range(RAW)]
        Wh = [sb(f"Wh{i}", [128, UNIT], f32r) for i in range(2)]
        Wl = [sb(f"Wl{i}", [128, UNIT], f32r) for i in range(2)]
        Hh = sb("Hh", [128, 8, S], f32r)
        Hl = sb("Hl", [128, 8, S], f32r)
        A = sb("A", [128, 2, 1920])
        QTh = sb("QTh", [128, 16, S], f32r)
        QTl = sb("QTl", [128, 16, S], f32r)
        Vh = sb("Vh", [128, 2, D], f32r)
        Vl = sb("Vl", [128, 2, D], f32r)
        BT = sb("BT", [128, 2, 4, S])
        GQ = sb("GQ", [128, 1920])
        G = GQ[:, 0:D]
        WK = sb("WK", [128, 1536])
        NW = sb("NW", [128, 512])
        SB = WK[:, 0:1536].rearrange("p (a b c) -> p a b c", a=3, b=2)
        HT = WK[:, 0:1024].rearrange("p (a b) -> p a b", a=4)
        PTh = sb("PTh", [128, 2, 4, 128], f32r)
        PTl = sb("PTl", [128, 2, 4, 128], f32r)
        ah = [PTh[:, i, 0:2, :].rearrange("p a b -> p (a b)") for i in range(2)]
        al = [PTl[:, i, 0:2, :].rearrange("p a b -> p (a b)") for i in range(2)]
        R = sb("R", [128, S])
        SM = sb("SM", [128, SM_N])
        CT = sb("CT", [128, C_N])
        Ur = sb("Ur", [128, 2, S], f32r)
        oner = sb("oner", [128, 2], f32r)
        lfr = sb("lfr", [128, 2, 8], f32r)
        mhalf = sb("mhalf", [128, 32])
        st = sb("st", [128, 640])
        ada_raw = BT[:, :, :, :].rearrange("p a b c -> p (a b c)").rearrange("p (s n) -> p s n", s=2)
        acc = GQ[:, 0:ADA_N]
        adab = GQ[0:1, ADA_N:2 * ADA_N]
        acch = Vh[:, 0, 0:ADA_N]
        accl = Vl[:, 0, 0:ADA_N]
        mcol = sb("mcol", [128, 4, 8])
        PS = ctx.enter_context(nc.psum_tensor("PS", [128, 8, 512], f32))
        modd = nc.dram_tensor("mod_scratch", (L, 6 * D), f32, kind="Internal").ap()

        def sm(name, a=0, b=None):
            o, n = SM_OFF[name]
            return SM[:, o + a:o + (n if b is None else b)]

        def cn(name, a=0, b=None):
            o, n = C_OFF[name]
            return CT[:, o + a:o + (n if b is None else b)]

        ident = cn("id")

        names = ["pe", "act", "dve", "pool"]
        sems = {n: semaphore("s_" + n) for n in names}
        count = {n: 0 for n in names}
        queue = {n: [] for n in names + ["sp"]}
        waited = {n: {} for n in queue}

        def emit(eng, fn, after, sem, by):
            for key, v in after:
                if waited[eng].get(key, 0) < v:
                    waited[eng][key] = v
                    queue[eng].append((("wait_ge", (key, v), {}), None, 0))
            if sem is None:
                queue[eng].append((fn(recorder), None, 0))
                return None
            count[sem] = count.get(sem, 0) + by
            queue[eng].append((fn(recorder), sem, by))
            return (sem, count[sem])

        def V(fn, *after):
            return emit("dve", fn, after, "dve", 1)

        def AC(fn, *after):
            return emit("act", fn, after, "act", 1)

        def GP(fn, *after):
            return emit("pool", fn, after, "pool", 1)

        def PE(fn, *after, inc=False):
            return emit("pe", fn, after, "pe" if inc else None, 1)

        def DMA(eng, sem, dst, src, *after, slow=False):
            if sem not in sems:
                sems[sem] = semaphore("d_" + sem)
            kw = dict(allow_slow_non_contiguous=True) if slow else {}
            return emit(eng, lambda e: e.dma_start(dst, src, **kw), after, sem, 16)

        free = [() for _ in range(8)]

        units = []

        def ffn_units(k):
            for f in range(NF):
                units.append((d["ffn"][k * NF + f], [(0, 1024), (1024, 2048), (2048, 3072)]))

        def cparts(nch, n):
            cut = [0, 3, 6, 8] if nch == 8 else list(range(nch + 1))
            return [(a * n, b * n) for a, b in zip(cut, cut[1:])]

        for l in range(L):
            ffn_units(2 * l)
            for u in range(WIN_U):
                units.append((d["win"][l * WIN_U + u], cparts(8, WIN_N)))
            for a, b in ((0, 3), (3, 6), (6, 8)):
                units.append((d["wo"][l][:, a * D:b * D], cparts(b - a, D)))
            ffn_units(2 * l + 1)
        for l in range(L):
            for u in range(WIN2_U):
                units.append((d["win2"][l * WIN2_U + u], cparts(8, WIN2_N)))
            units.append((d["lat"][l], [(0, 768), (768, 1536), (1536, 2560)]))
            for a, b in ((0, 3), (3, 6), (6, 8)):
                units.append((d["wo"][L + l][:, a * D:b * D], cparts(b - a, D)))
            ffn_units(4 + l)

        loaded = {}
        ready = {}
        done = {}
        high = {}
        state = {"load": 0, "piece": 0, "high": 0, "cur": 0}

        pieces = [(n, k) for n, u in enumerate(units) for k in range(len(u[1]))]

        def load_next():
            i = state["load"]
            if i >= len(pieces) or (i >= RAW and pieces[i - RAW] not in ready):
                return False
            n, k = pieces[i]
            a, b = units[n][1][k]
            loaded[n, k] = DMA("sp", f"raw{i % RAW}", raw[i % RAW][:, 0:b - a], units[n][0][:, a:b],
                               *(ready[pieces[i - RAW]] if i >= RAW else ()))
            state["load"] += 1
            return True

        def released(n, k):
            if n < 2:
                return ()
            a, b = units[n][1][k]
            got = []
            for j, (pa, pb) in enumerate(units[n - 2][1]):
                if pa < b and a < pb:
                    if (n - 2, j) not in done:
                        return None
                    got.append(done[n - 2, j])
            return got

        def tick_high():
            i = state["high"]
            if i >= len(pieces):
                return False
            while load_next():
                pass
            n, k = pieces[i]
            rel = released(n, k)
            if rel is None:
                return False
            a, b = units[n][1][k]
            r = raw[i % RAW][:, 0:b - a]
            h, lo = Wh[n % 2], Wl[n % 2]
            high[n, k] = (AC(lambda e: e.activation(h[:, a:b], r, ACT.Copy), loaded[n, k], *rel), rel)
            state["high"] += 1
            return True

        def tick():
            i = state["piece"]
            if i >= len(pieces) or (i == state["high"] and not tick_high()):
                return False
            n, k = pieces[i]
            a, b = units[n][1][k]
            r = raw[i % RAW][:, 0:b - a]
            h, lo = Wh[n % 2], Wl[n % 2]
            t1, rel = high[n, k]
            t2 = V(lambda e: e.tensor_tensor(lo[:, a:b], r, h[:, a:b].bitcast(f32), ALU.subtract),
                   loaded[n, k], t1, *rel)
            ready[n, k] = (t1, t2)
            state["piece"] += 1
            while load_next():
                pass
            return True

        ada = {"load": 0, "op": 0, "tok": None, "free": [(), ()], "acc_free": (), "row_free": (), "wait": [], "v_free": (),
               "loaded": {}}
        NADA = L * ADA_G * 4
        mod_written = {0: [], 1: []}

        def ada_load(limit):
            while ada["load"] < min(limit, ada["op"] // 2 + 2):
                u = ada["load"]
                ada["loaded"][u] = DMA("act", f"ada{u % 2}", ada_raw[:, u % 2, :], d["ada"][u], *ada["free"][u % 2])
                ada["load"] += 1

        def ada_tick(limit):
            ada_load(limit)
            u, k = ada["op"] // 2, ada["op"] % 2
            if u >= limit:
                return
            g = u // 4
            c = u % 4 * 2 + k
            if c == 0 and ada["wait"]:
                return
            w = ada_raw[:, u % 2, k * ADA_N:(k + 1) * ADA_N]
            if c == 0:
                t = V(lambda e: e.tensor_scalar(acc, w, cact[:, 0:1], None, ALU.mult),
                      ada["loaded"][u], cact_tok, *ada["acc_free"])
            else:
                t = V(lambda e: e.scalar_tensor_tensor(out=acc, in0=w, scalar=cact[:, c:c + 1], in1=acc,
                                                       op0=ALU.mult, op1=ALU.add), ada["loaded"][u], ada["tok"])
            ada["tok"] = t
            ada["op"] += 1
            if k == 1:
                ada["free"][u % 2] = (t,)
            if c == 7:
                t1 = AC(lambda e: e.activation(acch, acc, ACT.Copy), t, *ada["acc_free"], *ada["v_free"])
                t2 = V(lambda e: e.tensor_tensor(accl, acc, acch.bitcast(f32), ALU.subtract), t1)
                ada["wait"].append((g, (t1, t2)))

        def need(n, k):
            while (n, k) not in ready:
                assert tick(), (n, k, state)
            return ready[n, k]

        def next_unit():
            state["cur"] += 1
            return state["cur"] - 1

        def ada_finish(bank):
            if not ada["wait"]:
                return
            g, t = ada["wait"].pop()
            l, g = g // ADA_G, g % ADA_G
            cols = slice(g * ADA_N, (g + 1) * ADA_N)
            tb = DMA("act", "adab", adab, d["b_ada"][l:l + 1, cols], *ada["row_free"])
            PE(lambda e: e.matmul(PS[:, bank, 0:ADA_N], oner[:, 0:1].to_broadcast([128, 128]), acch, start=True,
                                  stop=False), *t, t_one, *free[bank])
            tp = PE(lambda e: e.matmul(PS[:, bank, 0:ADA_N], oner[:, 0:1].to_broadcast([128, 128]), accl, start=False,
                                       stop=True), inc=True)
            tv = V(lambda e: e.tensor_tensor(adab, PS[0:1, bank, 0:ADA_N], adab, ALU.add), tp, tb)
            to = DMA("sp", "mod", modd[l:l + 1, cols], adab, tv)
            free[bank] = (tv,)
            ada["acc_free"], ada["row_free"] = (tp,), (to,)
            mod_written[l].append(to)

        tx = [DMA("act", f"x{t}", X[:, t, :], d["x"][t * 128:t * 128 + 128, :]) for t in range(2)]
        tid = DMA("sp", "id", CT[:, 0:128], d["const"][:, 0:128])
        tsm = DMA("sp", "sm", SM[:, :], d["small"])
        for _ in range(RAW):
            load_next()
        tc = DMA("act", "ct", CT[:, 128:C_N], d["const"][:, 128:C_N])
        tcc = DMA("act", "cc", st[:, 0:8], d["c"])
        tu = DMA("act", "u", A[:, 0, 1408:1920], d["tri"])
        t_u = AC(lambda e: e.activation(Ur[:, :, :], A[:, 0, 1408:1920].rearrange("p (c q) -> p c q", c=2), ACT.Copy), tu)
        t = V(lambda e: e.memset(st[:, 8:10], 1.0))
        t_one = AC(lambda e: e.activation(oner[:, :], st[:, 8:10], ACT.Copy), t)
        tmh = GP(lambda e: e.memset(mhalf[:, :], -0.5))
        cact = sb("cact", [128, 8])
        t = AC(lambda e: e.activation(cact[:, :], st[:, 0:8], ACT.Silu), tcc)
        cact_tok = t

        SS, RS, NM, Z, ZR, LA, LF, FQ, NT = 16, 80, 144, 160, 240, 320, 330, 400, 512

        def rstd(a, b, n, *after, mul=None):
            s, r = st[:, SS + a:SS + b], st[:, RS + a:RS + b]
            t = GP(lambda e: e.tensor_scalar(s, s, 1.0 / n, EPS, ALU.mult, ALU.add), *after)
            t = GP(lambda e: e.tensor_tensor(r, s, mhalf[:, 0:b - a], ALU.pow), t, tmh)
            if mul is not None:
                t = GP(lambda e: e.tensor_scalar(r, r, mul, None, ALU.mult), t)
            return t

        def rstd_v(a, b, n, *after, mul=None):
            s, r, w = st[:, SS + a:SS + b], st[:, RS + a:RS + b], st[:, NT:NT + b - a]
            t = V(lambda e: e.tensor_scalar(s, s, 1.0 / n, EPS, ALU.mult, ALU.add), *after)
            t = V(lambda e: e.tensor_scalar(w.bitcast(i32), s.bitcast(i32), 1, None, ALU.logical_shift_right), t)
            t = V(lambda e: e.tensor_scalar(r.bitcast(i32), w.bitcast(i32), -1.0, 1597463007.0, ALU.mult, ALU.add), t)
            for _ in range(3):
                t = V(lambda e: e.tensor_tensor(w, r, r, ALU.mult), t)
                t = V(lambda e: e.scalar_tensor_tensor(out=w, in0=w, scalar=-0.5, in1=s, op0=ALU.mult, op1=ALU.mult), t)
                t = V(lambda e: e.scalar_tensor_tensor(out=r, in0=w, scalar=1.5, in1=r, op0=ALU.add, op1=ALU.mult), t)
            if mul is not None:
                t = V(lambda e: e.tensor_scalar(r, r, mul, None, ALU.mult), t)
            return t

        def to_T(src, cols, scale, after, shift=None, row=None, dst0=0, before=None):
            got, tps = [], {}
            n = len(cols)

            def turn(j, ts=(0, 1)):
                b = 4 + (j // 2) % 4
                for i in range(j, min(j + 2, n)):
                    for t in ts:
                        tps[j] = PE(lambda e: e.transpose(
                            PS[:, b, (i % 2) * S + t * 128:(i % 2) * S + t * 128 + 128],
                            src[:, t, cols[i]:cols[i] + 128], ident), tid, *after(i, t), *free[b], inc=True)

            if before is not None:
                for t in range(2):
                    for j in range(0, n, 2):
                        turn(j, (t,))
                    row_tok = (before(t),)
            else:
                row_tok = ()
            late = []

            def flush():
                while late:
                    t2, fn, key = late.pop(0)
                    t3 = V(fn, t2)
                    d["_ht_free"][key] = (t3,)
                    got.append((t2, t3))

            for j in range(0, n, 2):
                if j not in tps:
                    turn(j)
                b = 4 + (j // 2) % 4
                for i in range(j, min(j + 2, n)):
                    p = PS[:, b, (i % 2) * S:(i % 2) * S + S]
                    ht, hh, hl = HT[:, i % 4, :], Hh[:, dst0 + i, :], Hl[:, dst0 + i, :]
                    sc = scale[:, i:i + 1]
                    w = [tps[j], *d["_ht_free"][i % 4], *d["_h_free"], *d["_colw"], *row_tok]
                    if row is None:
                        t1 = V(lambda e: e.tensor_scalar(ht, p, sc, None, ALU.mult), *w)
                    else:
                        t1 = V(lambda e: e.scalar_tensor_tensor(out=ht, in0=p, scalar=sc, in1=row, op0=ALU.mult,
                                                                op1=ALU.mult), *w)
                    flush()
                    if shift is None:
                        t2 = AC(lambda e: e.activation(hh, ht, ACT.Copy), t1, *d["_h_free"])
                        late.append((t2, lambda e, hl=hl, ht=ht, hh=hh: e.tensor_tensor(
                            hl, ht, hh.bitcast(f32), ALU.subtract), i % 4))
                    else:
                        sh = shift[:, i:i + 1]
                        t2 = AC(lambda e: e.activation(hh, ht, ACT.Identity, bias=sh), t1, *d["_h_free"], *d["_colw"])
                        late.append((t2, lambda e, hl=hl, ht=ht, hh=hh, sh=sh: e.scalar_tensor_tensor(
                            out=hl, in0=ht, scalar=sh, in1=hh.bitcast(f32), op0=ALU.add, op1=ALU.subtract), i % 4))
                free[b] = (t1,)
            flush()
            return got

        d["_ht_free"] = [(), (), (), ()]
        d["_h_free"] = ()
        d["_colw"] = (tsm,)
        x_tok = [(tx[0],), (tx[1],)]
        a_free = [(t_u,)]

        def norm_T(scale, shift=None):
            rs = []
            for t in range(2):
                q = AC(lambda e: e.activation(A[:, t, 0:D], X[:, t, :], ACT.Square,
                                              accum_out=st[:, SS + t:SS + t + 1]),
                       *x_tok[t], *a_free[0], *d.get("_rs_free", ()))
                rs.append(rstd(t, t + 1, D, q))
                a_free[0] = (*a_free[0], q)
            for _ in range(3):
                tick()

            def spread(t):
                tp = PE(lambda e: e.matmul(PS[:, 0, t * 128:t * 128 + 128],
                                           st[:, RS + t:RS + t + 1].to_broadcast([128, 128]), ident,
                                           start=True, stop=True), rs[t], tid, *free[0], inc=True)
                if t == 0:
                    return None
                tr = AC(lambda e: e.activation(R[:, :], PS[:, 0, 0:S], ACT.Copy), tp)
                free[0] = (tr,)
                d["_rs_free"] = (tp,)
                return tr

            return to_T(X, [128 * c for c in range(8)], scale, lambda i, t: x_tok[t], shift, R[:, :], before=spread)

        def three(out_, xh, xl, wh, wl, first, last, *after, inc=False):
            PE(lambda e: e.matmul(out_, xh, wh, start=first, stop=False), *after)
            PE(lambda e: e.matmul(out_, xh, wl, start=False, stop=False))
            return PE(lambda e: e.matmul(out_, xl, wh, start=False, stop=last), inc=inc)

        def threeT(out_, xh, xl, wh, wl, first, last, *after, inc=False):
            PE(lambda e: e.matmul(out_, wh, xh, start=first, stop=False), *after)
            PE(lambda e: e.matmul(out_, wh, xl, start=False, stop=False))
            return PE(lambda e: e.matmul(out_, wl, xh, start=False, stop=last), inc=inc)

        def ffn(h_tok, ada_to=0, beside=None):
            sgt = SB[:, :, 0, :]
            att = SB[:, :, 1, :]
            silu_free = [d["_sb_free"], d["_sb_free"]]
            a_rel = d["_a_rel"]
            pend = None

            def down(f, n, s, tk):
                w = need(n, 2)
                h, lo = Wh[n % 2], Wl[n % 2]
                for t in range(2):
                    for j in range(2):
                        c = slice(2048 + 512 * j, 2560 + 512 * j)
                        tt = three(PS[:, 2 * t + j, :], ah[s][:, t * 128:t * 128 + 128], al[s][:, t * 128:t * 128 + 128],
                                   h[:, c], lo[:, c], f == 0, f == NF - 1, *w, *tk,
                                   *(free[2 * t + j] if f == 0 else ()), inc=(t == 1 and j == 1) or f == NF - 1)
                        if f == NF - 1:
                            last[2 * t + j] = tt
                done[n, 2] = tt
                a_rel[s] = (tt,)

            last = {}
            for f in range(NF):
                n = next_unit()
                b = 4 + f % 2
                s = f % 2
                h, lo = Wh[n % 2], Wl[n % 2]
                for m in range(2):
                    w = need(n, m)
                    for c in range(8):
                        cc = slice(m * 1024 + c * 128, m * 1024 + c * 128 + 128)
                        tp = threeT(PS[:, b, m * S:m * S + S], Hh[:, c, :], Hl[:, c, :], h[:, cc], lo[:, cc],
                                    c == 0, c == 7, *w, *h_tok[c], *(free[b] if c == 0 and m == 0 else ()), inc=c == 7)
                    done[n, m] = tp
                    if m == 0:
                        tg = tp
                        need(n, 1)
                ada_finish(7)
                need(n, 2)
                tick()
                ada_tick(ada_to)
                tick()
                ts = AC(lambda e: e.activation(sgt[:, s, :], PS[:, b, 0:S], ACT.Silu), tp, *silu_free[s])
                tm = V(lambda e, s=s: e.tensor_tensor(att[:, s, :], sgt[:, s, :], PS[:, b, S:2 * S], ALU.mult), ts, tp,
                       *silu_free[s])
                free[b] = (ts, tm)
                t1 = AC(lambda e, s=s: e.activation(ah[s], att[:, s, :], ACT.Copy), tm, *a_rel[s])
                t2 = V(lambda e, s=s: e.tensor_tensor(al[s], att[:, s, :], ah[s].bitcast(f32), ALU.subtract),
                       t1, *a_rel[s])
                silu_free[s] = (t2,)
                ada_tick(ada_to)
                if pend is not None:
                    down(*pend)
                tick()
                ada_tick(ada_to)
                if f == 6 and beside is not None:
                    beside()
                pend = (f, n, s, (t1, t2))
                d["_h_free"] = (tp,)
            tick()
            for _ in range(3):
                tick_high()
            down(*pend)
            while ada["op"] < 2 * ada_to:
                ada_finish(7)
                ada_tick(ada_to)
            ada_finish(7)
            d["_sb_free"] = silu_free[0] + silu_free[1]
            return last

        d["_a_rel"] = [(), ()]
        d["_sb_free"] = ()

        def residual(last, scale):
            for t in range(2):
                tt = []
                for j in range(2):
                    xs = X[:, t, j * 512:j * 512 + 512]
                    v = V(lambda e, xs=xs, t=t, j=j: e.scalar_tensor_tensor(
                        out=xs, in0=PS[:, 2 * t + j, :], scalar=scale, in1=xs, op0=ALU.mult, op1=ALU.add),
                        last[2 * t + j], *x_tok[t])
                    free[2 * t + j] = (v,)
                    tt.append(v)
                x_tok[t] = tuple(tt)

        def post_norm(last, g_tok):
            for t in range(2):
                q = AC(lambda e, t=t: e.activation(A[:, t, 0:D].rearrange("p (j n) -> p j n", j=2),
                                                   PS[:, 2 * t:2 * t + 2, :], ACT.Square,
                                                   accum_out=st[:, SS + t:SS + t + 1]),
                       last[2 * t], last[2 * t + 1], *a_free[0], *d["_rs_free"])
                r = rstd(t, t + 1, D, q)
                if t == 0:
                    tick()
                v = V(lambda e, t=t: e.scalar_tensor_tensor(
                    out=A[:, t, 0:D].rearrange("p (j n) -> p j n", j=2), in0=PS[:, 2 * t:2 * t + 2, :],
                    scalar=st[:, RS + t:RS + t + 1], in1=G.rearrange("p (j n) -> p j n", j=2),
                    op0=ALU.mult, op1=ALU.mult), r, q, g_tok["g"])
                free[2 * t] = free[2 * t + 1] = (v,)
                v2 = V(lambda e, t=t: e.tensor_tensor(X[:, t, :], X[:, t, :], A[:, t, 0:D], ALU.add), v, *x_tok[t])
                x_tok[t] = (v2,)
            d["_rs_free"] = (v,)
            d["_g_free"] = (v,)
            d["_gq_free"] = (v,)
            a_free[0] = (v2,)

        bg = []

        def background(k):
            while bg and k > 0:
                if bg[0] is None:
                    bg.pop(0)
                    return
                w, fn = bg.pop(0)
                fn()
                k -= w

        def background_all():
            while bg:
                background(1)

        def project(h_tok, nunits, ncol, segs, hook, bank, work):
            got = []
            for u in range(nunits):
                n = next_unit()
                h, lo = Wh[n % 2], Wl[n % 2]
                c0, c1 = u * ncol, (u + 1) * ncol
                toks = []
                for t in range(2):
                    b = bank(u, t)
                    for c in range(8):
                        k = min(c // 3, 2)
                        w = need(n, k)
                        cc = slice(c * ncol, (c + 1) * ncol)
                        ts = slice(t * 128, t * 128 + 128)
                        tp = three(PS[:, b, 0:ncol], Hh[:, c, ts], Hl[:, c, ts], h[:, cc], lo[:, cc], c == 0, c == 7,
                                   *w, *h_tok[c], *(free[b] if c == 0 else ()), inc=c in (2, 5, 7))
                        if t == 1 and c in (2, 5, 7):
                            done[n, k] = tp
                    own, lows = [], []
                    for a, z_, kind, to in segs:
                        a_, z_ = max(a, c0), min(z_, c1)
                        if a_ >= z_:
                            continue
                        src = PS[:, b, a_ - c0:z_ - c0]
                        ds = slice(to + a_ - a, to + z_ - a)
                        if kind == "A":
                            own.append(AC(lambda e: e.activation(A[:, t, ds], src, ACT.Copy), tp, *a_free[0]))
                        else:
                            own.append(AC(lambda e: e.activation(Vh[:, t, ds], src, ACT.Copy), tp, *d["_v_free"]))
                            lows.append((ds, src))
                    for ds, src in lows:
                        own.append(V(lambda e: e.tensor_tensor(Vl[:, t, ds], src, Vh[:, t, ds].bitcast(f32),
                                                               ALU.subtract), own[-1]))
                    free[b] = tuple(own)
                    toks += own
                    for _ in range(2 - t):
                        if pieces[state["piece"]][0] <= n + nunits - 1 - u:
                            tick()
                    if t == 1:
                        got.append(tuple(toks))
                        hook(u, got)
                    work()
            d["_h_free"] = (tp,)
            return got

        def out_proj(h_tok, at=None):
            last = {}
            for a, b2 in ((0, 3), (3, 6), (6, 8)):
                n = next_unit()
                h, lo = Wh[n % 2], Wl[n % 2]
                for c in range(a, b2):
                    if at and c in at:
                        at[c]()
                    w = need(n, c - a)
                    for t in range(2):
                        for j in range(2):
                            cc = slice((c - a) * D + j * 512, (c - a) * D + j * 512 + 512)
                            ts = slice(t * 128, t * 128 + 128)
                            tp = three(PS[:, 2 * t + j, :], Hh[:, c, ts], Hl[:, c, ts], h[:, cc], lo[:, cc],
                                       c == 0, c == 7, *w, *h_tok[c], *(free[2 * t + j] if c == 0 else ()),
                                       inc=c == 7 or (t == 1 and j == 1))
                            if c == 7:
                                last[2 * t + j] = tp
                    done[n, c - a] = tp
                    if c < 6:
                        tick()
            d["_h_free"] = (tp,)
            return last

        def transposes(jobs, after, banks):
            got = {}
            for i0 in range(0, len(jobs), 2):
                b = banks[(i0 // 2) % len(banks)]
                grp = jobs[i0:i0 + 2]
                for k, (src, blk, m) in enumerate(grp):
                    for t in range(2):
                        tp = PE(lambda e, k=k, t=t, src=src, m=m: e.transpose(
                            PS[0:m, b, k * S + t * 128:k * S + t * 128 + 128], src(t), ident),
                            tid, *after, *free[b], inc=True)
                blk0, m = grp[0][1], grp[0][2]
                g = len(grp)
                assert all(q[1] == blk0 + k and q[2] == m for k, q in enumerate(grp))
                th, tl = (QTh, QTl) if blk0 < 16 else (Hh, Hl)
                o = blk0 % 16
                src = PS[0:m, b, 0:g * S].rearrange("p (k s) -> p k s", k=g)
                t1 = AC(lambda e: e.activation(th[0:m, o:o + g, :], src, ACT.Copy), tp, *d["_qt_free"])
                t2 = V(lambda e: e.tensor_tensor(tl[0:m, o:o + g, :], src, th[0:m, o:o + g, :].bitcast(f32),
                                                 ALU.subtract), t1, *d["_qt_free"])
                free[b] = (t2,)
                for k in range(g):
                    got[blk0 + k] = t2
            return got

        def qk_parts(rows, blk, cols):
            th, tl = (QTh, QTl) if blk < 16 else (Hh, Hl)
            return th[rows, blk % 16, cols], tl[rows, blk % 16, cols]

        def rope(xs, cs, ss, h, ta, tb, *after, dst=None):
            t1 = V(lambda e: e.tensor_tensor(ta, xs, cs, ALU.mult), *after)
            t2 = V(lambda e: e.tensor_tensor(tb[..., 0:h], xs[..., h:2 * h], ss[..., 0:h], ALU.mult), *after)
            t3 = V(lambda e: e.tensor_tensor(tb[..., h:2 * h], xs[..., 0:h], ss[..., h:2 * h], ALU.mult), *after)
            dst = xs if dst is None else dst
            return V(lambda e: e.tensor_tensor(dst, ta, tb, ALU.add), t1, t2, t3)

        OT = A[:, :, 0:D].rearrange("p t (c q) -> p t c q", q=128)

        def attention(items):
            n = len(items)
            score, probs, ptoks, unit = {}, {}, {}, {}
            u = 0
            for i, it in enumerate(items):
                unit[i] = u
                if it["part"] != "first":
                    u += 1
            sb_free = [(*d["_sb_free"], *(x for y in d["_ht_free"] for x in y))] * 3
            pt_free = [(), ()]
            outs = {}

            def stage_s(i):
                it = items[i]
                nk = it["nk"]
                b = 1 + 2 * (i % 2)
                for j in range(3):
                    for k, ((qh, ql), (kh, kl)) in enumerate(it["heads"]):
                        w = (*it["after"](), *free[b + k]) if j == 0 else ()
                        tp = PE(lambda e: e.matmul(PS[:, b + k, 0:nk], ql if j == 2 else qh, kl if j == 1 else kh,
                                                   start=j == 0, stop=j == 2), *w, inc=j == 2 and k == 1)
                score[i] = tp

            def stage_a(i):
                it = items[i]
                nk, s = it["nk"], i % 3
                b = 1 + 2 * (i % 2)
                tp = score[i]
                src = PS[:, b:b + 2, 0:nk]
                nm = st[:, NM + 2 * s:NM + 2 * s + 2]
                if it["bias"] is not None:
                    dst = SB[:, s, :, 0:nk]
                    tb = V(lambda e: e.scalar_tensor_tensor(out=dst, in0=src, scalar=it["scale"], in1=it["bias"],
                                                            op0=ALU.mult, op1=it["op"]), tp, *sb_free[s], *it["after"]())
                    free[b] = free[b + 1] = (tb,)
                    tm = V(lambda e: e.tensor_reduce(nm, dst, AX.X, ALU.max, negate=True), tb)
                    src, sc = dst, 1.0
                else:
                    tb = tp
                    tm = V(lambda e: e.tensor_reduce(nm, src, AX.X, ALU.max, negate=True), tp, *sb_free[s])
                    tm = V(lambda e: e.tensor_scalar(nm, nm, it["scale"], None, ALU.mult), tm)
                    sc = it["scale"]
                score[i] = (src, sc, nm, tb, tm, b)

            def stage_e(i):
                it = items[i]
                nk, s = it["nk"], i % 3
                src, sc, nm, tb, tm, b = score[i]
                for k in range(2):
                    te = AC(lambda e: e.activation(SB[:, s, k, 0:nk], src[:, k, :], ACT.Exp, bias=nm[:, k:k + 1], scale=sc,
                                                   accum_out=st[:, Z + 2 * i + k:Z + 2 * i + k + 1]),
                            tb, tm, *sb_free[s], *d["_z_free"])
                if it["bias"] is None:
                    free[b] = free[b + 1] = (te, tm)
                probs[i] = te

            def stage_n(i):
                it = items[i]
                nk, s = it["nk"], i % 3
                zr = st[:, ZR + 2 * i:ZR + 2 * i + 2]
                p0, p1 = SB[:, s, 0, 0:nk], SB[:, s, 1, 0:nk]
                t = V(lambda e: e.reciprocal(zr, st[:, Z + 2 * i:Z + 2 * i + 2]), probs[i], *d["_z_free"])
                if it["part"] == "pair":
                    t = (GP(lambda e: e.tensor_scalar(p0, p0, zr[:, 0:1], None, ALU.mult), t),
                         V(lambda e: e.tensor_scalar(p1, p1, zr[:, 1:2], None, ALU.mult), t))
                else:
                    t = V(lambda e: e.tensor_tensor(zr[:, 1:2], zr[:, 1:2], st[:, LA:LA + 1], ALU.mult), t, it["lam"])
                    t = V(lambda e: e.tensor_scalar(p1, p1, zr[:, 1:2], None, ALU.mult), t)
                    t = V(lambda e: e.scalar_tensor_tensor(out=p0, in0=p0, scalar=zr[:, 0:1], in1=p1,
                                                           op0=ALU.mult, op1=ALU.add), t)
                    t = (t,)
                ptoks[i] = t

            def stage_b(i):
                it = items[i]
                nk, s, s3 = it["nk"], unit[i] % 2, i % 3
                nc_ = nk // 128
                b = 5 + s
                for k in {"pair": (0, 1), "first": (0,), "last": (1,)}[it["part"]]:
                    for c in range(nc_):
                        col = (2 * c + k) * 128
                        half = k if it["part"] == "pair" else 0
                        tp = PE(lambda e: e.transpose(PS[:, b, col:col + 128], SB[:, s3, half, c * 128:c * 128 + 128],
                                                      ident), *ptoks[i], *free[b], inc=True)
                sb_free[s3] = (tp,)
                if it["part"] == "first":
                    return
                w = 2 * nc_ * 128
                src = PS[:, b, 0:w]
                ph, pl = PTh[:, s, :, :].rearrange("p a b -> p (a b)")[:, 0:w], PTl[:, s, :, :].rearrange("p a b -> p (a b)")[:, 0:w]
                t1 = AC(lambda e: e.activation(ph, src, ACT.Copy), tp, *pt_free[s])
                te = V(lambda e: e.tensor_tensor(pl, src, ph.bitcast(f32), ALU.subtract), t1, *pt_free[s])
                free[b] = (te,)
                ptoks["u", i] = te

            def stage_c(i):
                it = items[i]
                if it["part"] == "first":
                    return
                nk, s, t, ch = it["nk"], unit[i] % 2, it["t"], it["chunk"]
                nc_ = nk // 128
                b = 7
                ph, pl = PTh[:, s, :, :].rearrange("p a b -> p (a b)"), PTl[:, s, :, :].rearrange("p a b -> p (a b)")
                for c in range(nc_):
                    m = slice(c * S, c * S + S)
                    tp = threeT(PS[:, b, 0:S], ph[:, m], pl[:, m], *it["v"][c], c == 0, c == nc_ - 1,
                                ptoks["u", i], *it["after"](), *free[b], inc=c == nc_ - 1)
                pt_free[s] = (tp,)
                got = []
                for k in range(2):
                    rows = slice(64 * k, 64 * k + 64)
                    src = PS[rows, b, k * 128:k * 128 + 128]
                    if it["direct"]:
                        hh = Hh[rows, ch, t * 128:t * 128 + 128]
                        hl = Hl[rows, ch, t * 128:t * 128 + 128]
                        t1 = AC(lambda e: e.activation(hh, src, ACT.Copy), tp, *d["_h_free"])
                        got.append(V(lambda e: e.tensor_tensor(hl, src, hh.bitcast(f32), ALU.subtract), t1,
                                     *d["_h_free"]))
                    elif k == 0:
                        got.append(AC(lambda e: e.activation(OT[rows, t, ch, :], src, ACT.Copy), tp, *it["ofree"]()))
                    else:
                        got.append(V(lambda e: e.tensor_copy(OT[rows, t, ch, :], src), tp, *it["ofree"]()))
                free[b] = tuple(got)
                outs[ch, t] = tuple(got)
                if it.get("done") is not None:
                    it["done"](ch, t, outs)

            at = {"i": -1}

            def step():
                i = at["i"]
                if i + 1 < n and not items[i + 1]["ready"]():
                    return False
                at["i"] += 1
                if 0 <= i < n:
                    stage_a(i)
                if 0 <= i - 1 < n:
                    stage_n(i - 1)
                if 0 <= i - 2 < n:
                    stage_b(i - 2)
                if 0 <= i < n:
                    stage_e(i)
                if 0 <= i - 3 < n:
                    stage_c(i - 3)
                if i + 1 < n:
                    stage_s(i + 1)
                return True

            def finish(work=lambda: None):
                while at["i"] < n + 3:
                    work()
                    if step() and at["i"] % 3 == 0:
                        tick()
                every = tuple(x for o in outs.values() for x in o)
                last = (*outs[items[-1]["chunk"], items[-1]["t"]], *outs[items[-2]["chunk"], items[-2]["t"]])
                d["_sb_free"] = every
                d["_qt_free"] = d["_v_free"] = ada["v_free"] = last
                d["_z_free"] = last
                return outs, every

            return step, finish

        def chunk_scaled(ch, row, scale, *after):
            ht = HT[:, ch % 4, :].rearrange("p (t q) -> p t q", t=2)
            t1 = V(lambda e: e.scalar_tensor_tensor(out=ht, in0=row, scalar=scale, in1=OT[:, :, ch, :],
                                                    op0=ALU.mult, op1=ALU.mult),
                   *after, *d["_ht_free"][ch % 4], *d["_sb_free"])
            hh, hl = Hh[:, ch, :], Hl[:, ch, :]
            hf = HT[:, ch % 4, :]
            t2 = AC(lambda e: e.activation(hh, hf, ACT.Copy), t1, *d["_h_free"])

            def rest():
                t3 = V(lambda e: e.tensor_tensor(hl, hf, hh.bitcast(f32), ALU.subtract), t2, *d["_h_free"])
                d["_ht_free"][ch % 4] = (t3,)
                return (t2, t3)

            return rest, t1

        d["_z_free"] = d["_v_free"] = d["_nw_free"] = ()
        d["_qt_free"] = ()
        d["_rs_free"] = ()
        d["_g_free"] = ()
        d["_bt_free"] = ()
        d["_gq_free"] = ()

        def bc(ap, shape):
            return ap.to_broadcast(shape)

        def first_mixer(l):
            tbt = DMA("sp", "bt", BT[:, :, :, :], d["nab"][l], *d["_bt_free"], *ada["free"][0], *ada["free"][1])
            tgq = DMA("sp", "gq", GQ[:, :], d["gq"][l], *d["_gq_free"], *ada["acc_free"], *ada["row_free"])
            lam_init = 0.8 - 0.6 * math.exp(-0.3 * l)
            la = sm(f"la{l}")
            lt = st[:, FQ + 32:FQ + 96].rearrange("p (a n) -> p a n", a=2)
            t = V(lambda e: e.tensor_tensor(lt, la.rearrange("p (a b n) -> p a b n", a=2, b=2)[:, :, 0, :],
                                            la.rearrange("p (a b n) -> p a b n", a=2, b=2)[:, :, 1, :], ALU.mult),
                  tsm, *d["_z_free"])
            t = V(lambda e: e.tensor_reduce(st[:, LA:LA + 2], lt, AX.X, ALU.add), t)
            h_tok = norm_T(sm(f"mx{l}"))
            t = AC(lambda e: e.activation(st[:, LA + 2:LA + 4], st[:, LA:LA + 2], ACT.Exp), t)
            t = V(lambda e: e.tensor_scalar(st[:, LA + 3:LA + 4], st[:, LA + 3:LA + 4], -lam_init, None, ALU.add), t)
            lam_tok = V(lambda e: e.tensor_tensor(st[:, LA:LA + 1], st[:, LA + 3:LA + 4], st[:, LA + 2:LA + 3],
                                                  ALU.subtract), t)
            groups = {1: (0, 8, 64), 3: (512, 8, 64), 5: (1024, 6, 64), 7: (1408, 16, 32)}
            blocks = {1: range(0, 4), 3: range(4, 8), 5: range(8, 11), 7: range(11, 15)}
            fin, tk, vt = {}, {}, []

            def norms(u, got):
                vt[:] = [x for p in got for x in p]
                if u < WIN_U - 1:
                    units_done[0] = u
                if u in groups:
                    bg.extend(norm_steps(u, list(vt)))

            def norm_steps(u, dep):
                c0, nh, n = groups[u]
                q = A[:, :, c0:c0 + nh * n].rearrange("p t (h n) -> p t h n", n=n)
                s_ = NW[:, 0:nh * n].rearrange("p (h n) -> p h n", h=nh)
                gb = GQ[:, c0:c0 + nh * n].rearrange("p (h n) -> p h n", n=n)
                ss = st[:, SS:SS + 2 * nh].rearrange("p (t h) -> p t h", t=2)
                rs = st[:, RS:RS + 2 * nh].rearrange("p (t h) -> p t h", t=2)
                box = {"t": None}

                def sums(t_):
                    t = AC(lambda e: e.activation(s_, q[:, t_], ACT.Square), *dep, *d["_nw_free"])
                    t = V(lambda e: e.tensor_reduce(ss[:, t_], s_, AX.X, ALU.add), t, *d["_rs_free"])
                    d["_nw_free"] = (t,)
                    box["t"] = t

                def root():
                    box["t"] = rstd_v(0, 2 * nh, n, box["t"])

                def scaled(t_):
                    v = V(lambda e: e.tensor_tensor(q[:, t_], q[:, t_],
                                                    rs[:, t_].unsqueeze(2).to_broadcast([128, nh, n]), ALU.mult),
                          box["t"])
                    d["_rs_free"] = (v,)
                    box[t_] = v

                def gained(t_):
                    fin[u, t_] = GP(lambda e: e.tensor_tensor(q[:, t_], q[:, t_], gb, ALU.mult), box[t_], tgq)

                return [(1, lambda: sums(0)), (1, lambda: sums(1)), (3, root), (1, lambda: scaled(0)),
                        (0, lambda: gained(0)), (1, lambda: scaled(1)), (0, lambda: gained(1)), *rope_steps(u),
                        None, *turn_steps(u)]

            def turn_steps(u):
                jobs = [(lambda t, c=c: A[:, t, c * 128:c * 128 + 128], c, 128) for c in blocks[u]]
                return [(1, lambda i=i: tk.update(transposes(jobs[i:i + 2], (fin[u, 0], fin[u, 1]), (5 + i // 2 % 2,))))
                        for i in range(0, len(jobs), 2)]

            ta, tb = NW[:, 0:256], NW[:, 256:512]

            def rope_steps(u):
                steps = []
                for t_ in range(2):
                    if u == 1:
                        continue
                    if u == 3:
                        jobs = [(A[:, t_, 512:1024].rearrange("p (h n) -> p h n", n=64)[:, :, 0:16], "dl", t_ * 16, 8, 16)]
                    elif u == 5:
                        jobs = []
                        for y in range(2):
                            jobs.append((A[:, t_, 1024:1408].rearrange("p (h y n) -> p h y n", y=2, n=32)[:, :, y, :],
                                         "ax", t_ * 64 + y * 32, 6, 32))
                    else:
                        jobs = [(A[:, t_, 1408:1920].rearrange("p (h n) -> p h n", n=32)[:, :, 0:8], "df", t_ * 8, 16, 8)]
                    for job in jobs:
                        steps.append((1.5, lambda t_=t_, job=job: rope_step(u, t_, *job)))
                return steps

            def rope_step(u, t_, xs, nm, o, nh, n):
                cs = bc(cn(nm + "c", o, o + n).unsqueeze(1), [128, nh, n])
                s_ = bc(cn(nm + "s", o, o + n).unsqueeze(1), [128, nh, n])
                r = rope(xs, cs, s_, n // 2, ta[:, 0:nh * n].rearrange("p (h n) -> p h n", n=n),
                         tb[:, 0:nh * n].rearrange("p (h n) -> p h n", n=n), fin[u, t_], tc, *d["_nw_free"])
                fin[u, t_] = r
                d["_nw_free"] = (r,)

            VN, VD, VG, VF = 0, 256, 512, 640
            items = []
            units_done = [-1]
            split, chunk_tok, box_outs = [], {}, {}

            def placed(ch, t, outs):
                if ch < 4 and (ch, 0) in outs and (ch, 1) in outs:
                    split.append(ch)
                    box_outs[ch] = (*outs[ch, 0], *outs[ch, 1])

            def item(t, heads, bias, op, chunk, scale, blocks, v0, part="pair", extra=()):
                unit = {0: 2, 1: 2, 2: 4, 3: 4, 4: 7, 5: 7, 6: 7, 7: 7}[chunk]
                own = range(0, 4) if chunk < 2 else range(0, 8)
                items.append(dict(t=t, nk=S, heads=heads, bias=bias, op=op, chunk=chunk, scale=scale, part=part,
                                  lam=lam_tok, direct=chunk in (4, 5),
                                  ready=lambda: units_done[0] >= unit and all(b in tk for b in blocks),
                                  after=lambda: (*(tk[b] for b in blocks), *vt, *extra),
                                  ofree=lambda: tuple(tk[b] for b in own), done=placed,
                                  v=[(Vh[:, c, v0:v0 + 128], Vl[:, c, v0:v0 + 128]) for c in range(2)]))

            al_ = slice(0, S)
            halves = [(t, slice(t * 128, t * 128 + 128)) for t in range(2)]
            half = [slice(64 * k, 64 * k + 64) for k in range(2)]
            for t, q_ in halves:
                for p in range(2):
                    hs = [(qk_parts(half[k], p, q_), qk_parts(half[k], 2 + p, al_)) for k in range(2)]
                    item(t, hs, BT[:, t, 2 * p:2 * p + 2, :], ALU.add, p, 0.125, (p, 2 + p), VN + p * 128,
                         extra=(tbt,))
            for t, q_ in halves:
                for p in range(2):
                    hs = [(qk_parts(half[k], 4 + p, q_), qk_parts(half[k], 6 + p, al_)) for k in range(2)]
                    lnb = cn("ln", t * S, t * S + S).unsqueeze(1).to_broadcast([128, 2, S])
                    item(t, hs, lnb, ALU.add, 2 + p, 0.125, (4 + p, 6 + p), VD + p * 128, extra=(tc,))
            for t, q_ in halves:
                for p in range(2):
                    hs = [(qk_parts(half[k], 8 + p, q_), qk_parts(half[k], 10, al_)) for k in range(2)]
                    item(t, hs, None, None, 4 + p, 0.125, (8 + p, 10), VG)
            for t, q_ in halves:
                for h in range(4):
                    hs = []
                    for k in range(2):
                        r = (2 * h + k) % 4 * 32
                        blk = (2 * h + k) // 4
                        rr = slice(r, r + 32)
                        hs.append((qk_parts(rr, 11 + blk, q_), qk_parts(rr, 13 + blk, al_)))
                    item(t, hs, None, None, 6 + h // 2, 32 ** -0.5, (11 + blk, 13 + blk), VF + h // 2 * 128,
                         part=("first", "last")[h % 2])
            step, finish = attention(items)

            def work():
                step()
                background(BG if not tk else BG2)

            project(h_tok, WIN_U, WIN_N,
                    [(0, 512, "A", 0), (512, 768, "V", 0), (768, 1280, "A", 512), (1280, 1536, "V", 256),
                     (1536, 1920, "A", 1024), (1920, 2048, "V", 512), (2048, 2560, "A", 1408), (2560, 2816, "V", 640)],
                    norms, lambda u, t: t if u < 3 else 0, work)
            units_done[0] = WIN_U

            def after_project():
                background(BG3)
                if split and split[0] not in chunk_tok:
                    ch = split.pop(0)
                    hh, hl = Hh[:, ch, :], Hl[:, ch, :]
                    src = OT[:, :, ch, :]
                    w = (*box_outs[ch], *d["_h_free"])
                    t1 = AC(lambda e: e.activation(hh.rearrange("p (t q) -> p t q", t=2), src, ACT.Copy), *w)
                    t2 = V(lambda e: e.tensor_tensor(hl.rearrange("p (t q) -> p t q", t=2), src,
                                                     hh.bitcast(f32).rearrange("p (t q) -> p t q", t=2), ALU.subtract),
                           t1, *w)
                    chunk_tok[ch] = (t1, t2)

            outs, every = finish(after_project)
            while split:
                after_project()
            background_all()
            d["_bt_free"] = every
            ada["free"] = [every, every]
            ada["acc_free"] = ada["row_free"] = every
            sq = WK[:, 1024:1536].rearrange("p (t c q) -> p t c q", t=2, c=2)
            tsq = AC(lambda e: e.activation(sq, OT[:, :, 6:8, :], ACT.Square),
                     *outs[6, 0], *outs[7, 0], *outs[6, 1], *outs[7, 1], *d["_sb_free"])
            dn = {}

            def diff_sums():
                for t_ in range(2):
                    for c in range(2):
                        o = 4 * t_ + 2 * c
                        tp = PE(lambda e: e.matmul(PS[:, 4, o:o + 2], sq[:, t_, c, :], cn("bo", 0, 2), start=True,
                                                   stop=True), tsq, tc, *free[4], inc=True)
                tv = V(lambda e: e.tensor_copy(st[:, SS:SS + 8], PS[:, 4, 0:8]), tp, *d["_rs_free"])
                free[4] = (tv,)
                r = rstd_v(0, 8, 64, tv, mul=1.0 - lam_init)
                dn["rw"] = V(lambda e: e.tensor_copy(
                    WK[:, 1024:1536].rearrange("p (g n) -> p g n", n=64),
                    st[:, RS:RS + 8].unsqueeze(2).to_broadcast([128, 8, 64])), r, tp)

            def diff_scaled():
                for c in range(2):
                    for t_ in range(2):
                        tp = PE(lambda e: e.matmul(PS[:, 5, c * S + t_ * 128:c * S + t_ * 128 + 128], sq[:, t_, c, :],
                                                   ident, start=True, stop=True), dn["rw"], tid, *free[5], inc=True)
                d["_sb_free"] = (*d["_sb_free"], tp)
                rests = []
                for c in range(2):
                    rest, tr = chunk_scaled(6 + c, PS[:, 5, c * S:c * S + S].rearrange("p (t q) -> p t q", t=2),
                                            sm(f"os{l}", 6 + c, 7 + c), tp, tsm)
                    rests.append(rest)
                h_tok.extend([rest() for rest in rests])
                free[5] = (tr,)
                d["_rs_free"] = (dn["rw"],)
                a_free[0] = (tr, tsq, *chunk_tok[0], *chunk_tok[1], *chunk_tok[2], *chunk_tok[3])

            h_tok = [chunk_tok[ch] for ch in range(4)] + [(*outs[ch, 0], *outs[ch, 1]) for ch in (4, 5)]
            residual(out_proj(h_tok, {2: diff_sums, 4: diff_scaled}), 1.0)

        def load_g(l, which, post):
            tmp = BT[:, 0, :, :].rearrange("p a b -> p (a b)")
            w = (*mod_written[l], *d["_g_free"], *d["_bt_free"], *d["_gq_free"], *x_tok[1])
            t1 = DMA("sp", "g", G, modd[l:l + 1, which * D:(which + 1) * D].to_broadcast([128, D]), *w)
            t2 = DMA("sp", "g2", tmp, d[post][l:l + 1, :].to_broadcast([128, D]), *w)

            def product():
                t = V(lambda e: e.tensor_tensor(G, G, tmp, ALU.mult), t1, t2)
                d["_bt_free"] = (t,)
                box["g"] = t

            box = {}
            return product, box

        def load_cols(l):
            for i, k in enumerate((0, 1, 3, 4)):
                t = DMA("sp", f"mc{i}", mcol[:, i, :], modd[l, k * D:(k + 1) * D].rearrange("(c p) -> p c", p=128),
                        *mod_written[l], *d["_mc_free"], slow=True)
                d["_mc"][i] = t
            t = V(lambda e: e.scalar_tensor_tensor(out=mcol[:, 1, :], in0=mcol[:, 1, :], scalar=1.0,
                                                   in1=sm(f"pm{l}"), op0=ALU.add, op1=ALU.mult), d["_mc"][1], tsm)
            t2 = V(lambda e: e.scalar_tensor_tensor(out=mcol[:, 3, :], in0=mcol[:, 3, :], scalar=1.0,
                                                    in1=sm(f"pf{l}"), op0=ALU.add, op1=ALU.mult), d["_mc"][3], tsm)
            d["_colw"] = (tsm, t, t2, d["_mc"][0], d["_mc"][2])

        d["_mc"] = {}
        d["_mc_free"] = ()

        def second_mixer(l):
            tbt = DMA("sp", "bt", BT[:, :, :, :], d["t5b"], *d["_bt_free"], *ada["free"][0], *ada["free"][1])
            load_cols(l)
            h_tok = norm_T(mcol[:, 1, :], mcol[:, 0, :])
            tk = {}
            box = {}

            def hook(u, got):
                if u == 3:
                    box["qk"] = [x for p in got for x in p]
                if u == 4:
                    tk.update(transposes([(lambda t, c=c: A[:, t, c * 128:c * 128 + 128], c, 128) for c in range(8)],
                                         box["qk"], (4, 5, 6, 7)))
                    bg.extend(late_steps([x for p in got for x in p]))

            z = st[:, LF:LF + 8].rearrange("p (t h) -> p t h", t=2)
            mn = st[:, LF + 8:LF + 16]
            mx = st[:, LF + 16:LF + 24]
            lf = st[:, LF + 24:LF + 32]
            lh, ll = lfr[:, 0, :], lfr[:, 1, :]
            KR = GQ[:, 1536:1600].rearrange("p (t n) -> p t n", t=2)
            ta, tb = WK[:, 0:256], WK[:, 256:512]

            def late_steps(dep):
                def forget():
                    bfv = sm(f"bf{l}").unsqueeze(1).to_broadcast([128, 2, 4])
                    t0 = V(lambda e: e.tensor_tensor(z, A[:, :, 1440:1444], bfv, ALU.add), *dep, tsm, *d["_lf_free"])
                    zf = st[:, LF:LF + 8]
                    t1 = V(lambda e: e.tensor_scalar(mn, zf, 0.0, None, ALU.min), t0)
                    t2 = V(lambda e: e.tensor_scalar(mx, zf, 0.0, None, ALU.max), t0)
                    t3 = V(lambda e: e.tensor_tensor(mx, mn, mx, ALU.subtract), t1, t2)
                    t4 = AC(lambda e: e.activation(mx, mx, ACT.Exp), t3)
                    t4 = AC(lambda e: e.activation(mx, mx, ACT.Ln, bias=1.0), t4)
                    t5 = V(lambda e: e.tensor_tensor(lf, mn, mx, ALU.subtract), t4, t1)
                    t6 = AC(lambda e: e.activation(lh, lf, ACT.Copy), t5)
                    box["lf"] = (t6, V(lambda e: e.tensor_tensor(ll, lf, lh.bitcast(f32), ALU.subtract), t6))

                def squares(t_):
                    q1 = AC(lambda e: e.activation(WK[:, 512 * t_:512 * t_ + 256], A[:, t_, 1024:1280], ACT.Square,
                                                   accum_out=st[:, SS + t_:SS + t_ + 1]), *dep, *d["_rs_free"],
                            *d["_sb_free"])
                    q2 = AC(lambda e: e.activation(WK[:, 512 * t_ + 256:512 * t_ + 384], A[:, t_, 1280:1408], ACT.Square,
                                                   accum_out=st[:, SS + 2 + t_:SS + 3 + t_]), *d["_rs_free"])
                    box["q", t_] = (q1, q2)

                def roots():
                    box["r"] = (rstd(0, 2, 256, *box["q", 0], *box["q", 1]), rstd(2, 4, 128))

                def scales(t_):
                    v1 = V(lambda e: e.tensor_scalar(A[:, t_, 1024:1280], A[:, t_, 1024:1280],
                                                     st[:, RS + t_:RS + t_ + 1], None, ALU.mult), *box["r"])
                    v2 = V(lambda e: e.tensor_scalar(A[:, t_, 1280:1408], A[:, t_, 1280:1408],
                                                     st[:, RS + 2 + t_:RS + 3 + t_], None, ALU.mult), *box["r"])
                    box["s", t_] = (v1, v2)
                    d["_rs_free"] = (v1, v2)

                def kr_rope(t_):
                    box["kr"] = rope(A[:, t_, 1408:1440], cn("mlc", t_ * 32, t_ * 32 + 32),
                                     cn("mls", t_ * 32, t_ * 32 + 32), 16, ta[:, 0:32], tb[:, 0:32],
                                     *dep, tc, *box["q", 0], *box["q", 1], *d["_sb_free"], *d["_gq_free"],
                                     *([box["kr"]] if "kr" in box else []), dst=KR[:, t_, :])

                return [(1, fn) for fn in (lambda: squares(0), lambda: squares(1), roots, forget, lambda: scales(0),
                                           lambda: scales(1), lambda: kr_rope(0), lambda: kr_rope(1))]

            pr = project(h_tok, WIN2_U, WIN2_N, [(0, 1444, "A", 0), (1444, 1956, "V", 0)], hook,
                         lambda u, t: u % 2 * 2 + t, lambda: background(3))
            background_all()
            pa = [x for p in pr for x in p]
            kr = box["kr"]
            tl = box["lf"]
            for h in range(4):
                b = 4 + h // 2
                for c in range(2):
                    for k, part in enumerate((lh, ll)):
                        tf = PE(lambda e: e.matmul(
                            PS[:, b, (h % 2) * S:(h % 2) * S + S],
                            part[:, 4 * c + h:4 * c + h + 1].to_broadcast([128, 128]), Ur[:, c, :],
                            start=c == 0 and k == 0, stop=c == 1 and k == 1), *tl, t_u, *free[b],
                            inc=h == 3 and c == 1 and k == 1)
            for t_ in range(2):
                for c in range(2):
                    for k, part in enumerate((lh, ll)):
                        tq = PE(lambda e: e.matmul(
                            PS[:, 6, 4 * t_:4 * t_ + 4], Ur[:, c, t_ * 128:t_ * 128 + 128], part[:, 4 * c:4 * c + 4],
                            start=c == 0 and k == 0, stop=c == 1 and k == 1), *free[6], inc=True)
            fq = V(lambda e: e.tensor_copy(st[:, FQ:FQ + 8], PS[:, 6, 0:8]), tq)
            free[6] = (fq,)
            FB = GQ[:, 0:1536].rearrange("p (h n) -> p h n", h=4)
            pmask = cn("pm")
            for h in range(4):
                for t_ in range(2):
                    nk = 128 * (t_ + 1)
                    o = 0 if t_ == 0 else 128
                    src = PS[:, 4 + h // 2, (h % 2) * S:(h % 2) * S + nk]
                    tfb = V(lambda e, h=h, t_=t_, nk=nk, o=o, src=src: e.scalar_tensor_tensor(
                        out=FB[:, h, o:o + nk], in0=src, scalar=st[:, FQ + 4 * t_ + h:FQ + 4 * t_ + h + 1],
                        in1=pmask[:, 256 - nk:256], op0=ALU.subtract, op1=ALU.add), tf, fq, *d["_gq_free"],
                        *ada["acc_free"], *ada["row_free"])
                    if t_:
                        free[4 + h // 2] = (tfb,)
            d["_lf_free"] = (tq, tfb)
            o0 = SM_OFF[f"pq{l}"][0]
            lt = to_T(A, [1024, 1152, 1280], SM[:, o0:o0 + 3], lambda i, t: box["s", t])
            n = next_unit()
            h, lo = Wh[n % 2], Wl[n % 2]
            ev = []
            KLv = A[:, :, 768:1536].rearrange("p t (h n) -> p t h n", n=96)
            QLv = A[:, :, 0:768].rearrange("p t (h n) -> p t h n", n=96)
            for t_ in range(2):
                kc_ = V(lambda e: e.tensor_copy(
                    KLv[:, t_, :, 64:96], KR[:, t_, :].unsqueeze(1).to_broadcast([128, 8, 32])), kr,
                    *tk.values(), *lt[0], *lt[1], *lt[2], *tl)
            tkv = tuple(tk.values())
            for t_ in range(2):
                ts = slice(t_ * 128, t_ * 128 + 128)
                for j, (a, w_) in enumerate(((0, 512), (512, 256))):
                    b = 2 * 0 + j
                    for c in range(2):
                        w = need(n, c)
                        cc = slice(c * 768 + a, c * 768 + a + w_)
                        tp = three(PS[:, b, 0:w_], Hh[:, c, ts], Hl[:, c, ts], h[:, cc], lo[:, cc], c == 0, c == 1,
                                   *w, *lt[c], *(free[b] if c == 0 else ()), inc=c == 1)
                    dst = QLv[:, t_, :, 0:64] if j == 0 else QLv[:, t_, :, 64:96]
                    src = PS[:, b, 0:w_].rearrange("p (h n) -> p h n", h=8)
                    e_ = AC(lambda e, dst=dst, src=src: e.activation(dst, src, ACT.Copy), tp, *tkv)
                    free[b] = (e_,)
                    ev.append(e_)
                if t_ == 1:
                    done[n, 0] = done[n, 1] = tp
                w = need(n, 2)
                for j in range(2):
                    b = 2 + j
                    cc = slice(1536 + j * 512, 2048 + j * 512)
                    tp = three(PS[:, b, 0:512], Hh[:, 2, ts], Hl[:, 2, ts], h[:, cc], lo[:, cc], True, True,
                               *w, *lt[2], *free[b], inc=True)
                    src = PS[:, b, 0:512].rearrange("p (h n) -> p h n", h=8)
                    if j == 0:
                        e_ = V(lambda e: e.tensor_copy(KLv[:, t_, :, 0:64], src), tp, kc_)
                    else:
                        vh_, vl_ = Vh[:, t_, 512:1024], Vl[:, t_, 512:1024]
                        e0 = AC(lambda e: e.activation(vh_, PS[:, b, 0:512], ACT.Copy), tp, *d["_v_free"])
                        e_ = V(lambda e: e.tensor_tensor(vl_, PS[:, b, 0:512], vh_.bitcast(f32), ALU.subtract), e0)
                        ev.append(e0)
                    free[b] = (e_,)
                    ev.append(e_)
                if t_ == 1:
                    done[n, 2] = tp
            d["_h_free"] = (tp,)
            rp = [kr, *ev]
            for t_ in range(2):
                xs = QLv[:, t_, :, 64:96]
                cs = bc(cn("mlc", t_ * 32, t_ * 32 + 32).unsqueeze(1), [128, 8, 32])
                s_ = bc(cn("mls", t_ * 32, t_ * 32 + 32).unsqueeze(1), [128, 8, 32])
                r1_ = rope(xs, cs, s_, 16, ta[:, 0:256].rearrange("p (h n) -> p h n", n=32),
                           tb[:, 0:256].rearrange("p (h n) -> p h n", n=32), *rp)
                rp = [r1_]
            d["_sb_free"] = (r1_,)
            jobs = [(lambda t, hh=hh: A[:, t, hh * 96:hh * 96 + 96], 8 + hh, 96) for hh in range(8)]
            jobs += [(lambda t, hh=hh: A[:, t, 768 + hh * 96:768 + hh * 96 + 96], 16 + hh, 96) for hh in range(8)]
            d["_qt_free"] = (*d["_qt_free"], *d["_h_free"])
            tk2 = transposes(jobs, (r1_, kc_, *ev), (4, 5, 6, 7))
            of = tuple(tk2.values())
            items = []

            def vv(c0, nk):
                return [(Vh[:, c, c0:c0 + 128], Vl[:, c, c0:c0 + 128]) for c in range(nk // 128)]

            sq_tok = {}

            def sqv(ch):
                return (R[:, :].rearrange("p (t q) -> p t q", t=2) if ch == 7
                        else A[:, :, D + 128 * ch:D + 128 * ch + 128])

            def squared(ch, t, outs):
                dst = sqv(ch)
                sq_tok[ch] = AC(lambda e: e.activation(dst, OT[:, :, ch, :], ACT.Square), *outs[ch, 0], *outs[ch, 1],
                                *of)

            for t in range(2):
                nk = 128 * (t + 1)
                q_ = slice(t * 128, t * 128 + 128)
                o = 0 if t == 0 else 128
                half = [slice(64 * k, 64 * k + 64) for k in range(2)]
                aft = (*tk.values(), *tk2.values(), *ev, *pa, tbt, tfb, tc)
                rest = dict(t=t, nk=nk, part="pair", direct=False, after=lambda: aft, ready=lambda: True,
                            ofree=lambda: of, done=squared if t else None)
                for p in range(2):
                    hs = [(qk_parts(half[k], p, q_), qk_parts(half[k], 2 + p, slice(0, nk))) for k in range(2)]
                    items.append(dict(heads=hs, bias=FB[:, 2 * p:2 * p + 2, o:o + nk], op=ALU.subtract,
                                      chunk=p, scale=0.125, v=vv(128 * p, nk), **rest))
                for p in range(2):
                    hs = [(qk_parts(half[k], 4 + p, q_), qk_parts(half[k], 6 + p, slice(0, nk))) for k in range(2)]
                    items.append(dict(heads=hs, bias=BT[:, t, 2 * p:2 * p + 2, 0:nk], op=ALU.add,
                                      chunk=2 + p, scale=0.125, v=vv(256 + 128 * p, nk), **rest))
                for p in range(4):
                    hs = [(qk_parts(slice(0, 96), 8 + 2 * p + k, q_), qk_parts(slice(0, 96), 16 + 2 * p + k, slice(0, nk)))
                          for k in range(2)]
                    items.append(dict(heads=hs,
                                      bias=pmask[:, 256 - nk:256].unsqueeze(1).to_broadcast([128, 2, nk]),
                                      op=ALU.subtract, chunk=4 + p, scale=96 ** -0.5, v=vv(512 + 128 * p, nk), **rest))
            outs, every = attention(items)[1]()
            d["_bt_free"] = d["_gq_free"] = d["_h_free"] = every
            product, tg = load_g(l, 2, "g_mix_post")
            for t_ in range(2):
                for ch in range(8):
                    tp = PE(lambda e: e.matmul(PS[:, 6, 8 * t_ + ch:8 * t_ + ch + 1], sqv(ch)[:, t_, :], cn("bo", 2, 3),
                                               start=True, stop=True), sq_tok[ch], tc, *free[6], inc=ch == 7)
            for g, (a, b) in enumerate(((0, 2), (2, 4), (4, 8))):
                tv = V(lambda e: e.tensor_reduce(
                    st[:, SS + 2 * g:SS + 2 * g + 2], PS[:, 6, 0:16].rearrange("p (t c) -> p t c", t=2)[:, :, a:b],
                    AX.X, ALU.add), tp, *d["_rs_free"])
            free[6] = (tv,)
            tv = V(lambda e: e.tensor_scalar(st[:, SS + 4:SS + 6], st[:, SS + 4:SS + 6], 0.5, None, ALU.mult), tv)
            r = rstd_v(0, 6, 256, tv)
            for g in range(3):
                for t_ in range(2):
                    o = RS + 2 * g + t_
                    tp = PE(lambda e: e.matmul(PS[:, 4 + g // 2, g % 2 * S + t_ * 128:g % 2 * S + t_ * 128 + 128],
                                               st[:, o:o + 1].to_broadcast([128, 128]), ident,
                                               start=True, stop=True), r, tid, *free[4], *free[5], inc=True)
            h_tok = []
            rest = None
            for ch in range(8):
                g = (0, 0, 1, 1, 2, 2, 2, 2)[ch]
                before = rest
                rest, tr = chunk_scaled(ch, PS[:, 4 + g // 2, g % 2 * S:g % 2 * S + S].rearrange("p (t q) -> p t q", t=2),
                                        sm(f"pg{l}", ch, ch + 1), tp, tsm, *every)
                if before is not None:
                    h_tok.append(before())
            h_tok.append(rest())
            free[4] = free[5] = (tr,)
            d["_rs_free"] = (tp,)
            a_free[0] = (tr, tp)
            post_norm(out_proj(h_tok, {4: product}), tg)

        d["_lf_free"] = ()

        for l in range(L):
            residual(ffn(norm_T(sm(f"f1{l}")), NADA * (2 * l + 1) // 4), 0.5)
            first_mixer(l)
            residual(ffn(norm_T(sm(f"f2{l}")), NADA * (2 * l + 2) // 4), 0.5)
        for l in range(L):
            second_mixer(l)
            h = norm_T(mcol[:, 3, :], mcol[:, 2, :])
            product, tg = load_g(l, 5, "g_ffn_post")
            last = ffn(h, 0, product)
            d["_mc_free"] = h[-1]
            post_norm(last, tg)
        assert state["piece"] == len(pieces) == state["load"]
        DMA("sp", "out", out.rearrange("(t p) n -> p t n", t=2), X[:, :, :], *x_tok[0], *x_tok[1])
        for key in ("out", "mod"):
            queue["sp"].append((("wait_ge", (key, count[key]), {}), None, 0))

        block = ctx.enter_context(nc.Block())

        def run(e, name):
            for (op, a, k), sem, by in queue[name]:
                if op == "wait_ge":
                    e.wait_ge(sems[a[0]], a[1])
                    continue
                ins = CALLS[op](e, a, k)
                if sem is not None:
                    ins.then_inc(sems[sem], by)

        block.sync(lambda e: run(e, "sp"))
        block.scalar(lambda e: run(e, "act"))
        block.vector(lambda e: run(e, "dve"))
        block.gpsimd(lambda e: run(e, "pool"))
        block.tensor(lambda e: run(e, "pe"))


def constants():
    f = np.float32
    c = np.zeros((128, C_N), f)
    bo = np.ones((128, 4), f)
    bo[64:, 0] = 0
    bo[:64, 1] = 0

    def put(name, v):
        o, n = C_OFF[name]
        c[:, o:o + n] = np.asarray(v, f).reshape(128, n)

    i = np.arange(128)
    put("id", np.eye(128))
    put("bo", bo)
    pm = np.zeros((128, 256), f)
    pm[:, 128:] = np.where(i[None, :] <= i[:, None], 0.0, BIG)
    put("pm", pm)
    q = np.arange(S)
    dd = q[None, :] - q[:, None]
    m = (np.abs(dd) <= 64).astype(np.float64) + (dd % 4 == 0) + (dd % 16 == 0)
    ln = np.where(m > 0, np.log(np.maximum(m, 1)), -BIG).astype(f)
    put("ln", ln.reshape(2, 128, S).transpose(1, 0, 2))

    def table(pos, dim, theta):
        inv = (f(1.0) / (f(theta) ** (np.arange(0, dim, 2, dtype=f) / f(dim)))).astype(f)
        ang = pos.astype(f)[:, None] * inv[None, :]
        co, si = np.cos(ang).astype(f), np.sin(ang).astype(f)
        return np.concatenate([co, co], 1), np.concatenate([-si, si], 1)

    def halves(a):
        return a.reshape(2, 128, -1).transpose(1, 0, 2)

    for n, args in (("df", (q, 8, 500000.0)), ("dl", (q, 16, 500000.0)), ("ml", (q, 32, 10000.0))):
        a, b = table(*args)
        put(n + "c", halves(a))
        put(n + "s", halves(b))
    r, k = table(q // 64, 32, 10000.0), table(q % 64, 32, 10000.0)
    put("axc", halves(np.concatenate([r[0], k[0]], 1)))
    put("axs", halves(np.concatenate([r[1], k[1]], 1)))
    return c


def t5_buckets(n):
    f = np.float32
    nf = np.maximum(n, 16).astype(f)
    large = 16 + (np.log(nf / f(16)).astype(f) / f(math.log(128 / 16)) * f(16)).astype(np.int32)
    return np.where(n < 16, n, np.minimum(large, 31))


def kernel(**inputs):
    import numpy as np
    import concourse.bacc as _bacc
    from concourse import mybir as _mybir
    from concourse.bass_utils import run_bass_kernel_spmd as _run

    I = {k: np.asarray(v) for k, v in inputs.items()}
    f = np.float32
    C = np.ascontiguousarray

    def chunks(w, a, b):
        k = w.shape[0] // 128
        return w[:, a:b].reshape(k, 128, b - a).transpose(1, 0, 2).reshape(128, -1)

    def ffn(gate, up, down):
        g = gate.reshape(8, 128, NF, 128).transpose(2, 1, 0, 3).reshape(NF, 128, 1024)
        u = up.reshape(8, 128, NF, 128).transpose(2, 1, 0, 3).reshape(NF, 128, 1024)
        return np.concatenate([g, u, down.reshape(NF, 128, 1024)], axis=2)

    ffns = []
    for l in range(L):
        ffns.append(ffn(I["ffn1_w_gate"][l], I["ffn1_w_up"][l], I["ffn1_w_down"][l]))
        ffns.append(ffn(I["ffn2_w_gate"][l], I["ffn2_w_up"][l], I["ffn2_w_down"][l]))
    for l in range(L):
        gu = I["w_gate_up_2"][l]
        ffns.append(ffn(gu[:, :F], gu[:, F:], I["w_down_2"][l]))
    A = {"ffn": np.concatenate(ffns)}

    names = ["nq", "nk", "nv", "fq", "fk", "fv", "gq", "gk", "gv", "dq", "dk", "dv"]
    sizes = [256, 256, 256, 256, 256, 256, 256, 128, 128, 256, 256, 256]
    at = dict(zip(names, np.cumsum([0] + sizes[:-1])))
    sz = dict(zip(names, sizes))
    rng = {n: np.arange(at[n], at[n] + sz[n]) for n in names}
    gq_perm = np.concatenate([np.arange(h * 64, h * 64 + 64) for h in (0, 2, 1, 3)])
    cols = np.concatenate([rng["nq"], rng["nk"], rng["nv"], rng["dq"], rng["dk"], rng["dv"],
                           rng["gq"][gq_perm], rng["gk"], rng["gv"], rng["fq"], rng["fk"], rng["fv"]])
    A["win"] = np.concatenate([np.stack([chunks(I["w_in"][l][:, cols], u * WIN_N, (u + 1) * WIN_N)
                                         for u in range(WIN_U)]) for l in range(L)])
    rows = np.concatenate([np.arange(0, 256), np.arange(768, 1024), 512 + gq_perm, np.arange(256, 512)])
    A["wo"] = np.stack([chunks(I["w_out"][l][rows], 0, D) for l in range(L)]
                       + [chunks(I["w_out_2"][l], 0, D) for l in range(L)])
    n2 = ["fq", "fk", "fv", "fl", "mq", "mk", "mv", "cq", "ck", "kr"]
    s2 = [256, 256, 256, 4, 256, 256, 256, 256, 128, 32]
    a2 = dict(zip(n2, np.cumsum([0] + s2[:-1])))
    z2 = dict(zip(n2, s2))
    cols2 = np.concatenate([np.arange(a2[n], a2[n] + z2[n])
                            for n in ("fq", "fk", "mq", "mk", "cq", "ck", "kr", "fl", "fv", "mv")])
    A["win2"] = np.concatenate([np.stack([chunks(I["w_in_2"][l][:, cols2], u * WIN2_N, (u + 1) * WIN2_N)
                                          for u in range(WIN2_U)]) for l in range(L)])
    uq = np.concatenate([np.arange(h * 96, h * 96 + 64) for h in range(8)]
                        + [np.arange(h * 96 + 64, h * 96 + 96) for h in range(8)])
    ukv = np.concatenate([np.arange(h * 128, h * 128 + 64) for h in range(8)]
                         + [np.arange(h * 128 + 64, h * 128 + 128) for h in range(8)])
    A["lat"] = np.stack([np.concatenate([chunks(I["w_uq_2"][l][:, uq], 0, 768),
                                         chunks(I["w_ukv_2"][l][:, ukv], 0, 1024)], 1) for l in range(L)])
    A["ada"] = np.concatenate([I["w_ada_2"][l].reshape(4, 2, 128, ADA_G, ADA_N).transpose(3, 0, 2, 1, 4)
                               .reshape(ADA_G * 4, 128, 2 * ADA_N) for l in range(L)])
    A["b_ada"] = I["b_ada_2"]
    A["g_mix_post"] = I["g_mix_post_2"]
    A["g_ffn_post"] = I["g_ffn_post_2"]
    A["x"] = I["x"][0]
    A["c"] = I["c_2"][0].reshape(8, 128).T
    A["const"] = constants()
    A["tri"] = (np.arange(S)[:, None] <= np.arange(S)[None, :]).astype(f).reshape(2, 128, S).transpose(1, 0, 2).reshape(128, 512)

    small = np.zeros((128, SM_N), f)

    def col(v):
        return v.reshape(-1, 128).T

    def row(v):
        return np.broadcast_to(v.reshape(1, -1), (128, v.size))

    for l in range(L):
        osc = np.concatenate([np.ones(768, f), np.tile(I["diff_out_norm"][l], 4)])
        vals = {"f1": col(I["ffn1_norm"][l]), "mx": col(I["mix_norm"][l]), "f2": col(I["ffn2_norm"][l]),
                "os": col(osc),
                "la": row(np.concatenate([I["diff_lambda_q1"][l], I["diff_lambda_k1"][l],
                                          I["diff_lambda_q2"][l], I["diff_lambda_k2"][l]])),
                "pm": col(I["g_mix_pre_2"][l]), "pf": col(I["g_ffn_pre_2"][l]), "pg": col(I["g_group_2"][l]),
                "pq": col(I["g_q_lat_2"][l]), "pk": col(I["g_kv_lat_2"][l]), "bf": row(I["b_forget_2"][l])}
        for k, v in vals.items():
            o, n = SM_OFF[f"{k}{l}"]
            small[:, o:o + n] = v
    A["small"] = small
    A["gq"] = np.stack([row(np.concatenate([
        np.tile(I["na_q_norm"][l], 4), np.tile(I["na_k_norm"][l], 4), np.tile(I["dil_q_norm"][l], 4),
        np.tile(I["dil_k_norm"][l], 4), np.tile(I["gqa_q_norm"][l], 4), np.tile(I["gqa_k_norm"][l], 2),
        np.tile(I["diff_q_norm"][l], 8), np.tile(I["diff_k_norm"][l], 8)])) for l in range(L)])

    q = np.arange(S)
    r, c = q // 64, q % 64
    start = np.clip(c - 8, 0, 48)
    inside = (c[None, :] >= start[:, None]) & (c[None, :] < start[:, None] + 16)
    ro = r[None, :] - r[:, None] + 7
    co = np.clip(c[None, :] - c[:, None] + 15, 0, 30)
    nab = np.where(inside[None, None], I["na_rel_bias"][:, :, ro, co], f(-BIG))
    A["nab"] = nab.reshape(L, 4, 2, 128, S).transpose(0, 3, 2, 1, 4)
    dist = q[:, None] - q[None, :]
    t5 = I["t5_table_2"].T[:, t5_buckets(np.maximum(dist, 0))]
    t5 = np.where(dist[None] >= 0, t5, f(-BIG))
    A["t5b"] = t5.reshape(4, 2, 128, S).transpose(2, 1, 0, 3)

    nc = _bacc.Bacc("TRN2", target_bir_lowering=False, num_devices=1)
    arrays, d = {}, {}
    for name, a in A.items():
        a = C(a)
        arrays[f"in_{name}"] = a
        d[name] = nc.dram_tensor(f"in_{name}", a.shape, _mybir.dt.from_np(a.dtype), kind="ExternalInput").ap()
    out = nc.dram_tensor("out_x", (S, D), _mybir.dt.float32, kind="ExternalOutput").ap()
    program(nc, d, out)
    res = _run(nc, [arrays], core_ids=[0])
    return res.results[0]["out_x"].reshape(1, S, D)
```
